# Optimizing a Trainium2 kernel written in Bass

```python
import math
import jax, jax.numpy as jnp
from jax import lax
import numpy as np

D_MODEL = 1024
BATCH = 1
SEQ = 512
DEPTH = 2

PLE_DIM = 256
HEAD_DIM = 64
DA_HEADS = 4
DA_V = 2 * HEAD_DIM
DA_QK = DA_HEADS * 2 * HEAD_DIM
DA_WIDTH = DA_HEADS * DA_V
MLA_HEADS = 8
MLA_NOPE = 64
MLA_ROPE = 32
MLA_V = 64
MLA_Q_RANK = 256
MLA_KV_RANK = 128
MLA_WIDTH = MLA_HEADS * MLA_V
SW_HEADS = 8
SW_KV_HEADS = 2
SW_GROUP = SW_HEADS // SW_KV_HEADS
SW_WINDOW = 128
SW_WIDTH = SW_HEADS * HEAD_DIM
N_BRANCHES = 3
REL_BUCKETS = 32
REL_MAX_DIST = 128
BIAS_HEADS = DA_HEADS + SW_HEADS
Q_BLOCK = 128
ROPE_THETA = 10000.0
EPS = 1e-6
NEG = -1e30

IN_SIZES = (DA_QK, DA_QK, DA_WIDTH, DA_WIDTH,
            MLA_Q_RANK, MLA_KV_RANK, MLA_ROPE, MLA_WIDTH,
            SW_HEADS * HEAD_DIM, SW_KV_HEADS * HEAD_DIM, SW_KV_HEADS * HEAD_DIM, SW_WIDTH,
            N_BRANCHES * D_MODEL)
IN_TOTAL = sum(IN_SIZES)


def rms_norm(x, w):
    xf = x.astype(jnp.float32)
    y = xf * lax.rsqrt(jnp.mean(xf * xf, axis=-1, keepdims=True) + EPS)
    return (y * w.astype(jnp.float32)).astype(x.dtype)

def rope(x, positions):
    half = x.shape[-1] // 2
    inv_freq = ROPE_THETA ** (-jnp.arange(half, dtype=jnp.float32) / half)
    ang = positions.astype(jnp.float32)[..., None] * inv_freq
    ang = ang.reshape(ang.shape[:2] + (1,) * (x.ndim - 3) + (half,))
    cos, sin = jnp.cos(ang), jnp.sin(ang)
    xf = x.astype(jnp.float32)
    x1, x2 = xf[..., :half], xf[..., half:]
    return jnp.concatenate([x1 * cos - x2 * sin, x2 * cos + x1 * sin], axis=-1).astype(x.dtype)

def t5_bucket(rel):
    n = jnp.maximum(rel, 0)
    max_exact = REL_BUCKETS // 2
    nf = jnp.maximum(n, 1).astype(jnp.float32)
    large = max_exact + (jnp.log(nf / max_exact) / math.log(REL_MAX_DIST / max_exact)
                         * (REL_BUCKETS - max_exact)).astype(jnp.int32)
    large = jnp.minimum(large, REL_BUCKETS - 1)
    return jnp.where(n < max_exact, n, large)

def sweep_query_blocks(block_fn, n_blocks):
    out = lax.map(block_fn, jnp.arange(n_blocks))
    out = jnp.moveaxis(out, 0, 1)
    return out.reshape((out.shape[0], n_blocks * Q_BLOCK) + out.shape[3:])

def diff_attention(q, k, v, lam, rel_table):
    S = q.shape[1]
    scale = HEAD_DIM ** -0.5
    kf = k.astype(jnp.float32)
    table = rel_table.astype(jnp.float32)
    k_idx = jnp.arange(S)

    def block(i):
        q0 = i * Q_BLOCK
        qb = lax.dynamic_slice_in_dim(q, q0, Q_BLOCK, axis=1).astype(jnp.float32)
        s = jnp.einsum('bqhmd,bkhmd->bhmqk', qb, kf) * scale
        rel = (q0 + jnp.arange(Q_BLOCK))[:, None] - k_idx[None, :]
        bias = jnp.moveaxis(table[t5_bucket(rel)][..., :DA_HEADS], -1, 0)
        s = jnp.where(rel >= 0, s + bias[None, :, None], NEG)
        pm = jax.nn.softmax(s, axis=-1)
        w = pm[:, :, 0] - lam * pm[:, :, 1]
        return jnp.einsum('bhqk,bkhe->bqhe', w.astype(v.dtype), v)

    return sweep_query_blocks(block, S // Q_BLOCK)

def mla_attention(q_nope, q_rope, k_nope, k_rope, v):
    S = q_nope.shape[1]
    scale = (MLA_NOPE + MLA_ROPE) ** -0.5
    kn = k_nope.astype(jnp.float32)
    kr = k_rope.astype(jnp.float32)
    k_idx = jnp.arange(S)

    def block(i):
        q0 = i * Q_BLOCK
        qn = lax.dynamic_slice_in_dim(q_nope, q0, Q_BLOCK, axis=1).astype(jnp.float32)
        qr = lax.dynamic_slice_in_dim(q_rope, q0, Q_BLOCK, axis=1).astype(jnp.float32)
        s = (jnp.einsum('bqhd,bkhd->bhqk', qn, kn)
             + jnp.einsum('bqhr,bkr->bhqk', qr, kr)) * scale
        rel = (q0 + jnp.arange(Q_BLOCK))[:, None] - k_idx[None, :]
        s = jnp.where(rel >= 0, s, NEG)
        pm = jax.nn.softmax(s, axis=-1)
        return jnp.einsum('bhqk,bkhd->bqhd', pm.astype(v.dtype), v)

    return sweep_query_blocks(block, S // Q_BLOCK)

def sliding_window_attention(q, k, v, sinks, rel_table):
    B, S = q.shape[:2]
    nb = S // Q_BLOCK
    scale = HEAD_DIM ** -0.5
    qb = q.reshape(B, nb, Q_BLOCK, SW_KV_HEADS, SW_GROUP, HEAD_DIM).astype(jnp.float32)

    def band(t):
        tp = jnp.pad(t, ((0, 0), (Q_BLOCK, 0), (0, 0), (0, 0)))
        tp = tp.reshape(B, nb + 1, Q_BLOCK, SW_KV_HEADS, HEAD_DIM)
        return jnp.concatenate([tp[:, :-1], tp[:, 1:]], axis=2)

    kb = band(k).astype(jnp.float32)
    vb = band(v)
    s = jnp.einsum('bnqhgd,bnkhd->bnhgqk', qb, kb) * scale
    qi = jnp.arange(Q_BLOCK)
    kj = jnp.arange(2 * Q_BLOCK)
    rel = Q_BLOCK + qi[:, None] - kj[None, :]
    bias = jnp.moveaxis(rel_table.astype(jnp.float32)[t5_bucket(rel)][..., DA_HEADS:], -1, 0)
    bias = bias.reshape(SW_KV_HEADS, SW_GROUP, Q_BLOCK, 2 * Q_BLOCK)
    in_window = (rel >= 0) & (rel < SW_WINDOW)
    key_valid = (jnp.arange(nb)[:, None] * Q_BLOCK + kj[None, :] - Q_BLOCK) >= 0
    mask = in_window[None] & key_valid[:, None, :]
    s = jnp.where(mask[None, :, None, None], s + bias, NEG)
    sink = jnp.broadcast_to(sinks.astype(jnp.float32).reshape(SW_KV_HEADS, SW_GROUP, 1, 1),
                            s.shape[:-1] + (1,))
    pm = jax.nn.softmax(jnp.concatenate([s, sink], axis=-1), axis=-1)[..., :-1]
    o = jnp.einsum('bnhgqk,bnkhd->bnqhgd', pm.astype(v.dtype), vb)
    return o.reshape(B, S, SW_WIDTH)

def first_inputs(seed: int = 0) -> dict:
    key = jax.random.key(seed)
    ks = jax.random.split(key, 24)
    f32 = jnp.float32

    def nrm(k, shape, scale):
        return jax.random.normal(k, shape, f32) * scale

    def gain(k, shape):
        return 1.0 + 0.05 * jax.random.normal(k, shape, f32)

    start = jax.random.randint(ks[2], (BATCH, 1), 0, 4096, dtype=jnp.int32)
    positions = start + jnp.arange(SEQ, dtype=jnp.int32)[None, :]
    return {
        "x": nrm(ks[0], (BATCH, SEQ, D_MODEL), 1.0),
        "p": nrm(ks[1], (DEPTH, BATCH, SEQ, PLE_DIM), 1.0),
        "positions": positions,
        "rel_bias": nrm(ks[3], (REL_BUCKETS, BIAS_HEADS), 0.3),
        "norm_pre": gain(ks[4], (DEPTH, D_MODEL)),
        "norm_post": gain(ks[5], (DEPTH, D_MODEL)),
        "w_in": nrm(ks[6], (DEPTH, D_MODEL, IN_TOTAL), D_MODEL ** -0.5),
        "da_lambda": nrm(ks[7], (DEPTH, 4, HEAD_DIM), 0.1),
        "da_subln": gain(ks[8], (DEPTH, DA_V)),
        "mla_q_norm": gain(ks[9], (DEPTH, MLA_Q_RANK)),
        "mla_w_qb": nrm(ks[10], (DEPTH, MLA_Q_RANK, MLA_HEADS * (MLA_NOPE + MLA_ROPE)), MLA_Q_RANK ** -0.5),
        "mla_kv_norm": gain(ks[11], (DEPTH, MLA_KV_RANK)),
        "mla_w_kvb": nrm(ks[12], (DEPTH, MLA_KV_RANK, MLA_HEADS * (MLA_NOPE + MLA_V)), MLA_KV_RANK ** -0.5),
        "sw_sinks": nrm(ks[13], (DEPTH, SW_HEADS), 0.5),
        "w_br_a": nrm(ks[14], (DEPTH, DA_WIDTH, D_MODEL), DA_WIDTH ** -0.5),
        "w_br_b": nrm(ks[15], (DEPTH, MLA_WIDTH, D_MODEL), MLA_WIDTH ** -0.5),
        "w_br_c": nrm(ks[16], (DEPTH, SW_WIDTH, D_MODEL), SW_WIDTH ** -0.5),
        "w_out": nrm(ks[17], (DEPTH, D_MODEL, D_MODEL), D_MODEL ** -0.5),
        "w_ple_gate": nrm(ks[18], (DEPTH, D_MODEL, D_MODEL), D_MODEL ** -0.5),
        "w_ple_proj": nrm(ks[19], (DEPTH, PLE_DIM, D_MODEL), PLE_DIM ** -0.5),
    }

def first_block(x, p, positions, rel_bias, norm_pre, norm_post, w_in, da_lambda, da_subln,
              mla_q_norm, mla_w_qb, mla_kv_norm, mla_w_kvb, sw_sinks,
              w_br_a, w_br_b, w_br_c, w_out, w_ple_gate, w_ple_proj):
    B, S, _ = x.shape
    split_points = tuple(int(c) for c in np.cumsum(IN_SIZES)[:-1])
    for l in range(DEPTH):
        h = rms_norm(x, norm_pre[l])
        u = h @ w_in[l]
        (a_q, a_k, a_v, a_z, b_q, b_kv, b_kr, b_z,
         c_q, c_k, c_v, c_z, g) = jnp.split(u, split_points, axis=-1)

        lam_init = 0.8 - 0.6 * math.exp(-0.3 * l)
        lf = da_lambda[l].astype(jnp.float32)
        lam = jnp.exp(jnp.sum(lf[0] * lf[1])) - jnp.exp(jnp.sum(lf[2] * lf[3])) + lam_init
        oa = diff_attention(a_q.reshape(B, S, DA_HEADS, 2, HEAD_DIM),
                            a_k.reshape(B, S, DA_HEADS, 2, HEAD_DIM),
                            a_v.reshape(B, S, DA_HEADS, DA_V), lam, rel_bias)
        oa = (rms_norm(oa, da_subln[l]) * (1.0 - lam_init)).reshape(B, S, DA_WIDTH)

        qm = (rms_norm(b_q, mla_q_norm[l]) @ mla_w_qb[l]).reshape(B, S, MLA_HEADS, MLA_NOPE + MLA_ROPE)
        q_nope, q_rope = qm[..., :MLA_NOPE], rope(qm[..., MLA_NOPE:], positions)
        kvm = (rms_norm(b_kv, mla_kv_norm[l]) @ mla_w_kvb[l]).reshape(B, S, MLA_HEADS, MLA_NOPE + MLA_V)
        k_nope, v_m = kvm[..., :MLA_NOPE], kvm[..., MLA_NOPE:]
        k_rope = rope(b_kr, positions)
        ob = mla_attention(q_nope, q_rope, k_nope, k_rope, v_m).reshape(B, S, MLA_WIDTH)

        oc = sliding_window_attention(c_q.reshape(B, S, SW_HEADS, HEAD_DIM),
                                      c_k.reshape(B, S, SW_KV_HEADS, HEAD_DIM),
                                      c_v.reshape(B, S, SW_KV_HEADS, HEAD_DIM),
                                      sw_sinks[l], rel_bias)

        gates = jax.nn.sigmoid(g).reshape(B, S, N_BRANCHES, D_MODEL)
        y = (gates[:, :, 0] * ((oa * jax.nn.silu(a_z)) @ w_br_a[l])
             + gates[:, :, 1] * ((ob * jax.nn.silu(b_z)) @ w_br_b[l])
             + gates[:, :, 2] * ((oc * jax.nn.silu(c_z)) @ w_br_c[l]))
        x = x + rms_norm(y @ w_out[l], norm_post[l])

        x = x + jax.nn.sigmoid(x @ w_ple_gate[l]) * (p[l] @ w_ple_proj[l])
    return x


N_A_LAYERS = DEPTH // 2
N_B_LAYERS = DEPTH - N_A_LAYERS
RMS_EPS = 1e-6
RET_HEADS = D_MODEL // 256
RET_QK_DIM = D_MODEL // RET_HEADS
RET_V_DIM = 2 * D_MODEL // RET_HEADS
RET_IN_WIDTH = 6 * D_MODEL
RET_CHUNK = 128
RET_ROT_BASE = 10000.0
GN_EPS = 1e-6
ATT_HEADS = 16
ATT_HEAD_DIM = D_MODEL // ATT_HEADS
DIL_GROUPS = ((128, 1), (512, 4), (2048, 16))
N_GROUPS = 3
ATT_BLOCK = 128
ROPE_THETA_2 = 500000.0
ROPE_DIMS = ATT_HEAD_DIM // 4
Q_WIDTH = N_GROUPS * ATT_HEADS * ATT_HEAD_DIM
D_FF = 2816
CONV_WIDTH = 3


def rmsnorm(x, g):
    xf = x.astype(jnp.float32)
    y = xf * lax.rsqrt(jnp.mean(xf * xf, axis=-1, keepdims=True) + RMS_EPS)
    return (y * g).astype(x.dtype)

def apply_rotary(t, pos, inv_freq):
    n = 2 * inv_freq.shape[0]
    S = t.shape[1]
    ang = pos.astype(jnp.float32)[:, None] * inv_freq[None, :]
    bshape = (1, S) + (1,) * (t.ndim - 3) + (n // 2,)
    cos = jnp.cos(ang).reshape(bshape)
    sin = jnp.sin(ang).reshape(bshape)
    t1, t2, rest = t[..., : n // 2], t[..., n // 2: n], t[..., n:]
    rot = jnp.concatenate([t1 * cos - t2 * sin, t2 * cos + t1 * sin], axis=-1).astype(t.dtype)
    return jnp.concatenate([rot, rest], axis=-1)

def retention_chunkwise(q, k, v, log_gamma):
    B, S, H, dk = q.shape
    dv = v.shape[-1]
    C = RET_CHUNK
    nc = S // C
    qc = q.reshape(B, nc, C, H, dk)
    kc = k.reshape(B, nc, C, H, dk)
    vc = v.reshape(B, nc, C, H, dv)
    n = jnp.arange(C, dtype=jnp.float32)
    diff = n[:, None] - n[None, :]
    decay_mask = jnp.where(diff[None] >= 0,
                           jnp.exp(jnp.maximum(diff, 0.0)[None] * log_gamma[:, None, None]), 0.0)
    scores = jnp.einsum('bnqhd,bnkhd->bnhqk', qc, kc) * decay_mask
    intra = jnp.einsum('bnhqk,bnkhe->bnqhe', scores, vc)
    xi = jnp.exp((n + 1.0)[None, :] * log_gamma[:, None]).T[None, :, :, None]
    zeta = jnp.exp((C - 1.0 - n)[None, :] * log_gamma[:, None]).T[None, :, :, None]
    chunk_decay = jnp.exp(C * log_gamma)[None, :, None, None]

    def step(state, inp):
        qi, ki, vi = inp
        cross = jnp.einsum('bchd,bhde->bche', qi, state) * xi
        state = state * chunk_decay + jnp.einsum('bchd,bche->bhde', ki * zeta, vi)
        return state, cross

    state0 = jnp.zeros((B, H, dk, dv), jnp.float32)
    _, cross = lax.scan(step, state0, (jnp.moveaxis(qc, 1, 0), jnp.moveaxis(kc, 1, 0), jnp.moveaxis(vc, 1, 0)))
    out = intra + jnp.moveaxis(cross, 0, 1)
    return out.reshape(B, S, H, dv).astype(v.dtype)

def retention_mixer(h, w_in, w_out, gn_gain, pos):
    B, S, _ = h.shape
    dqk = RET_HEADS * RET_QK_DIM
    dv = RET_HEADS * RET_V_DIM
    proj = h @ w_in
    q = proj[..., :dqk].reshape(B, S, RET_HEADS, RET_QK_DIM)
    k = proj[..., dqk:2 * dqk].reshape(B, S, RET_HEADS, RET_QK_DIM) * (RET_QK_DIM ** -0.5)
    v = proj[..., 2 * dqk:2 * dqk + dv].reshape(B, S, RET_HEADS, RET_V_DIM)
    g = proj[..., 2 * dqk + dv:]
    inv_freq = 1.0 / (RET_ROT_BASE ** jnp.linspace(0.0, 1.0, RET_QK_DIM // 2, dtype=jnp.float32))
    q = apply_rotary(q, pos, inv_freq)
    k = apply_rotary(k, pos, inv_freq)
    log_gamma = jnp.log(1.0 - 2.0 ** (-5.0 - jnp.arange(RET_HEADS, dtype=jnp.float32)))
    y = retention_chunkwise(q, k, v, log_gamma).astype(jnp.float32)
    mu = jnp.mean(y, axis=-1, keepdims=True)
    var = jnp.mean(jnp.square(y - mu), axis=-1, keepdims=True)
    yn = ((y - mu) * lax.rsqrt(var + GN_EPS)).reshape(B, S, dv) * gn_gain
    return (jax.nn.silu(g) * yn.astype(g.dtype)) @ w_out

def shared_kv(x, kv_norm, w_kv, pos):
    B, S, _ = x.shape
    kv = (rmsnorm(x, kv_norm) @ w_kv).reshape(B, S, 2, N_GROUPS, ATT_HEADS, ATT_HEAD_DIM)
    inv_freq = ROPE_THETA_2 ** (-jnp.arange(0, ROPE_DIMS, 2, dtype=jnp.float32) / ROPE_DIMS)
    k = apply_rotary(kv[:, :, 0], pos, inv_freq)
    v = kv[:, :, 1]
    return k, v

def dilated_group_attention(q, k, v, window, dilation):
    B, S, H, hd = q.shape
    blk = ATT_BLOCK
    steps = window // dilation
    span = dilation * blk
    s_pad = -(-S // span) * span
    L = s_pad // dilation
    nblk = L // blk

    def to_sub(t):
        t = jnp.pad(t, ((0, 0), (0, s_pad - S), (0, 0), (0, 0)))
        return t.reshape(B, L, dilation, H, hd).transpose(0, 2, 1, 3, 4)

    qs = to_sub(q)
    ks = jnp.pad(to_sub(k), ((0, 0), (0, 0), (blk, 0), (0, 0), (0, 0)))
    vs = jnp.pad(to_sub(v), ((0, 0), (0, 0), (blk, 0), (0, 0), (0, 0)))
    kj = jnp.arange(2 * blk)[None, :]
    dist = (jnp.arange(blk)[:, None] + blk) - kj
    band = (dist >= 0) & (dist <= steps)
    scale = hd ** -0.5

    def one_block(idx):
        r = idx // nblk
        b = idx % nblk
        qb = lax.dynamic_slice(qs, (0, r, b * blk, 0, 0), (B, 1, blk, H, hd))[:, 0]
        kb = lax.dynamic_slice(ks, (0, r, b * blk, 0, 0), (B, 1, 2 * blk, H, hd))[:, 0]
        vb = lax.dynamic_slice(vs, (0, r, b * blk, 0, 0), (B, 1, 2 * blk, H, hd))[:, 0]
        s = jnp.einsum('bqhd,bkhd->bhqk', qb, kb).astype(jnp.float32) * scale
        valid = band & (b * blk + kj - blk >= 0)
        s = jnp.where(valid, s, -jnp.inf)
        m = jnp.max(s, axis=-1, keepdims=True)
        p = jnp.exp(s - m)
        den = jnp.sum(p, axis=-1)
        o = jnp.einsum('bhqk,bkhd->bqhd', p, vb) / den.transpose(0, 2, 1)[..., None]
        lse = (m[..., 0] + jnp.log(den)).transpose(0, 2, 1)
        return o.astype(q.dtype), lse

    o, lse = lax.map(one_block, jnp.arange(dilation * nblk))
    o = o.reshape(dilation, nblk, B, blk, H, hd).transpose(2, 1, 3, 0, 4, 5).reshape(B, s_pad, H, hd)[:, :S]
    lse = lse.reshape(dilation, nblk, B, blk, H).transpose(2, 1, 3, 0, 4).reshape(B, s_pad, H)[:, :S]
    return o, lse

def dilated_mixer(h, w_q, w_o, k_sh, v_sh, pos):
    B, S, _ = h.shape
    q = (h @ w_q).reshape(B, S, N_GROUPS, ATT_HEADS, ATT_HEAD_DIM)
    inv_freq = ROPE_THETA_2 ** (-jnp.arange(0, ROPE_DIMS, 2, dtype=jnp.float32) / ROPE_DIMS)
    q = apply_rotary(q, pos, inv_freq)
    outs, lses = [], []
    for gi, (window, dilation) in enumerate(DIL_GROUPS):
        o, l = dilated_group_attention(q[:, :, gi], k_sh[:, :, gi], v_sh[:, :, gi], window, dilation)
        outs.append(o)
        lses.append(l)
    alpha = jax.nn.softmax(jnp.stack(lses, axis=0), axis=0)
    o = jnp.einsum('gbsh,gbshd->bshd', alpha, jnp.stack(outs, axis=0).astype(jnp.float32))
    return o.astype(h.dtype).reshape(B, S, ATT_HEADS * ATT_HEAD_DIM) @ w_o

def conv_ffn(h, w_up, conv_w, conv_b, w_down):
    S = h.shape[1]
    u = h @ w_up
    gate, val = u[..., :D_FF], u[..., D_FF:]
    gp = jnp.pad(gate, ((0, 0), (CONV_WIDTH - 1, 0), (0, 0)))
    conv = conv_b
    for i in range(CONV_WIDTH):
        conv = conv + conv_w[i] * gp[:, i:i + S]
    return (jax.nn.gelu(conv, approximate=True) * val) @ w_down

def second_inputs(seed: int = 0) -> dict:
    key = jax.random.key(seed)
    ks = jax.random.split(key, 17)
    f32 = jnp.float32

    def nrm(k, shape, fan_in):
        return jax.random.normal(k, shape, f32) * (fan_in ** -0.5)

    def gain(k, shape):
        return 1.0 + 0.02 * jax.random.normal(k, shape, f32)

    return {
        "x": jax.random.normal(ks[0], (BATCH, SEQ, D_MODEL), f32),
        "ret_w_in": nrm(ks[1], (N_A_LAYERS, D_MODEL, RET_IN_WIDTH), D_MODEL),
        "ret_w_out": nrm(ks[2], (N_A_LAYERS, RET_HEADS * RET_V_DIM, D_MODEL), RET_HEADS * RET_V_DIM),
        "ret_gn_gain": gain(ks[3], (N_A_LAYERS, RET_HEADS * RET_V_DIM)),
        "kv_norm": gain(ks[4], (D_MODEL,)),
        "att_w_kv": nrm(ks[5], (D_MODEL, 2 * Q_WIDTH), D_MODEL),
        "att_w_q": nrm(ks[6], (N_B_LAYERS, D_MODEL, Q_WIDTH), D_MODEL),
        "att_w_o": nrm(ks[7], (N_B_LAYERS, ATT_HEADS * ATT_HEAD_DIM, D_MODEL), ATT_HEADS * ATT_HEAD_DIM),
        "norm_mix_pre": gain(ks[8], (DEPTH, D_MODEL)),
        "norm_mix_post": gain(ks[9], (DEPTH, D_MODEL)),
        "norm_ffn_pre": gain(ks[10], (DEPTH, D_MODEL)),
        "norm_ffn_post": gain(ks[11], (DEPTH, D_MODEL)),
        "ffn_w_up": nrm(ks[12], (DEPTH, D_MODEL, 2 * D_FF), D_MODEL),
        "ffn_conv_w": nrm(ks[13], (DEPTH, CONV_WIDTH, D_FF), CONV_WIDTH),
        "ffn_conv_b": 0.02 * jax.random.normal(ks[14], (DEPTH, D_FF), f32),
        "ffn_w_down": nrm(ks[15], (DEPTH, D_FF, D_MODEL), D_FF),
    }

def second_block(x, ret_w_in, ret_w_out, ret_gn_gain, kv_norm, att_w_kv, att_w_q, att_w_o,
              norm_mix_pre, norm_mix_post, norm_ffn_pre, norm_ffn_post,
              ffn_w_up, ffn_conv_w, ffn_conv_b, ffn_w_down):
    pos = jnp.arange(x.shape[1], dtype=jnp.int32)
    k_sh, v_sh = None, None
    for layer in range(DEPTH):
        h = rmsnorm(x, norm_mix_pre[layer])
        if layer < N_A_LAYERS:
            m = retention_mixer(h, ret_w_in[layer], ret_w_out[layer], ret_gn_gain[layer], pos)
        else:
            bi = layer - N_A_LAYERS
            m = dilated_mixer(h, att_w_q[bi], att_w_o[bi], k_sh, v_sh, pos)
        x = x + rmsnorm(m, norm_mix_post[layer])
        f = conv_ffn(rmsnorm(x, norm_ffn_pre[layer]), ffn_w_up[layer], ffn_conv_w[layer],
                     ffn_conv_b[layer], ffn_w_down[layer])
        x = x + rmsnorm(f, norm_ffn_post[layer])
        if layer == N_A_LAYERS - 1:
            k_sh, v_sh = shared_kv(x, kv_norm, att_w_kv, pos)
    return x


def setup_inputs(seed=0):
    out = dict(first_inputs(seed))
    for name, value in second_inputs(seed + 1).items():
        if name != "x":
            out[name + "_2"] = value
    return out


def reference(
    x, p, positions, rel_bias, norm_pre, norm_post, w_in, da_lambda, da_subln, mla_q_norm,
    mla_w_qb, mla_kv_norm, mla_w_kvb, sw_sinks, w_br_a, w_br_b, w_br_c, w_out, w_ple_gate,
    w_ple_proj, ret_w_in_2, ret_w_out_2, ret_gn_gain_2, kv_norm_2, att_w_kv_2, att_w_q_2,
    att_w_o_2, norm_mix_pre_2, norm_mix_post_2, norm_ffn_pre_2, norm_ffn_post_2, ffn_w_up_2,
    ffn_conv_w_2, ffn_conv_b_2, ffn_w_down_2,
):
    x = first_block(
        x, p, positions, rel_bias, norm_pre, norm_post, w_in, da_lambda, da_subln, mla_q_norm,
        mla_w_qb, mla_kv_norm, mla_w_kvb, sw_sinks, w_br_a, w_br_b, w_br_c, w_out, w_ple_gate,
        w_ple_proj,
    )
    return second_block(
        x, ret_w_in_2, ret_w_out_2, ret_gn_gain_2, kv_norm_2, att_w_kv_2, att_w_q_2, att_w_o_2,
        norm_mix_pre_2, norm_mix_post_2, norm_ffn_pre_2, norm_ffn_post_2, ffn_w_up_2,
        ffn_conv_w_2, ffn_conv_b_2, ffn_w_down_2,
    )


_drawn_inputs = setup_inputs


def setup_inputs(seed=0):
    import zlib

    import numpy as np

    out = dict(_drawn_inputs(seed))
    spreads = {}
    factors = {'mla_q_norm': 3.226,
     'sw_sinks': 3.552,
     'ret_gn_gain_2': 4.827,
     'kv_norm_2': 5.278,
     'norm_mix_post_2': 4.051,
     'norm_ffn_pre_2': 3.164,
     'norm_ffn_post_2': 4.727,
     'ffn_conv_b_2': 4.657}
    for name, (base, spread) in spreads.items():
        noise = np.random.default_rng([zlib.crc32(name.encode()), seed]).standard_normal(out[name].shape)
        drawn = base * np.exp(spread * noise) if base else spread * noise
        out[name] = __import__('jax').numpy.asarray(drawn.astype(out[name].dtype))
    for name, factor in factors.items():
        out[name] = (out[name] * factor).astype(out[name].dtype)
    return out
```

```python
import math
from contextlib import ExitStack, contextmanager

import numpy as np

import concourse.bass as bass
from concourse import mybir

F32 = mybir.dt.float32
F32R = mybir.dt.float32r
I32 = mybir.dt.int32
ALU = mybir.AluOpType
ACT = mybir.ActivationFunctionType

P = 128
SEQ = 512
QT = SEQ // P
D = 1024
KT = D // P
DEPTH = 2
HEAD = 64
ROPE = 32
HALF = ROPE // 2
DFF = 2816
FT = DFF // P
FH = FT // 2
RET_HEADS = 4
RET_V = 512
EPS = 1e-6
NEG = -1e30
LOWEST = -3.0e38
RING = 2
SLOT = 12
LBANKS = 4
S0, TURN, OUTB = 4, 6, 7
BUCKETS, BHEADS = 32, 12
RV = 640
TWO_PI_A = 6.28125
TWO_PI_B = float(np.float32(2 * math.pi - 6.28125))
TWO_PI_C = float(np.float32(2 * math.pi - 6.28125 - TWO_PI_B))
MAGIC = 12582912.0
LAM_INIT = [0.8 - 0.6 * math.exp(-0.3 * l) for l in range(DEPTH)]

GAINS = {}
_at = 0
for _name, _n in (("pre0", KT), ("pre1", KT), ("post0", KT), ("post1", KT), ("mixpre0", KT), ("mixpre1", KT),
                  ("mixpost0", KT), ("mixpost1", KT), ("ffnpre0", KT), ("ffnpre1", KT), ("ffnpost0", KT),
                  ("ffnpost1", KT), ("kv", KT), ("mlaq0", 2), ("mlaq1", 2), ("mlakv0", 1), ("mlakv1", 1),
                  ("subln0", 1), ("subln1", 1), ("gn", 16), ("conv0", 4 * FT), ("conv1", 4 * FT)):
    GAINS[_name] = _at
    _at += _n
NGAIN = _at

STREAM = []
for _l in range(DEPTH):
    STREAM += [(f"lat{_l}", 7, 8), (f"da{_l}", 16, 8), (f"mla{_l}", 8, 8), (f"sw{_l}", 8, 8),
               (f"gate{_l}", 24, 12), (f"wout{_l}", 8, 8), (f"ple{_l}", 8, 10)]
STREAM += [("ret", 48, 8), ("retout", 16, 8), ("up0", 44, 8), ("down0", 16, FH),
           ("dil", 48, 12), ("wo", 8, 8), ("up1", 44, 8), ("down1", 16, FH)]
WIDTH = [w for _, n, w in STREAM for _ in range(n)]

SEMAPHORES = (
    "loaded", "scratch", "spread", "biased", "raw0", "raw1",
    "hi_done", "lo_done", "chunk_done",
    "dve_step", "act_step",
    "evicted",
    "squared", "summed", "var_ready", "std_ready",
    "operand",
    "s_ready", "scored", "exped", "probs", "turned", "pt_copied", "pv_done", "o_used",
    "v_turned", "v_token", "z_ready", "gate_in", "gate", "swapped", "rotated", "y_copied", "centred",
    "small",
    "stage_pe", "stage_act", "stage_dve",
    "stage_loads", "stored", "waits_passed",
)
CREDITS = {"chunk_done": RING, "lo_done": RING, "evicted": LBANKS, "scored": 2, "turned": 4,
           "pt_copied": 1, "pv_done": 2, "o_used": 1}
ALIASES = {"slot_free": "chunk_done", "raw_free": "lo_done"}


STAGES = ["setup"]
for _l in range(DEPTH):
    STAGES += [f"{_s}{_l}" for _s in ("pre", "lat", "da", "mla", "sw", "gate", "wout", "post", "ple")]
STAGES += ["pre_ret", "ret", "retout", "post_ret", "preffn0", "up0", "down0", "postffn0",
           "pre_dil", "dil", "wo", "post_dil", "preffn1", "up1", "down1", "postffn1"]
N_STAGES = len(STAGES)
STAGE = {n: i for i, n in enumerate(STAGES)}


class Tally:

    def __init__(self, eng):
        self.eng = eng
        self.base, self.k = {}, {}
        self.c = 0

    def up(self, name, n=1):
        self.k[name] = self.k.get(name, 0) + n

    def add(self, name, n):
        self.up(name, n)
        return n

    def one(self, name):
        return self.add(name, 1)

    def at(self, name, plus=0):
        value = self.base.get(name, 0) + self.k.get(name, 0) + plus
        assert not isinstance(value, int) or value > 0, (name, value)
        return value

    def turns(self, n, body):
        before, c0 = dict(self.k), self.c
        body(0)
        per = {s: v - before.get(s, 0) for s, v in self.k.items()}
        per_c = self.c - c0
        assert n == 1 or per_c % RING == 0
        if n > 2:
            outer = dict(self.base)
            for s in per:
                self.k[s] = 0
            with self.eng.Fori(1, n - 1) as i:
                for s, v in per.items():
                    self.base[s] = outer.get(s, 0) + before.get(s, 0) + i * v if v else outer.get(s, 0) + before.get(s, 0)
                body(i)
            for s, v in per.items():
                assert self.k[s] == v, (s, self.k[s], v)
                self.base[s] = outer.get(s, 0)
                self.k[s] = before.get(s, 0) + (n - 1) * v
            self.c = c0 + (n - 1) * per_c
        if n > 1:
            body(n - 1)


def rel_window(n):
    return n - 1 - np.arange(RV)


def constants():
    f = np.float32
    c = {}
    rel = rel_window(SEQ)
    n = np.maximum(rel, 0)
    large = 16 + (np.log(np.maximum(n, 1).astype(f) / f(16)) / f(math.log(8.0)) * f(16)).astype(np.int32)
    bucket = np.where(n < 16, n, np.minimum(large, BUCKETS - 1))
    for name, valid in (("oh_full", rel >= 0), ("oh_window", (rel >= 0) & (rel < 128))):
        oh = np.zeros((BUCKETS + 1, RV), f)
        oh[bucket[valid], np.nonzero(valid)[0]] = 1.0
        oh[BUCKETS, ~valid] = NEG
        c[name] = oh
    q, k = np.arange(P)[:, None], np.arange(SEQ)[None, :]
    rel = SEQ - P + q - k
    c["masks"] = np.stack([np.where(ok, f(0), f(NEG)) for ok in (
        rel >= 0, (rel >= 0) & (rel <= 128), (rel >= 0) & (rel % 4 == 0), (rel >= 0) & (rel % 16 == 0))], 1)
    p = np.arange(P)
    inv = (10000.0 ** (-np.arange(HALF, dtype=np.float64) / HALF)).astype(f)
    sign = np.where(p % ROPE < HALF, -1.0, 1.0)
    c["columns"] = np.stack([inv[p % HALF], sign], 1).astype(f)
    c["ident"] = np.eye(P, dtype=f)
    pos = np.arange(SEQ, dtype=f)[None, :]
    ret = (1.0 / (10000.0 ** np.linspace(0.0, 1.0, P, dtype=np.float64))).astype(f)
    ang = (pos * ret[:, None]).astype(np.float64)
    c["ret_angles"] = np.stack([np.cos(ang), np.sin(ang)], 1).astype(f)
    gamma = 1.0 - 2.0 ** (-5.0 - np.arange(RET_HEADS))
    diff = np.arange(SEQ)[None, :] - p[:, None]
    c["decay"] = np.stack([np.where(diff >= 0, g ** np.maximum(diff, 0), 0.0) / 16.0 for g in gamma]).astype(f)
    inv2 = (500000.0 ** (-np.arange(0, 16, 2, dtype=np.float64) / 16)).astype(f)
    r = p % HEAD
    ang = (pos * inv2[r % 8][:, None]).astype(np.float64)
    rot = (r < 16)[:, None]
    c["dil_angles"] = np.stack([np.where(rot, np.cos(ang), 1.0),
                                np.where(rot, np.sin(ang) * np.where(r < 8, -1.0, 1.0)[:, None], 0.0)], 1).astype(f)
    perm = np.zeros((P, P), f)
    for m in range(P):
        if m % HEAD < 16:
            perm[m + 8 if m % HEAD < 8 else m - 8, m] = 1.0
    c["perm"] = perm
    return {k: np.ascontiguousarray(v.astype(f)) for k, v in c.items()}


CONSTANTS = ("oh_full", "oh_window", "masks", "columns", "ident", "ret_angles", "decay", "dil_angles", "perm")


def two_stacks_kernel(nc, d, out):
    scratch = nc.dram_tensor("bias_vectors", (2, BHEADS, RV), F32, kind="Internal").ap()
    copies = nc.dram_tensor("bias_copies", (BHEADS, P, RV), F32, kind="Internal").ap()
    with ExitStack() as ctx:
        sems = {n: ctx.enter_context(nc.semaphore(n)) for n in SEMAPHORES}
        sems |= {a: sems[n] for a, n in ALIASES.items()}

        def sb(name, shape, dt=F32):
            return ctx.enter_context(nc.sbuf_tensor(name, shape, dt))

        X = sb("x_res", [P, KT, SEQ])
        HH = sb("h_hi", [P, KT, SEQ], F32R)
        HL = sb("h_lo", [P, KT, SEQ], F32R)
        RAW = [sb(f"w_raw{s}", [P, SLOT * P]) for s in range(RING)]
        WH = [sb(f"w_hi{s}", [P, SLOT * P], F32R) for s in range(RING)]
        WL = [sb(f"w_lo{s}", [P, SLOT * P], F32R) for s in range(RING)]
        G = sb("gains", [P, NGAIN])
        COLS = sb("columns", [P, 2])
        ID = sb("ident", [P, P])
        ONES = sb("ones", [P, P])
        RSTD = sb("rstd", [P, SEQ])
        RSTD2 = sb("rstd2", [P, SEQ])
        VAR = sb("var", [P, SEQ])
        TA = sb("ta", [P, SEQ])
        TB = sb("tb", [P, SEQ])
        TC = sb("tc", [P, SEQ])
        SM = sb("small_columns", [P, 64])
        arena_bytes = 54 * SEQ * 4
        base = -(-nc.sbuf_base // 32) * 32
        sb("arena", [P, arena_bytes // 4])

        def at(name, shape, offset, dt=F32):
            size = int(np.prod(shape[1:])) * 4
            assert offset + size <= arena_bytes, (name, offset + size, arena_bytes)
            return nc.alloc_sbuf_tensor_at(name, shape, dt, offset=base + offset)

        T1 = SEQ * 4
        ZH = at("zo_hi", [P, 12, SEQ], 0, F32R)
        ZL = at("zo_lo", [P, 12, SEQ], 12 * T1, F32R)
        M1 = at("m1", [P, KT, SEQ], 0)
        SQ1 = at("sq1", [P, KT, SEQ], KT * T1)
        o = 24 * T1
        YH = at("y_hi", [P, KT, SEQ], o, F32R)
        YL = at("y_lo", [P, KT, SEQ], o + KT * T1, F32R)
        PX = at("ple_raw", [P, 2, SEQ], o)
        PH = at("ple_hi", [P, 2, SEQ], o + 2 * T1, F32R)
        PL = at("ple_lo", [P, 2, SEQ], o + 4 * T1, F32R)
        QNH = at("qn_hi", [P, 2, SEQ], o, F32R)
        QNL = at("qn_lo", [P, 2, SEQ], o + 2 * T1, F32R)
        KNH = at("kvn_hi", [P, 1, SEQ], o + 4 * T1, F32R)
        KNL = at("kvn_lo", [P, 1, SEQ], o + 5 * T1, F32R)
        KR = at("k_rope", [P, SEQ], o + 6 * T1)
        CK = at("c_k", [P, SEQ], o + 7 * T1)
        CV = at("c_v", [P, QT, P], o + 8 * T1)
        LQ = at("lat_q", [P, 3, SEQ], o + 9 * T1)
        AQ = at("att_q", [P, SEQ], o + 9 * T1)
        AK = at("att_k", [P, SEQ], o + 10 * T1)
        AR = at("att_qr", [P, SEQ], o + 11 * T1)
        BT = AR
        VF = RSTD2
        VT = at("att_vt", [P, QT, P], o + 12 * T1)
        SS = [at(f"probs{n}", [P, SEQ], o + (13 + n) * T1) for n in range(4)]
        PT = [at(f"pt{n}", [P, SEQ], o + (17 + n) * T1) for n in range(2)]
        COS = at("cos", [P, SEQ], o + 19 * T1)
        SIN = at("sin", [P, SEQ], o + 20 * T1)
        MASK = at("mask", [P, SEQ], o + 21 * T1)
        BDA = at("bias_da", [P, 4, SEQ], o + 22 * T1)
        BSW = at("bias_sw", [P, 4, SEQ], o + 26 * T1)
        POSI = at("pos_i", [P, SEQ], 0, I32)
        ANG = at("ang", [P, SEQ], T1)
        OHF = at("oh_full_sb", [BUCKETS + 1, RV], 2 * T1)
        OHW = at("oh_window_sb", [BUCKETS + 1, RV], 4 * T1)
        TAB = at("table", [BUCKETS + 1, BHEADS], 6 * T1)
        RVF = at("rv_full", [BHEADS, RV], 7 * T1)
        RVW = at("rv_window", [BHEADS, RV], 9 * T1)
        LAM = at("lam_in", [P, DEPTH, 4, HEAD], 11 * T1)
        RH = at("ret_hi", [P, 16, SEQ], 0, F32R)
        RL = at("ret_lo", [P, 16, SEQ], 16 * T1, F32R)
        RQ = at("ret_q", [P, 2, SEQ], 32 * T1)
        RK = at("ret_k", [P, 2, SEQ], 34 * T1)
        RY = at("ret_y", [P, QT, SEQ], 32 * T1)
        RVT = at("ret_vt", [P, QT, RET_V], 36 * T1)
        RSQ = at("ret_sq", [P, QT, SEQ], 36 * T1)
        RP = at("ret_p", [P, QT, SEQ], 40 * T1)
        RVF2 = at("ret_vf", [P, SEQ], 44 * T1)
        RC = at("ret_cos", [P, SEQ], 45 * T1)
        RS = at("ret_sin", [P, SEQ], 46 * T1)
        RD = at("ret_decay", [P, RET_HEADS, SEQ], 47 * T1)
        FHI = at("f_hi", [P, FT, SEQ], 0, F32R)
        FLO = at("f_lo", [P, FT, SEQ], FT * T1, F32R)
        M2 = at("m2", [P, KT, SEQ], 2 * FT * T1)
        SQ2 = at("sq2", [P, KT, SEQ], 0)
        GE = [at(f"conv_in{n}", [P, SEQ + 2], (2 * FT + 2 * n) * T1) for n in range(2)]
        CO = [at(f"conv_out{n}", [P, SEQ], (2 * FT + 4 + n) * T1) for n in range(2)]
        GL = [at(f"gelu{n}", [P, SEQ], (2 * FT + 6 + n) * T1) for n in range(2)]
        DH = at("dil_hi", [P, KT, SEQ], 0, F32R)
        DL = at("dil_lo", [P, KT, SEQ], KT * T1, F32R)
        H2H = at("h2_hi", [P, KT, SEQ], 16 * T1, F32R)
        H2L = at("h2_lo", [P, KT, SEQ], 24 * T1, F32R)
        DQ = at("dil_q", [P, 3, SEQ], 32 * T1)
        DK = at("dil_k", [P, 3, SEQ], 35 * T1)
        DVT = at("dil_vt", [P, 3, QT, P], 38 * T1)
        DP = [at(f"dil_p{n}", [P, 10 * P], 41 * T1 + n * 5 * P * 8) for n in range(2)]
        DPT = [at(f"dil_pt{n}", [P, SEQ], 46 * T1 + n * T1) for n in range(3)]
        DC = at("dil_cos", [P, SEQ], 49 * T1)
        DS = at("dil_sin", [P, SEQ], 50 * T1)
        DM = [at("dil_mask0", [P, 2 * P], 51 * T1), at("dil_mask1", [P, SEQ], 52 * T1),
              at("dil_mask2", [P, SEQ], 53 * T1)]
        PERM = at("perm_sb", [P, P], 51 * T1 + T1 // 2)
        DF = RSTD2

        MX, NM, DEN, ES, RC1, SINK, ST, NST, LAMC, SUBG = 0, 8, 16, 24, 32, 40, 48, 50, 56, 58

        def sm(c, n=1):
            return SM[:, c:c + n]

        def gain(name, k=0):
            c = GAINS[name] + k
            return G[:, c:c + 1]

        banks = [ctx.enter_context(nc.psum_tensor(f"bank{b}", [P, SEQ], F32)) for b in range(8)]
        block = ctx.enter_context(nc.Block())

        @block.sync
        def _(sp):
            t = Tally(sp)
            for dst, src in ((X[:], d["x_t"]), (G[:], d["gains"]), (COLS[:], d["columns"]), (ID[:], d["ident"]),
                             (POSI[:], d["positions"].to_broadcast([P, SEQ])), (OHF[:], d["oh_full"]),
                             (OHW[:], d["oh_window"]), (TAB[0:BUCKETS, :], d["rel_bias"]),
                             (LAM[:].rearrange("p a b c -> p (a b c)"),
                              d["da_lambda"].to_broadcast([P, DEPTH * 4 * HEAD])),
                             (MASK[:], d["masks"][:, 0, :])):
                sp.dma_start(dst, src).then_inc(sems["loaded"], t.add("loaded", 16))

            def load(w, width, i):
                slot = t.c % RING
                t.up("raw_free")
                sp.wait_ge(sems["raw_free"], t.at("raw_free"))
                src = w[i] if isinstance(i, int) else w[bass.ds(i, 1), :, :].rearrange("o p n -> p (o n)")
                sp.dma_start(RAW[slot][:, 0:width * P], src).then_inc(sems[f"raw{slot}"], t.add(f"raw{slot}", 16))
                t.c += 1

            for name, n, width in STREAM:
                w = d["w_" + name]

                def pair(i):
                    load(w, width, 2 * i)
                    load(w, width, 2 * i + 1)
                t.turns(n // 2, pair)
                if n % 2:
                    load(w, width, n - 1)
            t.up("stage_dve", N_STAGES)
            sp.wait_ge(sems["stage_dve"], t.at("stage_dve"))
            sp.dma_start(out, X[:]).then_inc(sems["stored"], t.add("stored", 16))
            sp.wait_ge(sems["stored"], t.at("stored"))

        @block.gpsimd
        def _(pool):
            t = Tally(pool)

            def after(stage):
                pool.wait_ge(sems["stage_pe"], stage)
                pool.wait_ge(sems["stage_act"], stage)
                pool.wait_ge(sems["stage_dve"], stage)

            def fetch(dst, src):
                pool.dma_start(dst, src).then_inc(sems["stage_loads"], t.add("stage_loads", 16))

            t.up("scratch", 32)
            pool.wait_ge(sems["scratch"], t.at("scratch"))
            for h in range(BHEADS):
                pool.dma_start(copies[h], scratch[0 if h < 4 else 1, h:h + 1, :].to_broadcast([P, RV])).then_inc(sems["spread"], t.add("spread", 16))
            pool.wait_ge(sems["spread"], t.at("spread"))

            def window(h, start, n):
                return bass.AP(copies.tensor, h * P * RV + start, [[RV - 1, P], [1, n]])

            for h in range(4):
                pool.dma_start(BDA[:, h, :], window(h, P - 1, SEQ)).then_inc(sems["biased"], t.add("biased", 16))
            for h in range(8):
                pool.dma_start(BSW[:, h % 4, h // 4 * 2 * P:(h // 4 + 1) * 2 * P],
                        window(4 + h, SEQ // 2 + P - 1, 2 * P)).then_inc(sems["biased"], t.add("biased", 16))
            for l in range(DEPTH):
                after(STAGE[f"lat{l}"])
                for h in range(8):
                    fetch(sm(SINK + 2 * (h % 4) + h // 4), d["sw_sinks"][l:l + 1, h:h + 1].to_broadcast([P, 1]))
                after(STAGE[f"ple{l}"])
                fetch(PX[:], d["p_t"][l])
            after(STAGE["ret"])
            fetch(RC[:], d["ret_angles"][:, 0, :])
            fetch(RS[:], d["ret_angles"][:, 1, :])
            fetch(RD[:], d["decay"].rearrange("h p n -> p h n"))
            after(STAGE["dil"])
            fetch(DC[:], d["dil_angles"][:, 0, :])
            fetch(DS[:], d["dil_angles"][:, 1, :])
            fetch(DM[0][:], d["masks"][:, 1, SEQ - 2 * P:SEQ])
            fetch(DM[1][:], d["masks"][:, 2, :])
            fetch(DM[2][:], d["masks"][:, 3, :])
            fetch(PERM[:], d["perm"])

        def run(e):
            def stage(name, f, *args):
                assert STAGES[e.stage] == name
                e.stage += 1
                if e.stage > 1:
                    e.begin_stage()
                f(*args)
                e.end()
                for s in ("stage_pe", "stage_act", "stage_dve"):
                    if s != e.mine:
                        e.t.up(s)

            stage("setup", e.setup)
            for l in range(DEPTH):
                stage(f"pre{l}", e.prenorm, [(HH, HL, f"pre{l}")], SQ1)
                stage(f"lat{l}", e.latents, l)
                stage(f"da{l}", e.attention, "da", l)
                stage(f"mla{l}", e.attention, "mla", l)
                stage(f"sw{l}", e.attention, "sw", l)
                stage(f"gate{l}", e.gates, l)
                stage(f"wout{l}", e.linear, 1, YH, YL, M1)
                stage(f"post{l}", e.postnorm, M1, SQ1, f"post{l}")
                stage(f"ple{l}", e.ple, l)
            stage("pre_ret", e.prenorm, [(HH, HL, "mixpre0")], SQ1)
            stage("ret", e.retention)
            stage("retout", e.linear, 2, RH, RL, M2)
            stage("post_ret", e.postnorm, M2, SQ2, "mixpost0")
            for l in range(DEPTH):
                if l == 1:
                    stage("pre_dil", e.prenorm, [(HH, HL, "kv"), (H2H, H2L, "mixpre1")], SQ2)
                    stage("dil", e.dilated)
                    stage("wo", e.linear, 1, DH, DL, M2)
                    stage("post_dil", e.postnorm, M2, SQ2, "mixpost1")
                stage(f"preffn{l}", e.prenorm, [(HH, HL, f"ffnpre{l}")], SQ2)
                stage(f"up{l}", e.ffn_up, l)
                stage(f"down{l}", e.linear, 2, FHI, FLO, M2)
                stage(f"postffn{l}", e.postnorm, M2, SQ2, f"ffnpost{l}")

        def key_blocks(kind, i):
            n = min(i + 1, 2) if kind == "sw" else i + 1
            return i + 1 - n, n

        DILS = ((4, 5, 3), (0, 1, 2))

        def dil_width(i):
            return (key_blocks("sw", i)[1] + 2 * (i + 1)) * P

        UNITS = [(i, m) for i in range(QT) for m in range(2)]

        @block.tensor
        def _(pe):
            t = Tally(pe)

            class Programs:
                mine, stage = "stage_pe", 0

                def begin_stage(self):
                    pe.wait_ge(sems["stage_pe"], t.at("stage_pe"))
                    pe.wait_ge(sems["stage_act"], t.at("stage_act"))
                    pe.wait_ge(sems["stage_dve"], t.at("stage_dve"))

                def end(self):
                    pe.drain().then_inc(sems["stage_pe"], t.one("stage_pe"))

                def setup(self):
                    for n, c in (("chunk_done", RING), ("turned", 4), ("pv_done", 2)):
                        pe.sem_inc(sems[n], c)
                    t.up("loaded", 160)
                    pe.wait_ge(sems["loaded"], t.at("loaded"))
                    t.up("operand")
                    pe.wait_ge(sems["operand"], t.at("operand"))
                    for n, oh in enumerate((OHF, OHW)):
                        for h in range(2):
                            ins = pe.matmul(banks[2 * n + h][0:BHEADS, 0:RV // 2], TAB[:], oh[:, h * RV // 2:(h + 1) * RV // 2],
                                            start=True, stop=True)
                    ins.then_inc(sems["small"], t.one("small"))
                    t.up("operand", 2)

                def products(self, bank, tile, width, hi, lo, k, start, stop):
                    slot = t.c % RING
                    w = slice(tile * P, (tile + 1) * P)
                    pe.matmul(banks[bank][:], WH[slot][:, w], hi[:, k, :], start=start, stop=False)
                    pe.matmul(banks[bank][:], WH[slot][:, w], lo[:, k, :], start=False, stop=False)
                    return pe.matmul(banks[bank][:], WL[slot][:, w], hi[:, k, :], start=False, stop=stop)

                def begin(self):
                    t.up("lo_done")
                    pe.wait_ge(sems["lo_done"], t.at("lo_done", CREDITS["lo_done"]))

                def finish(self, ins):
                    ins.then_inc(sems["chunk_done"], t.one("chunk_done"))
                    t.c += 1

                def bank_free(self, of=LBANKS):
                    t.up("evicted")
                    pe.wait_ge(sems["evicted"], t.at("evicted", LBANKS - of))

                def whole(self, bank, hi=HH, lo=HL, of=LBANKS):
                    self.bank_free(of)
                    self.begin()
                    for k in range(KT):
                        ins = self.products(bank, k, 8, hi, lo, k, k == 0, k == KT - 1)
                    self.finish(ins)

                def sums(self, bank, n, src, name="squared"):
                    for k in range(n):
                        t.up(name)
                        pe.wait_ge(sems[name], t.at(name))
                        ins = pe.matmul(banks[bank][:], ONES[:], src(k), start=(k == 0), stop=(k == n - 1))
                    ins.then_inc(sems["summed"], t.one("summed"))

                def prenorm(self, targets, sq):
                    self.sums(OUTB, KT, lambda k: sq[:, k, :])

                def postnorm(self, m, sq, g):
                    self.sums(OUTB, KT, lambda k: sq[:, k, :])

                def turn_v(self, src):
                    for b in range(QT):
                        ins = pe.transpose(banks[TURN][:, b * P:(b + 1) * P], src[:, b * P:(b + 1) * P], ID[:])
                    ins.then_inc(sems["v_turned"], t.one("v_turned"))

                def latents(self, l):
                    for j in range(7):
                        self.whole(j % LBANKS)
                    pe.wait_ge(sems["evicted"], t.at("evicted", LBANKS))
                    self.turn_v(VF)
                    t.up("v_token")
                    t.up("operand")
                    self.sums(OUTB, 2, lambda k: SS[k][:])
                    self.sums(S0, 1, lambda k: SS[2][:])

                def attention(self, kind, l):
                    def s_unit(i, m):
                        kb, n = key_blocks(kind, i)
                        r = slice(64 * m, 64 * m + 64)
                        keys = CK if kind == "sw" else AK
                        t.up("scored")
                        pe.wait_ge(sems["scored"], t.at("scored"))
                        q = slice(i * P, (i + 1) * P)
                        kk = slice(kb * P, (kb + n) * P)
                        o_ = banks[S0 + m][:, 0:n * P]
                        ins = pe.matmul(o_, AQ[r, q], keys[r, kk], start=True, stop=(kind != "mla"))
                        if kind == "mla":
                            rr = slice(64 * m, 64 * m + ROPE)
                            ins = pe.matmul(o_, AR[rr, q], KR[rr, kk], start=False, stop=True)
                        ins.then_inc(sems["s_ready"], t.one("s_ready"))

                    def t_unit(u, i):
                        _, n = key_blocks(kind, i)
                        t.up("probs")
                        pe.wait_ge(sems["probs"], t.at("probs"))
                        t.up("pt_copied")
                        pe.wait_ge(sems["pt_copied"], t.at("pt_copied"))
                        for b in range(n):
                            ins = pe.transpose(banks[TURN][:, b * P:(b + 1) * P], SS[u % 4][:, b * P:(b + 1) * P], ID[:])
                        ins.then_inc(sems["turned"], t.one("turned"))

                    def pv_unit(n_unit, i, m):
                        kb, n = key_blocks(kind, i)
                        pe.wait_ge(sems["pt_copied"], t.at("pt_copied", CREDITS["pt_copied"]))
                        for b in range(n):
                            v = (CV if kind == "sw" else VT)[:, kb + b, :]
                            if kind != "da":
                                v = v[:, 64 * m:64 * m + 64]
                            r = slice(0, P) if kind == "da" else slice(64 * m, 64 * m + 64)
                            ins = pe.matmul(banks[OUTB][r, i * P:(i + 1) * P], v, PT[n_unit % 2][:, b * P:(b + 1) * P],
                                            start=(b == 0), stop=(b == n - 1))
                        ins.then_inc(sems["pv_done"], t.one("pv_done"))

                    def body(it):
                        if kind == "da":
                            for b in range(4):
                                self.whole(b)
                        elif kind == "sw":
                            for b in range(2):
                                self.whole(b)
                            t.up("evicted", 2)
                        else:
                            self.begin()
                            for b, (n, k0, hi, lo) in enumerate(((2, 0, QNH, QNL), (2, 2, QNH, QNL), (2, 4, QNH, QNL), (1, 6, KNH, KNL))):
                                self.bank_free()
                                for k in range(n):
                                    self.products(b, k0 + k, 8, hi, lo, k, k == 0, k == n - 1)
                            self.finish(self.products(S0, 7, 8, KNH, KNL, 0, True, True))
                            t.up("evicted")
                            self.whole(0, of=5)
                            t.up("evicted", 2)
                        if kind != "sw":
                            pe.wait_ge(sems["evicted"], t.at("evicted", LBANKS - (1 if kind == "da" else 3)))
                            self.turn_v(VF)
                            t.up("v_token")
                            pe.wait_ge(sems["v_token"], t.at("v_token"))
                        pe.wait_ge(sems["evicted"], t.at("evicted", LBANKS))
                        t.up("o_used")
                        pe.wait_ge(sems["o_used"], t.at("o_used"))
                        if kind == "da":
                            s_unit(0, 0)
                            s_unit(0, 1)
                            for i in range(QT):
                                if i + 1 < QT:
                                    s_unit(i + 1, 0)
                                    s_unit(i + 1, 1)
                                t_unit(2 * i, i)
                                pv_unit(i, i, 0)
                            self.sums(S0, 1, lambda k: TA[:])
                        else:
                            s_unit(0, 0)
                            for u, (i, m) in enumerate(UNITS):
                                if u + 1 < len(UNITS):
                                    s_unit(*UNITS[u + 1])
                                t_unit(u, i)
                                pv_unit(u, i, m)
                    t.turns(4, body)

                def gates(self, l):
                    def body(it):
                        for j in range(6):
                            b, g = j % 3, 2 * (j % 2)
                            self.bank_free(2)
                            self.begin()
                            for k in range(KT):
                                self.products(g, k, 12, HH, HL, k, k == 0, k == KT - 1)
                            for k in range(4):
                                ins = self.products(g + 1, KT + k, 12, ZH, ZL, 4 * b + k, k == 0, k == 3)
                            self.finish(ins)
                    t.turns(4, body)

                def linear(self, parts, hi, lo, m):
                    def body(it):
                        for j in range(2):
                            self.bank_free(2)
                            for c in range(parts):
                                self.begin()
                                n = WIDTH[t.c]
                                for k in range(n):
                                    ins = self.products(j, k, n, hi, lo, c * n + k, c + k == 0, c == parts - 1 and k == n - 1)
                                self.finish(ins)
                    t.turns(4, body)

                def ple(self, l):
                    t.up("operand", 10)
                    pe.wait_ge(sems["operand"], t.at("operand"))

                    def body(it):
                        for j in range(2):
                            self.bank_free(2)
                            self.begin()
                            for k in range(KT):
                                self.products(2 * j, k, 10, HH, HL, k, k == 0, k == KT - 1)
                            for k in range(2):
                                ins = self.products(2 * j + 1, KT + k, 10, PH, PL, k, k == 0, k == 1)
                            self.finish(ins)
                    t.turns(4, body)

                def ffn_up(self, l):
                    def body(it):
                        for j in range(2):
                            self.whole(2 * j)
                            self.whole(2 * j + 1)
                    t.turns(FT // 2, body)

                def retention(self):
                    def body(h):
                        for j in range(4):
                            self.whole(j)
                        for j in range(4):
                            self.whole(j)
                            pe.wait_ge(sems["evicted"], t.at("evicted", LBANKS))
                            if j:
                                pe.wait_ge(sems["v_token"], t.at("v_token"))
                            self.turn_v(RVF2)
                            t.up("v_token")
                        t.up("rotated", 4)
                        pe.wait_ge(sems["rotated"], t.at("rotated"))
                        for kt in range(QT):
                            if kt >= 2:
                                t.up("operand")
                                pe.wait_ge(sems["operand"], t.at("operand"))
                            n = SEQ - kt * P
                            for c in range(2):
                                ins = pe.matmul(banks[S0 + kt % 2][:, 0:n], RK[:, c, kt * P:(kt + 1) * P],
                                                RQ[:, c, kt * P:SEQ], start=(c == 0), stop=(c == 1))
                            ins.then_inc(sems["s_ready"], t.one("s_ready"))
                        t.up("operand", 2)
                        pe.wait_ge(sems["operand"], t.at("operand"))
                        pe.wait_ge(sems["v_token"], t.at("v_token"))
                        for e in range(4):
                            t.up("y_copied")
                            if e >= 2:
                                pe.wait_ge(sems["y_copied"], t.at("y_copied", -2))
                            for kt in range(QT):
                                ins = pe.matmul(banks[TURN + e % 2][:, kt * P:SEQ], RVT[:, kt, e * P:(e + 1) * P],
                                                RP[:, kt, kt * P:SEQ], start=(kt == 0), stop=(kt == QT - 1))
                            ins.then_inc(sems["small"], t.one("small"))
                        for j in range(4):
                            self.whole(j)
                        pe.wait_ge(sems["y_copied"], t.at("y_copied"))
                        for e in range(4):
                            ins = pe.matmul(banks[S0][:], ONES[:], RY[:, e, :], start=(e == 0), stop=(e == 3))
                        ins.then_inc(sems["small"], t.one("small"))
                        self.sums(S0 + 1, 4, lambda e: RSQ[:, e, :])
                    t.turns(RET_HEADS, body)

                def dilated(self):
                    def group(g):
                        for a in range(3):
                            hi, lo = (H2H, H2L) if a == 0 else (HH, HL)
                            self.bank_free(3)
                            for k in range(KT):
                                n = a * KT + k
                                if n % 12 == 0:
                                    self.begin()
                                ins = self.products(a, n % 12, 12, hi, lo, k, k == 0, k == KT - 1)
                                if n % 12 == 11:
                                    self.finish(ins)
                        for a in range(2):
                            t.up("operand")
                            pe.wait_ge(sems["operand"], t.at("operand"))
                            pe.matmul(banks[3][:], PERM[:], (TA if a == 0 else TB)[:], start=True, stop=True).then_inc(sems["swapped"], t.one("swapped"))
                            t.up("rotated")
                            pe.wait_ge(sems["rotated"], t.at("rotated"))
                        pe.wait_ge(sems["evicted"], t.at("evicted", LBANKS))
                        self.turn_v(DF)
                        t.up("v_token")
                        pe.wait_ge(sems["v_token"], t.at("v_token"))

                    def s_unit(u):
                        i, m = UNITS[u]
                        r = slice(64 * m, 64 * m + 64)
                        t.up("scored")
                        pe.wait_ge(sems["scored"], t.at("scored"))
                        for g in range(3):
                            kb, n = key_blocks("sw" if g == 0 else "da", i)
                            ins = pe.matmul(banks[DILS[u % 2][g]][:, 0:n * P], DQ[r, g, i * P:(i + 1) * P],
                                            DK[r, g, kb * P:(kb + n) * P], start=True, stop=True)
                        ins.then_inc(sems["s_ready"], t.one("s_ready"))

                    def t_unit(u):
                        i, m = UNITS[u]
                        t.up("probs")
                        pe.wait_ge(sems["probs"], t.at("probs"))
                        at_ = 0
                        for g in range(3):
                            _, n = key_blocks("sw" if g == 0 else "da", i)
                            t.up("pt_copied")
                            pe.wait_ge(sems["pt_copied"], t.at("pt_copied"))
                            for b in range(n):
                                ins = pe.transpose(banks[TURN][:, b * P:(b + 1) * P], DP[u % 2][:, at_ + b * P:at_ + (b + 1) * P], ID[:])
                            ins.then_inc(sems["turned"], t.one("turned"))
                            at_ += n * P

                    def pv_unit(u):
                        i, m = UNITS[u]
                        pe.wait_ge(sems["pt_copied"], t.at("pt_copied", CREDITS["pt_copied"]))
                        r = slice(64 * m, 64 * m + 64)
                        for g in range(3):
                            kb, n = key_blocks("sw" if g == 0 else "da", i)
                            for b in range(n):
                                ins = pe.matmul(banks[OUTB][r, i * P:(i + 1) * P], DVT[:, g, kb + b, 64 * m:64 * m + 64],
                                                DPT[g][:, b * P:(b + 1) * P], start=(g + b == 0), stop=(g == 2 and b == n - 1))
                        ins.then_inc(sems["pv_done"], t.one("pv_done"))

                    def body(it):
                        for g in range(3):
                            group(g)
                        t.up("o_used")
                        pe.wait_ge(sems["o_used"], t.at("o_used"))
                        s_unit(0)
                        for u in range(len(UNITS)):
                            if u + 1 < len(UNITS):
                                s_unit(u + 1)
                            t_unit(u)
                            pv_unit(u)
                    t.turns(8, body)

            e = Programs()
            e.t = t
            run(e)

        @block.scalar
        def _(act):
            t = Tally(act)

            def hi_part():
                if t.c >= len(WIDTH):
                    return
                slot, n = t.c % RING, WIDTH[t.c] * P
                t.up(f"raw{slot}", 16)
                act.wait_ge(sems[f"raw{slot}"], t.at(f"raw{slot}"))
                t.up("slot_free")
                act.wait_ge(sems["slot_free"], t.at("slot_free"))
                act.copy(WH[slot][:, 0:n], RAW[slot][:, 0:n]).then_inc(sems["hi_done"], t.one("hi_done"))
                t.c += 1

            def std():
                t.up("var_ready")
                act.wait_ge(sems["var_ready"], t.at("var_ready"))
                act.activation(VAR[:], VAR[:], ACT.Sqrt).then_inc(sems["std_ready"], t.one("std_ready"))

            def squares(n, src, dst):
                for k in range(n):
                    act.activation(dst(k), src(k), ACT.Square).then_inc(sems["squared"], t.one("squared"))

            class Programs:
                mine, stage = "stage_act", 0

                def begin_stage(self):
                    act.wait_ge(sems["stage_pe"], t.at("stage_pe"))
                    act.wait_ge(sems["stage_act"], t.at("stage_act"))
                    act.wait_ge(sems["stage_dve"], t.at("stage_dve"))

                def end(self):
                    act.drain().then_inc(sems["stage_act"], t.one("stage_act"))

                def setup(self):
                    act.sem_inc(sems["pt_copied"], 1)
                    hi_part()
                    t.up("operand")
                    t.up("var_ready")
                    act.wait_ge(sems["var_ready"], t.at("var_ready"))
                    act.activation(SIN[:], TA[:], ACT.Sin).then_inc(sems["std_ready"], t.one("std_ready"))
                    act.activation(COS[:], TB[:], ACT.Sin).then_inc(sems["std_ready"], t.one("std_ready"))
                    t.up("var_ready")
                    act.wait_ge(sems["var_ready"], t.at("var_ready"))
                    act.activation(sm(DEN, 4), sm(MX, 4), ACT.Exp).then_inc(sems["std_ready"], t.one("std_ready"))
                    t.up("operand", 2)
                    act.wait_ge(sems["operand"], t.at("operand"))
                    act.dma_start(scratch[0], RVF[:]).then_inc(sems["scratch"], t.add("scratch", 16))
                    act.dma_start(scratch[1], RVW[:]).then_inc(sems["scratch"], t.add("scratch", 16))
                    act.wait_ge(sems["scratch"], t.at("scratch"))
                    t.up("small")

                def prenorm(self, targets, sq):
                    squares(KT, lambda k: X[:, k, :], lambda k: sq[:, k, :])
                    std()

                def postnorm(self, m, sq, g):
                    squares(KT, lambda k: m[:, k, :], lambda k: sq[:, k, :])
                    std()

                def v_out(self, dst):
                    t.up("v_turned")
                    act.wait_ge(sems["v_turned"], t.at("v_turned"))
                    act.copy(dst, banks[TURN][:].rearrange("p (b k) -> p b k", b=QT)).then_inc(sems["v_token"], t.one("v_token"))

                def latents(self, l):
                    for j in range(7):
                        hi_part()
                    self.v_out(CV[:])
                    t.up("operand")
                    act.wait_ge(sems["operand"], t.at("operand"))
                    squares(3, lambda k: LQ[:, k, :], lambda k: SS[k][:])
                    std()
                    std()

                def attention(self, kind, l):
                    def e_unit(u, m):
                        _, n = key_blocks(kind, UNITS[u][0])
                        t.up("scored")
                        act.wait_ge(sems["scored"], t.at("scored", CREDITS["scored"]))
                        if kind == "sw":
                            act.activation(sm(ES + u), sm(ST + m), ACT.Exp, bias=sm(NM + u)).then_inc(sems["act_step"], t.one("act_step"))
                        act.activation(SS[u % 4][:, 0:n * P], SS[u % 4][:, 0:n * P], ACT.Exp, bias=sm(NM + u), accum_out=sm(DEN + u)).then_inc(sems["exped"], t.one("exped"))

                    def c_unit(n_unit, i):
                        _, n = key_blocks(kind, i)
                        t.up("turned")
                        act.wait_ge(sems["turned"], t.at("turned", CREDITS["turned"]))
                        t.up("pv_done")
                        act.wait_ge(sems["pv_done"], t.at("pv_done"))
                        act.copy(PT[n_unit % 2][:, 0:n * P], banks[TURN][:, 0:n * P]).then_inc(sems["pt_copied"], t.one("pt_copied"))

                    def body(it):
                        for _ in range(4 if kind == "da" else 2):
                            hi_part()
                        if kind != "sw":
                            self.v_out(VT[:])
                        t.up("z_ready")
                        act.wait_ge(sems["z_ready"], t.at("z_ready"))
                        act.activation(TC[:], TC[:], ACT.Silu).then_inc(sems["gate"], t.one("gate"))
                        if kind == "da":
                            e_unit(0, 0)
                            e_unit(1, 1)
                            for i in range(QT):
                                if i + 1 < QT:
                                    e_unit(2 * i + 2, 0)
                                    e_unit(2 * i + 3, 1)
                                c_unit(i, i)
                            act.wait_ge(sems["pv_done"], t.at("pv_done", CREDITS["pv_done"]))
                            act.activation(TA[:], banks[OUTB][:], ACT.Square).then_inc(sems["squared"], t.one("squared"))
                            std()
                        else:
                            e_unit(0, 0)
                            for u, (i, m) in enumerate(UNITS):
                                if u + 1 < len(UNITS):
                                    e_unit(u + 1, UNITS[u + 1][1])
                                c_unit(u, i)
                    t.turns(4, body)

                def gates(self, l):
                    def body(it):
                        for j in range(6):
                            hi_part()
                            t.up("gate_in")
                            act.wait_ge(sems["gate_in"], t.at("gate_in"))
                            T_ = (TA, TB)[j % 2]
                            act.activation(T_[:], T_[:], ACT.Sigmoid).then_inc(sems["gate"], t.one("gate"))
                    t.turns(4, body)

                def linear(self, parts, hi, lo, m):
                    def body(it):
                        for j in range(2 * parts):
                            hi_part()
                    t.turns(4, body)

                def ple(self, l):
                    def body(it):
                        for j in range(2):
                            hi_part()
                            t.up("chunk_done")
                            act.wait_ge(sems["chunk_done"], t.at("chunk_done", CREDITS["chunk_done"]))
                            act.activation((TA, TB)[j][:], banks[2 * j][:], ACT.Sigmoid).then_inc(sems["gate"], t.one("gate"))
                    t.k["chunk_done"] = t.c - 1
                    t.up("operand", 10)
                    t.turns(4, body)

                def ffn_up(self, l):
                    def body(it):
                        for j in range(2):
                            hi_part()
                            hi_part()
                            t.up("gate_in")
                            act.wait_ge(sems["gate_in"], t.at("gate_in"))
                            act.activation(GL[j][:], CO[j][:], ACT.Gelu_apprx_tanh).then_inc(sems["gate"], t.one("gate"))
                    t.turns(FT // 2, body)

                def retention(self):
                    def body(h):
                        for j in range(4):
                            hi_part()
                        for j in range(4):
                            hi_part()
                            self.v_out(RVT[:, :, j * P:(j + 1) * P])
                        for e in range(4):
                            t.up("small")
                            act.wait_ge(sems["small"], t.at("small"))
                            act.copy(RY[:, e, :], banks[TURN + e % 2][:]).then_inc(sems["y_copied"], t.one("y_copied"))
                        for j in range(4):
                            hi_part()
                        t.up("small")
                        for e in range(4):
                            t.up("centred")
                            act.wait_ge(sems["centred"], t.at("centred"))
                            act.activation(RSQ[:, e, :], RY[:, e, :], ACT.Square).then_inc(sems["squared"], t.one("squared"))
                        std()
                        for e in range(4):
                            t.up("gate_in")
                            act.wait_ge(sems["gate_in"], t.at("gate_in"))
                            T_ = (TA, TB)[e % 2]
                            act.activation(T_[:], T_[:], ACT.Silu).then_inc(sems["gate"], t.one("gate"))
                    t.turns(RET_HEADS, body)

                def dilated(self):
                    def e_unit(u):
                        t.up("scored")
                        act.wait_ge(sems["scored"], t.at("scored", CREDITS["scored"]))
                        w = dil_width(UNITS[u][0])
                        act.activation(DP[u % 2][:, 0:w], DP[u % 2][:, 0:w], ACT.Exp, bias=sm(NM + u), accum_out=sm(DEN + u)).then_inc(sems["exped"], t.one("exped"))

                    def c_unit(u):
                        i, m = UNITS[u]
                        for g in range(3):
                            _, n = key_blocks("sw" if g == 0 else "da", i)
                            t.up("turned")
                            act.wait_ge(sems["turned"], t.at("turned", CREDITS["turned"]))
                            if g == 0:
                                act.wait_ge(sems["pv_done"], t.at("pv_done", CREDITS["pv_done"]))
                            act.copy(DPT[g][:, 0:n * P], banks[TURN][:, 0:n * P]).then_inc(sems["pt_copied"], t.one("pt_copied"))
                        t.up("pv_done")

                    def body(it):
                        for g in range(3):
                            hi_part()
                            hi_part()
                            self.v_out(DVT[:, g])
                        e_unit(0)
                        for u in range(len(UNITS)):
                            if u + 1 < len(UNITS):
                                e_unit(u + 1)
                            c_unit(u)
                    t.turns(8, body)

            e = Programs()
            e.t = t
            run(e)

        @block.vector
        def _(dve):
            t = Tally(dve)

            def lo_part():
                if t.c >= len(WIDTH):
                    return
                slot, n = t.c % RING, WIDTH[t.c] * P
                t.up("hi_done")
                dve.wait_ge(sems["hi_done"], t.at("hi_done"))
                dve.tensor_tensor(WL[slot][:, 0:n], RAW[slot][:, 0:n], WH[slot][:, 0:n].bitcast(F32), ALU.subtract).then_inc(sems["lo_done"], t.one("lo_done"))
                t.c += 1

            def passed():
                dve.sem_inc(sems["waits_passed"], 1)

            def signal(name):
                dve.sem_inc(sems[name], 1)
                t.up(name)

            def chunk():
                t.up("chunk_done")
                dve.wait_ge(sems["chunk_done"], t.at("chunk_done", CREDITS["chunk_done"]))

            def split(hi, lo, src):
                dve.tensor_copy(hi, src).then_inc(sems["dve_step"], t.one("dve_step"))
                dve.wait_ge(sems["dve_step"], t.at("dve_step"))
                dve.tensor_tensor(lo, src, hi.bitcast(F32), ALU.subtract).then_inc(sems["dve_step"], t.one("dve_step"))
                dve.wait_ge(sems["dve_step"], t.at("dve_step"))

            def rstd(bank, n, dst=RSTD):
                t.up("summed")
                dve.wait_ge(sems["summed"], t.at("summed"))
                dve.tensor_scalar(VAR[:], banks[bank][:], 1.0 / n, EPS, ALU.mult, ALU.add).then_inc(sems["var_ready"], t.one("var_ready"))
                t.up("std_ready")
                dve.wait_ge(sems["std_ready"], t.at("std_ready"))
                dve.reciprocal(dst[:], VAR[:]).then_inc(sems["dve_step"], t.one("dve_step"))
                dve.wait_ge(sems["dve_step"], t.at("dve_step"))

            class Programs:
                mine, stage = "stage_dve", 0

                def begin_stage(self):
                    dve.wait_ge(sems["stage_pe"], t.at("stage_pe"))
                    dve.wait_ge(sems["stage_act"], t.at("stage_act"))
                    dve.wait_ge(sems["stage_dve"], t.at("stage_dve"))

                def end(self):
                    dve.drain().then_inc(sems["stage_dve"], t.one("stage_dve"))

                def setup(self):
                    for n, c in (("lo_done", RING), ("evicted", LBANKS), ("scored", 2), ("o_used", 1)):
                        dve.sem_inc(sems[n], c)
                    dve.memset(ONES[:], 1.0).then_inc(sems["dve_step"], t.one("dve_step"))
                    dve.wait_ge(sems["dve_step"], t.at("dve_step"))
                    lo_part()
                    t.up("loaded", 160)
                    dve.wait_ge(sems["loaded"], t.at("loaded"))
                    dve.memset(TAB[BUCKETS:BUCKETS + 1, :], 1.0).then_inc(sems["operand"], t.one("operand"))
                    dve.wait_ge(sems["operand"], t.at("operand"))
                    dve.tensor_copy(ANG[:], POSI[:]).then_inc(sems["dve_step"], t.one("dve_step"))
                    dve.wait_ge(sems["dve_step"], t.at("dve_step"))
                    dve.tensor_scalar(ANG[:], ANG[:], COLS[:, 0:1], None, ALU.mult).then_inc(sems["dve_step"], t.one("dve_step"))
                    dve.wait_ge(sems["dve_step"], t.at("dve_step"))
                    dve.tensor_scalar(TC[:], ANG[:], 1.0 / (2 * math.pi), None, ALU.mult).then_inc(sems["dve_step"], t.one("dve_step"))
                    dve.wait_ge(sems["dve_step"], t.at("dve_step"))
                    dve.tensor_scalar(TC[:], TC[:], MAGIC, None, ALU.add).then_inc(sems["dve_step"], t.one("dve_step"))
                    dve.wait_ge(sems["dve_step"], t.at("dve_step"))
                    dve.tensor_scalar(TC[:], TC[:], -MAGIC, None, ALU.add).then_inc(sems["dve_step"], t.one("dve_step"))
                    dve.wait_ge(sems["dve_step"], t.at("dve_step"))
                    for part in (TWO_PI_A, TWO_PI_B, TWO_PI_C):
                        dve.scalar_tensor_tensor(ANG[:], TC[:], -part, ANG[:], ALU.mult, ALU.add).then_inc(sems["dve_step"], t.one("dve_step"))
                        dve.wait_ge(sems["dve_step"], t.at("dve_step"))
                    dve.tensor_scalar(TB[:], ANG[:], math.pi / 2, None, ALU.add).then_inc(sems["dve_step"], t.one("dve_step"))
                    dve.wait_ge(sems["dve_step"], t.at("dve_step"))
                    dve.tensor_scalar(TC[:], TB[:], math.pi, -2 * math.pi, ALU.is_gt, ALU.mult).then_inc(sems["dve_step"], t.one("dve_step"))
                    dve.wait_ge(sems["dve_step"], t.at("dve_step"))
                    dve.tensor_tensor(TB[:], TB[:], TC[:], ALU.add).then_inc(sems["dve_step"], t.one("dve_step"))
                    dve.wait_ge(sems["dve_step"], t.at("dve_step"))
                    dve.tensor_scalar(TB[:], TB[:], 3.1415925, -3.1415925, ALU.min, ALU.max).then_inc(sems["dve_step"], t.one("dve_step"))
                    dve.wait_ge(sems["dve_step"], t.at("dve_step"))
                    dve.tensor_scalar(TA[:], ANG[:], 3.1415925, -3.1415925, ALU.min, ALU.max).then_inc(sems["var_ready"], t.one("var_ready"))
                    t.up("std_ready", 2)
                    dve.wait_ge(sems["std_ready"], t.at("std_ready"))
                    dve.tensor_scalar(SIN[:], SIN[:], COLS[:, 1:2], None, ALU.mult).then_inc(sems["dve_step"], t.one("dve_step"))
                    dve.wait_ge(sems["dve_step"], t.at("dve_step"))
                    for l in range(DEPTH):
                        for a in range(2):
                            ins = dve.tensor_tensor_reduce(TC[:, 0:HEAD], LAM[:, l, 2 * a, :], LAM[:, l, 2 * a + 1, :], 1.0, 0.0,
                                                           ALU.mult, ALU.add, sm(MX + 2 * l + a))
                            if (l, a) == (DEPTH - 1, 1):
                                ins.then_inc(sems["var_ready"], t.one("var_ready"))
                            else:
                                ins.then_inc(sems["dve_step"], t.one("dve_step"))
                                dve.wait_ge(sems["dve_step"], t.at("dve_step"))
                    t.up("std_ready")
                    dve.wait_ge(sems["std_ready"], t.at("std_ready"))
                    for l in range(DEPTH):
                        dve.tensor_tensor(sm(LAMC + l), sm(DEN + 2 * l + 1), sm(DEN + 2 * l), ALU.subtract).then_inc(sems["dve_step"], t.one("dve_step"))
                        dve.wait_ge(sems["dve_step"], t.at("dve_step"))
                        dve.tensor_scalar(sm(LAMC + l), sm(LAMC + l), -LAM_INIT[l], None, ALU.add).then_inc(sems["dve_step"], t.one("dve_step"))
                        dve.wait_ge(sems["dve_step"], t.at("dve_step"))
                        dve.tensor_scalar(sm(SUBG + l), gain(f"subln{l}"), 1.0 - LAM_INIT[l], None, ALU.mult).then_inc(sems["dve_step"], t.one("dve_step"))
                        dve.wait_ge(sems["dve_step"], t.at("dve_step"))
                    t.up("small")
                    dve.wait_ge(sems["small"], t.at("small"))
                    for n, dst in enumerate((RVF, RVW)):
                        dve.tensor_copy(dst[:, 0:RV // 2], banks[2 * n][0:BHEADS, 0:RV // 2]).then_inc(sems["dve_step"], t.one("dve_step"))
                        dve.wait_ge(sems["dve_step"], t.at("dve_step"))
                        dve.tensor_copy(dst[:, RV // 2:RV], banks[2 * n + 1][0:BHEADS, 0:RV // 2]).then_inc(sems["operand"], t.one("operand"))
                        dve.wait_ge(sems["operand"], t.at("operand"))

                def prenorm(self, targets, sq):
                    for hi, lo, g in targets:
                        for k in range(KT):
                            dve.tensor_scalar(hi[:, k, :], X[:, k, :], gain(g, k), None, ALU.mult).then_inc(sems["dve_step"], t.one("dve_step"))
                        dve.wait_ge(sems["dve_step"], t.at("dve_step"))
                        for k in range(KT):
                            dve.scalar_tensor_tensor(lo[:, k, :], X[:, k, :], gain(g, k), hi[:, k, :].bitcast(F32),
                                    ALU.mult, ALU.subtract).then_inc(sems["dve_step"], t.one("dve_step"))
                    rstd(OUTB, D)

                def postnorm(self, m, sq, g):
                    rstd(OUTB, D)
                    for k in range(KT):
                        dve.scalar_tensor_tensor(m[:, k, :], m[:, k, :], gain(g, k), RSTD[:], ALU.mult, ALU.mult).then_inc(sems["dve_step"], t.one("dve_step"))
                    dve.wait_ge(sems["dve_step"], t.at("dve_step"))
                    for k in range(KT):
                        dve.tensor_tensor(X[:, k, :], X[:, k, :], m[:, k, :], ALU.add).then_inc(sems["dve_step"], t.one("dve_step"))

                def latents(self, l):
                    for j, dst in enumerate((LQ[:, 0, :], LQ[:, 1, :], LQ[:, 2, :], TA[:], TB[:], CK[:], VF[:])):
                        lo_part()
                        chunk()
                        dve.tensor_tensor(dst, banks[j % LBANKS][:], RSTD[:], ALU.mult).then_inc(sems["evicted"], t.one("evicted"))
                        dve.wait_ge(sems["evicted"], t.at("evicted", CREDITS["evicted"]))
                    dve.tensor_tensor(TA[:], TA[:], COS[:], ALU.mult).then_inc(sems["dve_step"], t.one("dve_step"))
                    dve.wait_ge(sems["dve_step"], t.at("dve_step"))
                    dve.tensor_tensor(TB[:], TB[:], SIN[:], ALU.mult).then_inc(sems["dve_step"], t.one("dve_step"))
                    dve.wait_ge(sems["dve_step"], t.at("dve_step"))
                    dve.tensor_tensor(KR[:], TA[:], TB[:], ALU.add).then_inc(sems["operand"], t.one("operand"))
                    dve.wait_ge(sems["operand"], t.at("operand"))
                    rstd(OUTB, 2 * P, RSTD2)
                    for k in range(2):
                        dve.scalar_tensor_tensor(TA[:], LQ[:, k, :], gain(f"mlaq{l}", k), RSTD2[:], ALU.mult, ALU.mult).then_inc(sems["dve_step"], t.one("dve_step"))
                        dve.wait_ge(sems["dve_step"], t.at("dve_step"))
                        split(QNH[:, k, :], QNL[:, k, :], TA[:])
                    rstd(S0, P, RSTD2)
                    dve.scalar_tensor_tensor(TA[:], LQ[:, 2, :], gain(f"mlakv{l}"), RSTD2[:], ALU.mult, ALU.mult).then_inc(sems["dve_step"], t.one("dve_step"))
                    dve.wait_ge(sems["dve_step"], t.at("dve_step"))
                    split(KNH[:, 0, :], KNL[:, 0, :], TA[:])
                    t.up("stage_loads", 128)
                    dve.wait_ge(sems["stage_loads"], t.at("stage_loads"))
                    if l == 0:
                        t.up("biased", 16 * BHEADS)
                        dve.wait_ge(sems["biased"], t.at("biased"))

                def attention(self, kind, l):
                    scale = float((HEAD + ROPE) ** -0.5) if kind == "mla" else float(HEAD ** -0.5)
                    branch = ("da", "mla", "sw").index(kind)

                    def u1(u):
                        i, m = UNITS[u]
                        _, n = key_blocks(kind, i)
                        w = n * P
                        t.up("s_ready")
                        dve.wait_ge(sems["s_ready"], t.at("s_ready"))
                        if kind == "da":
                            if m == 0:
                                t.up("turned")
                            dve.wait_ge(sems["turned"], t.at("turned", CREDITS["turned"] - 2))
                        else:
                            t.up("turned")
                            dve.wait_ge(sems["turned"], t.at("turned"))
                        if kind == "sw":
                            bias = BT[:, (m + 1) * 2 * P - w:(m + 1) * 2 * P]
                        else:
                            bias = (BT if kind == "da" else MASK)[:, SEQ - w:SEQ]
                        passed()
                        dve.tensor_tensor_reduce(SS[u % 4][:, 0:w], banks[S0 + m][:, 0:w], bias, 1.0, LOWEST, ALU.add, ALU.max, sm(MX + u)).then_inc(sems["dve_step"], t.one("dve_step"))
                        dve.wait_ge(sems["dve_step"], t.at("dve_step"))
                        if kind == "sw":
                            ins = dve.tensor_scalar(sm(NM + u), sm(MX + u), -1.0, sm(NST + m), ALU.mult, ALU.min)
                        else:
                            ins = dve.tensor_scalar(sm(NM + u), sm(MX + u), -1.0, None, ALU.mult)
                        ins.then_inc(sems["scored"], t.one("scored"))

                    def u2(u):
                        i, m = UNITS[u]
                        w = key_blocks(kind, i)[1] * P
                        t.up("exped")
                        dve.wait_ge(sems["exped"], t.at("exped"))
                        if kind == "sw":
                            dve.tensor_tensor(sm(DEN + u), sm(DEN + u), sm(ES + u), ALU.add).then_inc(sems["dve_step"], t.one("dve_step"))
                            dve.wait_ge(sems["dve_step"], t.at("dve_step"))
                        dve.reciprocal(sm(RC1 + u), sm(DEN + u)).then_inc(sems["dve_step"], t.one("dve_step"))
                        dve.wait_ge(sems["dve_step"], t.at("dve_step"))
                        S_ = SS[u % 4][:, 0:w]
                        if kind != "da":
                            dve.tensor_scalar(S_, S_, sm(RC1 + u), None, ALU.mult).then_inc(sems["probs"], t.one("probs"))
                        elif m == 1:
                            dve.tensor_scalar(S_, S_, sm(RC1 + u), sm(LAMC + l), ALU.mult, ALU.mult).then_inc(sems["dve_step"], t.one("dve_step"))
                            dve.wait_ge(sems["dve_step"], t.at("dve_step"))
                            F_ = SS[(u - 1) % 4][:, 0:w]
                            dve.scalar_tensor_tensor(F_, F_, sm(RC1 + u - 1), S_, ALU.mult, ALU.add).then_inc(sems["probs"], t.one("probs"))

                    def evict(dst, bank, s=None):
                        if s is None:
                            dve.tensor_tensor(dst, banks[bank][:], RSTD[:], ALU.mult).then_inc(sems["evicted"], t.one("evicted"))
                            dve.wait_ge(sems["evicted"], t.at("evicted", CREDITS["evicted"]))
                        else:
                            dve.scalar_tensor_tensor(dst, banks[bank][:], s, RSTD[:], ALU.mult, ALU.mult).then_inc(sems["evicted"], t.one("evicted"))
                            dve.wait_ge(sems["evicted"], t.at("evicted", CREDITS["evicted"]))

                    def body(it):
                        if kind != "mla":
                            src = (BDA if kind == "da" else BSW)[:, bass.ds(it, 1), :].rearrange("p o n -> p (o n)")
                            dve.tensor_scalar(BT[:], src, 1.0, None, ALU.mult).then_inc(sems["dve_step"], t.one("dve_step"))
                        if kind == "sw":
                            dve.tensor_scalar(sm(ST, 2), SM[:, bass.ds(SINK + 2 * it, 2)], 1.0, None, ALU.mult).then_inc(sems["dve_step"], t.one("dve_step"))
                            dve.tensor_scalar(sm(NST, 2), SM[:, bass.ds(SINK + 2 * it, 2)], -1.0, None, ALU.mult).then_inc(sems["dve_step"], t.one("dve_step"))
                        if kind == "da":
                            for j in range(4):
                                lo_part()
                                chunk()
                                if j == 0:
                                    evict(AQ[:], 0, scale)
                                elif j == 3:
                                    evict(TC[:], 3)
                                else:
                                    evict((None, AK, VF)[j][:], j)
                            signal("z_ready")
                        elif kind == "sw":
                            for j in range(2):
                                lo_part()
                                chunk()
                                evict((AQ, TC)[j][:], j, (scale, None)[j])
                            dve.sem_inc(sems["evicted"], 2)
                            t.up("evicted", 2)
                            signal("z_ready")
                        else:
                            lo_part()
                            chunk()
                            dve.tensor_scalar(AQ[:], banks[0][:], scale, None, ALU.mult).then_inc(sems["evicted"], t.one("evicted"))
                            dve.wait_ge(sems["evicted"], t.at("evicted", CREDITS["evicted"]))
                            dve.scalar_tensor_tensor(AR[:], banks[1][:], scale, COS[:], ALU.mult, ALU.mult).then_inc(sems["evicted"], t.one("evicted"))
                            dve.wait_ge(sems["evicted"], t.at("evicted", CREDITS["evicted"]))
                            dve.scalar_tensor_tensor(TA[:], banks[2][:], scale, SIN[:], ALU.mult, ALU.mult).then_inc(sems["evicted"], t.one("evicted"))
                            dve.wait_ge(sems["evicted"], t.at("evicted", CREDITS["evicted"]))
                            dve.tensor_tensor(AR[:], AR[:], TA[:], ALU.add).then_inc(sems["dve_step"], t.one("dve_step"))
                            dve.wait_ge(sems["dve_step"], t.at("dve_step"))
                            dve.tensor_copy(AK[:], banks[3][:]).then_inc(sems["evicted"], t.one("evicted"))
                            dve.wait_ge(sems["evicted"], t.at("evicted", CREDITS["evicted"]))
                            dve.tensor_copy(VF[:], banks[S0][:]).then_inc(sems["evicted"], t.one("evicted"))
                            dve.wait_ge(sems["evicted"], t.at("evicted", CREDITS["evicted"]))
                            lo_part()
                            chunk()
                            evict(TC[:], 0)
                            dve.sem_inc(sems["evicted"], 2)
                            t.up("evicted", 2)
                            signal("z_ready")
                        if kind == "da":
                            u1(0)
                            u1(1)
                            for i in range(QT):
                                if i + 1 < QT:
                                    u1(2 * i + 2)
                                    u1(2 * i + 3)
                                u2(2 * i)
                                u2(2 * i + 1)
                            t.up("pv_done", QT)
                            dve.wait_ge(sems["pv_done"], t.at("pv_done", CREDITS["pv_done"]))
                            t.up("gate")
                            dve.wait_ge(sems["gate"], t.at("gate"))
                            rstd(S0, P, RSTD2)
                            dve.scalar_tensor_tensor(TA[:], banks[OUTB][:], sm(SUBG + l), RSTD2[:], ALU.mult, ALU.mult).then_inc(sems["dve_step"], t.one("dve_step"))
                            dve.wait_ge(sems["dve_step"], t.at("dve_step"))
                            dve.tensor_tensor(TB[:], TA[:], TC[:], ALU.mult).then_inc(sems["dve_step"], t.one("dve_step"))
                            dve.wait_ge(sems["dve_step"], t.at("dve_step"))
                            t.up("turned", 0)
                        else:
                            u1(0)
                            for u in range(len(UNITS)):
                                if u + 1 < len(UNITS):
                                    u1(u + 1)
                                u2(u)
                            t.up("pv_done", len(UNITS))
                            dve.wait_ge(sems["pv_done"], t.at("pv_done", CREDITS["pv_done"]))
                            t.up("gate")
                            dve.wait_ge(sems["gate"], t.at("gate"))
                            dve.tensor_tensor(TB[:], banks[OUTB][:], TC[:], ALU.mult).then_inc(sems["dve_step"], t.one("dve_step"))
                            dve.wait_ge(sems["dve_step"], t.at("dve_step"))
                        z = bass.ds(it + 4 * branch, 1)
                        zh = ZH[:, z, :].rearrange("p o n -> p (o n)")
                        zl = ZL[:, z, :].rearrange("p o n -> p (o n)")
                        dve.tensor_copy(zh, TB[:]).then_inc(sems["dve_step"], t.one("dve_step"))
                        dve.wait_ge(sems["dve_step"], t.at("dve_step"))
                        dve.tensor_tensor(zl, TB[:], zh.bitcast(F32), ALU.subtract).then_inc(sems["o_used"], t.one("o_used"))
                        dve.wait_ge(sems["o_used"], t.at("o_used", CREDITS["o_used"]))
                    t.turns(4, body)

                def gates(self, l):
                    def body(it):
                        for j in range(6):
                            b, g, T_ = j % 3, 2 * (j % 2), (TA, TB)[j % 2]
                            lo_part()
                            chunk()
                            dve.tensor_tensor(T_[:], banks[g][:], RSTD[:], ALU.mult).then_inc(sems["gate_in"], t.one("gate_in"))
                            t.up("gate")
                            dve.wait_ge(sems["gate"], t.at("gate"))
                            if b == 0:
                                dve.tensor_tensor(TC[:], T_[:], banks[g + 1][:], ALU.mult).then_inc(sems["evicted"], t.one("evicted"))
                                dve.wait_ge(sems["evicted"], t.at("evicted", CREDITS["evicted"]))
                            else:
                                dve.tensor_tensor(T_[:], T_[:], banks[g + 1][:], ALU.mult).then_inc(sems["evicted"], t.one("evicted"))
                                dve.wait_ge(sems["evicted"], t.at("evicted", CREDITS["evicted"]))
                                dve.tensor_tensor(TC[:], TC[:], T_[:], ALU.add).then_inc(sems["dve_step"], t.one("dve_step"))
                                dve.wait_ge(sems["dve_step"], t.at("dve_step"))
                            if b == 2:
                                n = bass.ds(2 * it + j // 3, 1)
                                split(YH[:, n, :].rearrange("p o n -> p (o n)"), YL[:, n, :].rearrange("p o n -> p (o n)"), TC[:])
                    t.turns(4, body)

                def linear(self, parts, hi, lo, m):
                    def body(it):
                        for j in range(2):
                            for c in range(parts):
                                lo_part()
                                chunk()
                            n = bass.ds(2 * it + j, 1)
                            dve.tensor_copy(m[:, n, :].rearrange("p o n -> p (o n)"), banks[j][:]).then_inc(sems["evicted"], t.one("evicted"))
                    t.turns(4, body)

                def ple(self, l):
                    for k in range(KT):
                        dve.tensor_copy(HH[:, k, :], X[:, k, :]).then_inc(sems["dve_step"], t.one("dve_step"))
                        dve.wait_ge(sems["dve_step"], t.at("dve_step"))
                        dve.tensor_tensor(HL[:, k, :], X[:, k, :], HH[:, k, :].bitcast(F32), ALU.subtract).then_inc(sems["operand"], t.one("operand"))
                        dve.wait_ge(sems["operand"], t.at("operand"))
                    t.up("stage_loads", 16)
                    dve.wait_ge(sems["stage_loads"], t.at("stage_loads"))
                    for k in range(2):
                        dve.tensor_copy(PH[:, k, :], PX[:, k, :]).then_inc(sems["dve_step"], t.one("dve_step"))
                        dve.wait_ge(sems["dve_step"], t.at("dve_step"))
                        dve.tensor_tensor(PL[:, k, :], PX[:, k, :], PH[:, k, :].bitcast(F32), ALU.subtract).then_inc(sems["operand"], t.one("operand"))
                        dve.wait_ge(sems["operand"], t.at("operand"))

                    def body(it):
                        for j in range(2):
                            lo_part()
                            chunk()
                            t.up("gate")
                            dve.wait_ge(sems["gate"], t.at("gate"))
                            T_ = (TA, TB)[j]
                            dve.tensor_tensor(T_[:], T_[:], banks[2 * j + 1][:], ALU.mult).then_inc(sems["evicted"], t.one("evicted"))
                            dve.wait_ge(sems["evicted"], t.at("evicted", CREDITS["evicted"]))
                            xn = X[:, bass.ds(2 * it + j, 1), :].rearrange("p o n -> p (o n)")
                            dve.tensor_tensor(xn, xn, T_[:], ALU.add).then_inc(sems["dve_step"], t.one("dve_step"))
                            dve.wait_ge(sems["dve_step"], t.at("dve_step"))
                    t.turns(4, body)

                def ffn_up(self, l):
                    for n in range(2):
                        dve.memset(GE[n][:, 0:2], 0.0).then_inc(sems["dve_step"], t.one("dve_step"))
                        dve.wait_ge(sems["dve_step"], t.at("dve_step"))

                    def body(it):
                        for j in range(2):
                            def conv(c):
                                k = GAINS[f"conv{l}"] + c * FT + 2 * it + j
                                return G[:, bass.ds(k, 1)]
                            lo_part()
                            chunk()
                            dve.tensor_tensor(GE[j][:, 2:SEQ + 2], banks[2 * j][:], RSTD[:], ALU.mult).then_inc(sems["evicted"], t.one("evicted"))
                            dve.wait_ge(sems["evicted"], t.at("evicted", CREDITS["evicted"]))
                            dve.tensor_scalar(CO[j][:], GE[j][:, 0:SEQ], conv(0), conv(3), ALU.mult, ALU.add).then_inc(sems["dve_step"], t.one("dve_step"))
                            dve.wait_ge(sems["dve_step"], t.at("dve_step"))
                            dve.scalar_tensor_tensor(CO[j][:], GE[j][:, 1:SEQ + 1], conv(1), CO[j][:], ALU.mult, ALU.add).then_inc(sems["dve_step"], t.one("dve_step"))
                            dve.wait_ge(sems["dve_step"], t.at("dve_step"))
                            dve.scalar_tensor_tensor(CO[j][:], GE[j][:, 2:SEQ + 2], conv(2), CO[j][:], ALU.mult, ALU.add).then_inc(sems["gate_in"], t.one("gate_in"))
                            lo_part()
                            chunk()
                            dve.tensor_tensor(TA[:], banks[2 * j + 1][:], RSTD[:], ALU.mult).then_inc(sems["evicted"], t.one("evicted"))
                            dve.wait_ge(sems["evicted"], t.at("evicted", CREDITS["evicted"]))
                            t.up("gate")
                            dve.wait_ge(sems["gate"], t.at("gate"))
                            dve.tensor_tensor(TA[:], TA[:], GL[j][:], ALU.mult).then_inc(sems["dve_step"], t.one("dve_step"))
                            dve.wait_ge(sems["dve_step"], t.at("dve_step"))
                            n = bass.ds(2 * it + j, 1)
                            split(FHI[:, n, :].rearrange("p o n -> p (o n)"), FLO[:, n, :].rearrange("p o n -> p (o n)"), TA[:])
                    t.turns(FT // 2, body)

                def retention(self):
                    t.up("stage_loads", 48)
                    dve.wait_ge(sems["stage_loads"], t.at("stage_loads"))

                    def body(h):
                        for dst, b in ((RQ, 0), (RK, 2)):
                            for a in range(2):
                                lo_part()
                                chunk()
                                dve.tensor_tensor((TA, TB)[a][:], banks[b + a][:], RSTD[:], ALU.mult).then_inc(sems["evicted"], t.one("evicted"))
                                dve.wait_ge(sems["evicted"], t.at("evicted", CREDITS["evicted"]))
                            dve.tensor_tensor(dst[:, 0, :], TA[:], RC[:], ALU.mult).then_inc(sems["dve_step"], t.one("dve_step"))
                            dve.wait_ge(sems["dve_step"], t.at("dve_step"))
                            dve.tensor_tensor(TC[:], TB[:], RS[:], ALU.mult).then_inc(sems["dve_step"], t.one("dve_step"))
                            dve.wait_ge(sems["dve_step"], t.at("dve_step"))
                            dve.tensor_tensor(dst[:, 0, :], dst[:, 0, :], TC[:], ALU.subtract).then_inc(sems["rotated"], t.one("rotated"))
                            dve.wait_ge(sems["rotated"], t.at("rotated"))
                            dve.tensor_tensor(dst[:, 1, :], TB[:], RC[:], ALU.mult).then_inc(sems["dve_step"], t.one("dve_step"))
                            dve.wait_ge(sems["dve_step"], t.at("dve_step"))
                            dve.tensor_tensor(TC[:], TA[:], RS[:], ALU.mult).then_inc(sems["dve_step"], t.one("dve_step"))
                            dve.wait_ge(sems["dve_step"], t.at("dve_step"))
                            dve.tensor_tensor(dst[:, 1, :], dst[:, 1, :], TC[:], ALU.add).then_inc(sems["rotated"], t.one("rotated"))
                            dve.wait_ge(sems["rotated"], t.at("rotated"))
                        for j in range(4):
                            lo_part()
                            chunk()
                            t.up("v_turned")
                            if j:
                                dve.wait_ge(sems["v_turned"], t.at("v_turned", -1))
                            dve.tensor_tensor(RVF2[:], banks[j][:], RSTD[:], ALU.mult).then_inc(sems["evicted"], t.one("evicted"))
                        for kt in range(QT):
                            t.up("s_ready")
                            dve.wait_ge(sems["s_ready"], t.at("s_ready"))
                            n = SEQ - kt * P
                            dec = RD[:, bass.ds(h, 1), 0:n].rearrange("p o n -> p (o n)")
                            dve.tensor_tensor(RP[:, kt, kt * P:SEQ], banks[S0 + kt % 2][:, 0:n], dec, ALU.mult).then_inc(sems["operand"], t.one("operand"))
                        for j in range(4):
                            lo_part()
                        t.up("small", 5)
                        dve.wait_ge(sems["small"], t.at("small"))
                        dve.tensor_scalar(VAR[:], banks[S0][:], 1.0 / RET_V, None, ALU.mult).then_inc(sems["dve_step"], t.one("dve_step"))
                        dve.wait_ge(sems["dve_step"], t.at("dve_step"))
                        for e in range(4):
                            dve.tensor_tensor(RY[:, e, :], RY[:, e, :], VAR[:], ALU.subtract).then_inc(sems["centred"], t.one("centred"))
                            dve.wait_ge(sems["centred"], t.at("centred"))
                        rstd(S0 + 1, RET_V, RSTD2)
                        for e in range(4):
                            T_ = (TA, TB)[e % 2]
                            chunk()
                            dve.tensor_tensor(T_[:], banks[e][:], RSTD[:], ALU.mult).then_inc(sems["evicted"], t.one("evicted"))
                            dve.wait_ge(sems["evicted"], t.at("evicted", CREDITS["evicted"]))
                            signal("gate_in")
                            gn = G[:, bass.ds(GAINS["gn"] + 4 * h + e, 1)]
                            dve.scalar_tensor_tensor(TC[:], RY[:, e, :], gn, RSTD2[:], ALU.mult, ALU.mult).then_inc(sems["dve_step"], t.one("dve_step"))
                            dve.wait_ge(sems["dve_step"], t.at("dve_step"))
                            t.up("gate")
                            dve.wait_ge(sems["gate"], t.at("gate"))
                            dve.tensor_tensor(TC[:], TC[:], T_[:], ALU.mult).then_inc(sems["dve_step"], t.one("dve_step"))
                            dve.wait_ge(sems["dve_step"], t.at("dve_step"))
                            n = bass.ds(4 * h + e, 1)
                            split(RH[:, n, :].rearrange("p o n -> p (o n)"), RL[:, n, :].rearrange("p o n -> p (o n)"), TC[:])
                    t.turns(RET_HEADS, body)

                def dilated(self):
                    t.up("stage_loads", 96)
                    dve.wait_ge(sems["stage_loads"], t.at("stage_loads"))

                    def body(it):
                        for g in range(3):
                            lo_part()
                            chunk()
                            dve.scalar_tensor_tensor(TA[:], banks[0][:], float(HEAD ** -0.5), RSTD[:], ALU.mult, ALU.mult).then_inc(sems["evicted"], t.one("evicted"))
                            dve.wait_ge(sems["evicted"], t.at("evicted", CREDITS["evicted"]))
                            lo_part()
                            chunk()
                            dve.tensor_tensor(TB[:], banks[1][:], RSTD[:], ALU.mult).then_inc(sems["evicted"], t.one("evicted"))
                            dve.wait_ge(sems["evicted"], t.at("evicted", CREDITS["evicted"]))
                            dve.tensor_tensor(DF[:], banks[2][:], RSTD[:], ALU.mult).then_inc(sems["evicted"], t.one("evicted"))
                            dve.wait_ge(sems["evicted"], t.at("evicted", CREDITS["evicted"]))
                            for a, dst in enumerate((DQ, DK)):
                                T_ = (TA, TB)[a]
                                signal("operand")
                                dve.tensor_tensor(dst[:, g, :], T_[:], DC[:], ALU.mult).then_inc(sems["dve_step"], t.one("dve_step"))
                                dve.wait_ge(sems["dve_step"], t.at("dve_step"))
                                t.up("swapped")
                                dve.wait_ge(sems["swapped"], t.at("swapped"))
                                dve.tensor_tensor(TC[:], banks[3][:], DS[:], ALU.mult).then_inc(sems["dve_step"], t.one("dve_step"))
                                dve.wait_ge(sems["dve_step"], t.at("dve_step"))
                                dve.tensor_tensor(dst[:, g, :], dst[:, g, :], TC[:], ALU.add).then_inc(sems["rotated"], t.one("rotated"))
                                dve.wait_ge(sems["rotated"], t.at("rotated"))

                        def u1(u):
                            i, m = UNITS[u]
                            t.up("s_ready")
                            dve.wait_ge(sems["s_ready"], t.at("s_ready"))
                            if u >= 2:
                                t.up("turned", 3)
                                dve.wait_ge(sems["turned"], t.at("turned", CREDITS["turned"]))
                            at_ = 0
                            for g in range(3):
                                w = key_blocks("sw" if g == 0 else "da", i)[1] * P
                                full = 2 * P if g == 0 else SEQ
                                passed()
                                dve.tensor_tensor_reduce(DP[u % 2][:, at_:at_ + w], banks[DILS[u % 2][g]][:, 0:w],
                                        DM[g][:, full - w:full], 1.0, LOWEST, ALU.add, ALU.max, sm((MX, RC1, ES)[g] + u)).then_inc(sems["dve_step"], t.one("dve_step"))
                                dve.wait_ge(sems["dve_step"], t.at("dve_step"))
                                at_ += w
                            dve.tensor_tensor(sm(MX + u), sm(MX + u), sm(RC1 + u), ALU.max).then_inc(sems["dve_step"], t.one("dve_step"))
                            dve.wait_ge(sems["dve_step"], t.at("dve_step"))
                            dve.tensor_tensor(sm(MX + u), sm(MX + u), sm(ES + u), ALU.max).then_inc(sems["dve_step"], t.one("dve_step"))
                            dve.wait_ge(sems["dve_step"], t.at("dve_step"))
                            dve.tensor_scalar(sm(NM + u), sm(MX + u), -1.0, None, ALU.mult).then_inc(sems["scored"], t.one("scored"))

                        def u2(u):
                            w = dil_width(UNITS[u][0])
                            t.up("exped")
                            dve.wait_ge(sems["exped"], t.at("exped"))
                            dve.reciprocal(sm(RC1 + u), sm(DEN + u)).then_inc(sems["dve_step"], t.one("dve_step"))
                            dve.wait_ge(sems["dve_step"], t.at("dve_step"))
                            dve.tensor_scalar(DP[u % 2][:, 0:w], DP[u % 2][:, 0:w], sm(RC1 + u), None, ALU.mult).then_inc(sems["probs"], t.one("probs"))

                        u1(0)
                        for u in range(len(UNITS)):
                            if u + 1 < len(UNITS):
                                u1(u + 1)
                            u2(u)
                        t.up("turned", 6)
                        t.up("pv_done", len(UNITS))
                        dve.wait_ge(sems["pv_done"], t.at("pv_done", CREDITS["pv_done"]))
                        z = bass.ds(it, 1)
                        zh = DH[:, z, :].rearrange("p o n -> p (o n)")
                        zl = DL[:, z, :].rearrange("p o n -> p (o n)")
                        dve.tensor_copy(zh, banks[OUTB][:]).then_inc(sems["dve_step"], t.one("dve_step"))
                        dve.wait_ge(sems["dve_step"], t.at("dve_step"))
                        dve.tensor_tensor(zl, banks[OUTB][:], zh.bitcast(F32), ALU.subtract).then_inc(sems["o_used"], t.one("o_used"))
                        dve.wait_ge(sems["o_used"], t.at("o_used", CREDITS["o_used"]))
                    t.turns(8, body)

            e = Programs()
            e.t = t
            run(e)


def tiles(w, columns):
    columns = np.asarray(columns)
    part = w[:, np.maximum(columns, 0)]
    if (columns < 0).any():
        part = part.copy()
        part[:, columns < 0] = 0
    return part.reshape(-1, P, P).transpose(1, 0, 2)


def plain(w, at=0, n=None):
    n = (w.shape[1] - at) // P if n is None else n
    return [tiles(w, np.arange(at + j * P, at + (j + 1) * P)) for j in range(n)]


def chunks(parts, width):
    a = np.concatenate(parts, 1)
    return np.ascontiguousarray(a.reshape(P, -1, width * P).transpose(1, 0, 2))


def interleave(*lists):
    return [x for group in zip(*lists) for x in group]


def per_partition(v):
    return v.reshape(-1, P).T


def lay_out(a):
    names, w = {}, {}
    in_sizes = (512, 512, 512, 512, 256, 128, ROPE, 512, 512, 128, 128, 512, 3072)
    o = dict(zip(("aq", "ak", "av", "az", "bq", "bkv", "bkr", "bz", "cq", "ck", "cv", "cz", "g"),
                 np.cumsum((0,) + in_sizes[:-1])))
    sw_cols = [np.concatenate([np.arange(HEAD) + HEAD * h for h in (n, 4 + n)]) for n in range(4)]
    rope, swap, gap = np.arange(ROPE), np.roll(np.arange(ROPE), HALF), np.full(ROPE, -1)
    for l in range(DEPTH):
        wi = a["w_in"][l]
        kr = [tiles(wi, np.concatenate([o["bkr"] + r, gap, o["bkr"] + r, gap])) for r in (rope, swap)]
        w[f"lat{l}"] = chunks(plain(wi, o["bq"], 3) + kr + plain(wi, o["ck"], 2), 8)
        w[f"da{l}"] = chunks(interleave(*(plain(wi, o[n], 4) for n in ("aq", "ak", "av", "az"))), 8)
        parts = []
        qb, kvb = a["mla_w_qb"][l], a["mla_w_kvb"][l]
        bz = plain(wi, o["bz"], 4)
        for n in range(4):
            h = (2 * n, 2 * n + 1)
            parts += [tiles(qb, np.concatenate([96 * x + np.arange(HEAD) for x in h])),
                      tiles(qb, np.concatenate([y for x in h for y in (96 * x + HEAD + rope, gap)])),
                      tiles(qb, np.concatenate([y for x in h for y in (96 * x + HEAD + swap, gap)])),
                      tiles(kvb, np.concatenate([P * x + np.arange(HEAD) for x in h])),
                      tiles(kvb, np.concatenate([P * x + HEAD + np.arange(HEAD) for x in h])), bz[n]]
        w[f"mla{l}"] = chunks(parts, 8)
        w[f"sw{l}"] = chunks([tiles(wi, o[s] + c) for c in sw_cols for s in ("cq", "cz")], 8)
        g = [plain(wi, o["g"] + D * b, KT) for b in range(3)]
        rows = np.concatenate(sw_cols)
        br = [plain(x, 0, KT) for x in (a["w_br_a"][l], a["w_br_b"][l], a["w_br_c"][l][rows])]
        w[f"gate{l}"] = chunks(interleave(g[0], br[0], g[1], br[1], g[2], br[2]), 12)
        w[f"wout{l}"] = chunks(plain(a["w_out"][l]), 8)
        w[f"ple{l}"] = chunks(interleave(plain(a["w_ple_gate"][l]), plain(a["w_ple_proj"][l])), 10)
    ri = a["ret_w_in_2"][0]
    parts = []
    for h in range(RET_HEADS):
        parts += plain(ri, 256 * h, 2) + plain(ri, D + 256 * h, 2) + plain(ri, 2 * D + RET_V * h, 4)
        parts += plain(ri, 4 * D + RET_V * h, 4)
    w["ret"] = chunks(parts, 8)
    w["retout"] = chunks(plain(a["ret_w_out_2"][0]), 8)
    kv, q = a["att_w_kv_2"], a["att_w_q_2"][0]
    parts = []
    for n in range(KT):
        for g in range(3):
            parts += plain(q, D * g + P * n, 1) + plain(kv, D * g + P * n, 1) + plain(kv, 3 * D + D * g + P * n, 1)
    w["dil"] = chunks(parts, 12)
    w["wo"] = chunks(plain(a["att_w_o_2"][0]), 8)
    for l in range(DEPTH):
        up = a["ffn_w_up_2"][l]
        w[f"up{l}"] = chunks(interleave(plain(up, 0, FT), plain(up, DFF, FT)), 8)
        w[f"down{l}"] = chunks(plain(a["ffn_w_down_2"][l]), FH)
    for n, k, width in STREAM:
        assert w[n].shape == (k, P, width * P), (n, w[n].shape)
        names["w_" + n] = w[n]
    gains = []
    for n in GAINS:
        stem, l = n.rstrip("01"), int(n[-1]) if n[-1] in "01" else 0
        if stem == "conv":
            gains += [per_partition(a["ffn_conv_w_2"][l, c]) for c in range(3)] + [per_partition(a["ffn_conv_b_2"][l])]
        else:
            src = {"pre": "norm_pre", "post": "norm_post", "mixpre": "norm_mix_pre_2", "mixpost": "norm_mix_post_2",
                   "ffnpre": "norm_ffn_pre_2", "ffnpost": "norm_ffn_post_2", "kv": "kv_norm_2", "mlaq": "mla_q_norm",
                   "mlakv": "mla_kv_norm", "subln": "da_subln", "gn": "ret_gn_gain_2"}[stem]
            gains.append(per_partition(a[src] if stem == "kv" else a[src][l]))
    names["gains"] = np.ascontiguousarray(np.concatenate(gains, 1))
    names["x_t"] = np.ascontiguousarray(a["x"][0].T.reshape(KT, P, SEQ).transpose(1, 0, 2))
    names["p_t"] = np.ascontiguousarray(a["p"][:, 0].transpose(0, 2, 1).reshape(DEPTH, 2, P, SEQ).transpose(0, 2, 1, 3))
    names["positions"] = np.ascontiguousarray(a["positions"])
    names["rel_bias"] = np.ascontiguousarray(a["rel_bias"])
    names["da_lambda"] = np.ascontiguousarray(a["da_lambda"].reshape(1, -1))
    names["sw_sinks"] = np.ascontiguousarray(a["sw_sinks"])
    names.update(constants())
    return names


def kernel(**inputs):
    import concourse.bacc as _bacc
    from concourse.bass_utils import run_bass_kernel_spmd as _run

    nc = _bacc.Bacc("TRN2", target_bir_lowering=False, num_devices=1)
    arrays, aps = {}, {}
    for name, value in lay_out({k: np.asarray(v) for k, v in inputs.items()}).items():
        arrays[f"in_{name}"] = value
        aps[name] = nc.dram_tensor(f"in_{name}", value.shape, mybir.dt.from_np(value.dtype), kind="ExternalInput").ap()
    out = nc.dram_tensor("out_x", (P, KT, SEQ), F32, kind="ExternalOutput").ap()
    two_stacks_kernel(nc, aps, out)
    r = _run(nc, [arrays], core_ids=[0])
    got = r.results[0]["out_x"]
    return np.ascontiguousarray(got.transpose(1, 0, 2).reshape(1, D, SEQ).transpose(0, 2, 1))
```

```python
import math
from contextlib import ExitStack, contextmanager

import numpy as np

import concourse.bass as bass
from concourse import mybir

F32 = mybir.dt.float32
F32R = mybir.dt.float32r
I32 = mybir.dt.int32
ALU = mybir.AluOpType
ACT = mybir.ActivationFunctionType

P = 128
SEQ = 512
QT = SEQ // P
D = 1024
KT = D // P
DEPTH = 2
HEAD = 64
ROPE = 32
HALF = ROPE // 2
DFF = 2816
FT = DFF // P
FH = FT // 2
RET_HEADS = 4
RET_V = 512
EPS = 1e-6
NEG = -1e30
LOWEST = -3.0e38
RING = 2
SLOT = 12
LBANKS = 4
S0, TURN, OUTB = 4, 6, 7
BUCKETS, BHEADS = 32, 12
RV = 640
TWO_PI_A = 6.28125
TWO_PI_B = float(np.float32(2 * math.pi - 6.28125))
TWO_PI_C = float(np.float32(2 * math.pi - 6.28125 - TWO_PI_B))
MAGIC = 12582912.0
LAM_INIT = [0.8 - 0.6 * math.exp(-0.3 * l) for l in range(DEPTH)]

GAINS = {}
_at = 0
for _name, _n in (("pre0", KT), ("pre1", KT), ("post0", KT), ("post1", KT), ("mixpre0", KT), ("mixpre1", KT),
                  ("mixpost0", KT), ("mixpost1", KT), ("ffnpre0", KT), ("ffnpre1", KT), ("ffnpost0", KT),
                  ("ffnpost1", KT), ("kv", KT), ("mlaq0", 2), ("mlaq1", 2), ("mlakv0", 1), ("mlakv1", 1),
                  ("subln0", 1), ("subln1", 1), ("gn", 16), ("conv0", 4 * FT), ("conv1", 4 * FT)):
    GAINS[_name] = _at
    _at += _n
NGAIN = _at

STREAM = []
for _l in range(DEPTH):
    STREAM += [(f"lat{_l}", 7, 8), (f"da{_l}", 16, 8), (f"mla{_l}", 8, 8), (f"sw{_l}", 8, 8),
               (f"gate{_l}", 24, 12), (f"wout{_l}", 8, 8), (f"ple{_l}", 8, 10)]
STREAM += [("ret", 48, 8), ("retout", 16, 8), ("up0", 44, 8), ("down0", 16, FH),
           ("dil", 72, 8), ("wo", 8, 8), ("up1", 44, 8), ("down1", 16, FH)]
WIDTH = [w for _, n, w in STREAM for _ in range(n)]

SEMAPHORES = (
    "loaded", "scratch", "spread", "biased", "raw0", "raw1",
    "hi_done", "lo_done", "chunk_done",
    "dve_step", "act_step",
    "evicted", "part_done",
    "squared", "summed", "var_ready", "std_ready",
    "operand",
    "operand_hi",
    "s_ready", "scored", "exped", "probs", "turned", "pt_copied", "pv_done", "o_used", "sum_used",
    "v_turned", "v_token", "z_ready", "gate_in", "gate", "swapped", "rotated", "y_copied", "centred",
    "small",
    "stage_pe", "stage_act", "stage_dve",
    "stage_loads", "stored", "waits_passed",
)
CREDITS = {"chunk_done": RING, "lo_done": RING, "evicted": LBANKS, "scored": 2, "turned": 4,
           "pt_copied": 1, "pv_done": 2, "o_used": 1, "sum_used": 1}
ALIASES = {"slot_free": "chunk_done", "raw_free": "lo_done"}


STAGES = ["setup"]
for _l in range(DEPTH):
    STAGES += [f"{_s}{_l}" for _s in ("pre", "lat", "da", "mla", "sw", "gate", "wout", "post", "ple")]
STAGES += ["pre_ret", "ret", "retout", "post_ret", "preffn0", "up0", "down0", "postffn0",
           "pre_dil", "dil", "wo", "post_dil", "preffn1", "up1", "down1", "postffn1"]
N_STAGES = len(STAGES)
STAGE = {n: i for i, n in enumerate(STAGES)}


class Tally:

    def __init__(self, eng):
        self.eng = eng
        self.base, self.k = {}, {}
        self.c = 0

    def up(self, name, n=1):
        self.k[name] = self.k.get(name, 0) + n

    def add(self, name, n):
        self.up(name, n)
        return n

    def one(self, name):
        return self.add(name, 1)

    def at(self, name, plus=0):
        value = self.base.get(name, 0) + self.k.get(name, 0) + plus
        assert not isinstance(value, int) or value > 0, (name, value)
        return value

    def turns(self, n, body):
        before, c0 = dict(self.k), self.c
        body(0)
        per = {s: v - before.get(s, 0) for s, v in self.k.items()}
        per_c = self.c - c0
        assert n == 1 or per_c % RING == 0
        if n > 2:
            outer = dict(self.base)
            for s in per:
                self.k[s] = 0
            with self.eng.Fori(1, n - 1) as i:
                for s, v in per.items():
                    self.base[s] = outer.get(s, 0) + before.get(s, 0) + i * v if v else outer.get(s, 0) + before.get(s, 0)
                body(i)
            for s, v in per.items():
                assert self.k[s] == v, (s, self.k[s], v)
                self.base[s] = outer.get(s, 0)
                self.k[s] = before.get(s, 0) + (n - 1) * v
            self.c = c0 + (n - 1) * per_c
        if n > 1:
            body(n - 1)


def rel_window(n):
    return n - 1 - np.arange(RV)


def constants():
    f = np.float32
    c = {}
    rel = rel_window(SEQ)
    n = np.maximum(rel, 0)
    large = 16 + (np.log(np.maximum(n, 1).astype(f) / f(16)) / f(math.log(8.0)) * f(16)).astype(np.int32)
    bucket = np.where(n < 16, n, np.minimum(large, BUCKETS - 1))
    for name, valid in (("oh_full", rel >= 0), ("oh_window", (rel >= 0) & (rel < 128))):
        oh = np.zeros((BUCKETS + 1, RV), f)
        oh[bucket[valid], np.nonzero(valid)[0]] = 1.0
        oh[BUCKETS, ~valid] = NEG
        c[name] = oh
    q, k = np.arange(P)[:, None], np.arange(SEQ)[None, :]
    rel = SEQ - P + q - k
    c["masks"] = np.stack([np.where(ok, f(0), f(NEG)) for ok in (
        rel >= 0, (rel >= 0) & (rel <= 128), (rel >= 0) & (rel % 4 == 0), (rel >= 0) & (rel % 16 == 0))], 1)
    p = np.arange(P)
    inv = (10000.0 ** (-np.arange(HALF, dtype=np.float64) / HALF)).astype(f)
    sign = np.where(p % ROPE < HALF, -1.0, 1.0)
    c["columns"] = np.stack([inv[p % HALF], sign], 1).astype(f)
    c["ident"] = np.eye(P, dtype=f)
    pos = np.arange(SEQ, dtype=f)[None, :]
    ret = (1.0 / (10000.0 ** np.linspace(0.0, 1.0, P, dtype=np.float64))).astype(f)
    ang = (pos * ret[:, None]).astype(np.float64)
    c["ret_angles"] = np.stack([np.cos(ang), np.sin(ang)], 1).astype(f)
    gamma = 1.0 - 2.0 ** (-5.0 - np.arange(RET_HEADS))
    diff = np.arange(SEQ)[None, :] - p[:, None]
    c["decay"] = np.stack([np.where(diff >= 0, g ** np.maximum(diff, 0), 0.0) / 16.0 for g in gamma]).astype(f)
    inv2 = (500000.0 ** (-np.arange(0, 16, 2, dtype=np.float64) / 16)).astype(f)
    r = p % HEAD
    ang = (pos * inv2[r % 8][:, None]).astype(np.float64)
    rot = (r < 16)[:, None]
    c["dil_angles"] = np.stack([np.where(rot, np.cos(ang), 1.0),
                                np.where(rot, np.sin(ang) * np.where(r < 8, -1.0, 1.0)[:, None], 0.0)], 1).astype(f)
    perm = np.zeros((P, P), f)
    for m in range(P):
        if m % HEAD < 16:
            perm[m + 8 if m % HEAD < 8 else m - 8, m] = 1.0
    c["perm"] = perm
    return {k: np.ascontiguousarray(v.astype(f)) for k, v in c.items()}


CONSTANTS = ("oh_full", "oh_window", "masks", "columns", "ident", "ret_angles", "decay", "dil_angles", "perm")


def two_stacks_kernel(nc, d, out):
    scratch = nc.dram_tensor("bias_vectors", (2, BHEADS, RV), F32, kind="Internal").ap()
    copies = nc.dram_tensor("bias_copies", (BHEADS, P, RV), F32, kind="Internal").ap()
    with ExitStack() as ctx:
        sems = {n: ctx.enter_context(nc.semaphore(n)) for n in SEMAPHORES}
        sems |= {a: sems[n] for a, n in ALIASES.items()}

        def sb(name, shape, dt=F32):
            return ctx.enter_context(nc.sbuf_tensor(name, shape, dt))

        X = sb("x_res", [P, KT, SEQ])
        HH = sb("h_hi", [P, KT, SEQ], F32R)
        HL = sb("h_lo", [P, KT, SEQ], F32R)
        RAW = [sb(f"w_raw{s}", [P, SLOT * P]) for s in range(RING)]
        WH = [sb(f"w_hi{s}", [P, SLOT * P], F32R) for s in range(RING)]
        WL = [sb(f"w_lo{s}", [P, SLOT * P], F32R) for s in range(RING)]
        G = sb("gains", [P, NGAIN])
        COLS = sb("columns", [P, 2])
        ID = sb("ident", [P, P])
        ONES = sb("ones", [P, P])
        RSTD = sb("rstd", [P, SEQ])
        RSTD2 = sb("rstd2", [P, SEQ])
        VAR = sb("var", [P, SEQ])
        TA = sb("ta", [P, SEQ])
        TB = sb("tb", [P, SEQ])
        TC = sb("tc", [P, SEQ])
        SM = sb("small_columns", [P, 64])
        arena_bytes = 54 * SEQ * 4
        base = -(-nc.sbuf_base // 32) * 32
        sb("arena", [P, arena_bytes // 4])

        def at(name, shape, offset, dt=F32):
            size = int(np.prod(shape[1:])) * 4
            assert offset + size <= arena_bytes, (name, offset + size, arena_bytes)
            return nc.alloc_sbuf_tensor_at(name, shape, dt, offset=base + offset)

        T1 = SEQ * 4
        ZH = at("zo_hi", [P, 12, SEQ], 0, F32R)
        ZL = at("zo_lo", [P, 12, SEQ], 12 * T1, F32R)
        M1 = at("m1", [P, KT, SEQ], 0)
        SQ1 = at("sq1", [P, KT, SEQ], KT * T1)
        o = 24 * T1
        YH = at("y_hi", [P, KT, SEQ], o, F32R)
        YL = at("y_lo", [P, KT, SEQ], o + KT * T1, F32R)
        PX = at("ple_raw", [P, 2, SEQ], o)
        PH = at("ple_hi", [P, 2, SEQ], o + 2 * T1, F32R)
        PL = at("ple_lo", [P, 2, SEQ], o + 4 * T1, F32R)
        QNH = at("qn_hi", [P, 2, SEQ], o, F32R)
        QNL = at("qn_lo", [P, 2, SEQ], o + 2 * T1, F32R)
        KNH = at("kvn_hi", [P, 1, SEQ], o + 4 * T1, F32R)
        KNL = at("kvn_lo", [P, 1, SEQ], o + 5 * T1, F32R)
        KR = at("k_rope", [P, SEQ], o + 6 * T1)
        CK = at("c_k", [P, SEQ], o + 7 * T1)
        CV = at("c_v", [P, QT, P], o + 8 * T1)
        LQ = at("lat_q", [P, 3, SEQ], o + 9 * T1)
        AQ = at("att_q", [P, SEQ], o + 9 * T1)
        AK = at("att_k", [P, SEQ], o + 10 * T1)
        AR = at("att_qr", [P, SEQ], o + 11 * T1)
        BT = AR
        NZ = VAR
        VF = RSTD2
        VT = at("att_vt", [P, QT, P], o + 12 * T1)
        SS = [at(f"probs{n}", [P, SEQ], o + (13 + n) * T1) for n in range(4)]
        PT = [at(f"pt{n}", [P, SEQ], o + (17 + n) * T1) for n in range(2)]
        COS = at("cos", [P, SEQ], o + 19 * T1)
        SIN = at("sin", [P, SEQ], o + 20 * T1)
        MASK = at("mask", [P, SEQ], o + 21 * T1)
        BDA = at("bias_da", [P, 4, SEQ], o + 22 * T1)
        BSW = at("bias_sw", [P, 4, SEQ], o + 26 * T1)
        POSI = at("pos_i", [P, SEQ], 0, I32)
        ANG = at("ang", [P, SEQ], T1)
        OHF = at("oh_full_sb", [BUCKETS + 1, RV], 2 * T1)
        OHW = at("oh_window_sb", [BUCKETS + 1, RV], 4 * T1)
        TAB = at("table", [BUCKETS + 1, BHEADS], 6 * T1)
        RVF = at("rv_full", [BHEADS, RV], 7 * T1)
        RVW = at("rv_window", [BHEADS, RV], 9 * T1)
        LAM = at("lam_in", [P, DEPTH, 4, HEAD], 11 * T1)
        RH = at("ret_hi", [P, 16, SEQ], 0, F32R)
        RL = at("ret_lo", [P, 16, SEQ], 16 * T1, F32R)
        RQ = at("ret_q", [P, 2, SEQ], 32 * T1)
        RK = at("ret_k", [P, 2, SEQ], 34 * T1)
        RY = at("ret_y", [P, QT, SEQ], 32 * T1)
        RVT = at("ret_vt", [P, QT, RET_V], 36 * T1)
        RSQ = at("ret_sq", [P, QT, SEQ], 36 * T1)
        RP = at("ret_p", [P, QT, SEQ], 40 * T1)
        RVF2 = at("ret_vf", [P, SEQ], 44 * T1)
        RC = at("ret_cos", [P, SEQ], 45 * T1)
        RS = at("ret_sin", [P, SEQ], 46 * T1)
        RD = at("ret_decay", [P, RET_HEADS, SEQ], 47 * T1)
        FHI = at("f_hi", [P, FT, SEQ], 0, F32R)
        FLO = at("f_lo", [P, FT, SEQ], FT * T1, F32R)
        M2 = at("m2", [P, KT, SEQ], 2 * FT * T1)
        SQ2 = at("sq2", [P, KT, SEQ], 0)
        GE = [at(f"conv_in{n}", [P, SEQ + 2], (2 * FT + 2 * n) * T1) for n in range(2)]
        CO = [at(f"conv_out{n}", [P, SEQ], (2 * FT + 4 + n) * T1) for n in range(2)]
        GL = [at(f"gelu{n}", [P, SEQ], (2 * FT + 6 + n) * T1) for n in range(2)]
        DO = at("dil_out", [P, KT, SEQ], 0)
        H2H = at("h2_hi", [P, KT, SEQ], 8 * T1, F32R)
        H2L = at("h2_lo", [P, KT, SEQ], 16 * T1, F32R)
        DQ = [at(f"dil_q{n}", [P, 3, SEQ], (24 + 9 * n) * T1) for n in range(2)]
        DK = [at(f"dil_k{n}", [P, 3, SEQ], (27 + 9 * n) * T1) for n in range(2)]
        DVT = [at(f"dil_vt{n}", [P, 3, QT, P], (30 + 9 * n) * T1) for n in range(2)]
        DP = [at(f"dil_p{n}", [P, 10 * P], 42 * T1 + n * 5 * P * 8) for n in range(2)]
        DPT = [at(f"dil_pt{n}", [P, SEQ], 47 * T1 + n * T1) for n in range(2)] + [VAR]
        DC = at("dil_cos", [P, SEQ], 49 * T1)
        DS = at("dil_sin", [P, SEQ], 50 * T1)
        DM = [at("dil_mask0", [P, 2 * P], 51 * T1), at("dil_mask1", [P, SEQ], 52 * T1),
              at("dil_mask2", [P, SEQ], 53 * T1)]
        PERM = at("perm_sb", [P, P], 51 * T1 + T1 // 2)
        DF = RSTD2

        MX, NM, DEN, ES, RC1, SINK, ST, NST, LAMC, SUBG = 0, 8, 16, 24, 32, 40, 48, 50, 56, 58

        def sm(c, n=1):
            return SM[:, c:c + n]

        def gain(name, k=0):
            c = GAINS[name] + k
            return G[:, c:c + 1]

        banks = [ctx.enter_context(nc.psum_tensor(f"bank{b}", [P, SEQ], F32)) for b in range(8)]
        block = ctx.enter_context(nc.Block())

        @block.sync
        def _(sp):
            t = Tally(sp)
            for dst, src in ((X[:], d["x_t"]), (G[:], d["gains"]), (COLS[:], d["columns"]), (ID[:], d["ident"]),
                             (POSI[:], d["positions"].to_broadcast([P, SEQ])), (OHF[:], d["oh_full"]),
                             (OHW[:], d["oh_window"]), (TAB[0:BUCKETS, :], d["rel_bias"]),
                             (LAM[:].rearrange("p a b c -> p (a b c)"),
                              d["da_lambda"].to_broadcast([P, DEPTH * 4 * HEAD])),
                             (MASK[:], d["masks"][:, 0, :])):
                sp.dma_start(dst, src).then_inc(sems["loaded"], t.add("loaded", 16))

            def load(w, width, i):
                slot = t.c % RING
                t.up("raw_free")
                sp.wait_ge(sems["raw_free"], t.at("raw_free"))
                src = w[i] if isinstance(i, int) else w[bass.ds(i, 1), :, :].rearrange("o p n -> p (o n)")
                sp.dma_start(RAW[slot][:, 0:width * P], src).then_inc(sems[f"raw{slot}"], t.add(f"raw{slot}", 16))
                t.c += 1

            for name, n, width in STREAM:
                w = d["w_" + name]

                def pair(i):
                    load(w, width, 2 * i)
                    load(w, width, 2 * i + 1)
                t.turns(n // 2, pair)
                if n % 2:
                    load(w, width, n - 1)
            t.up("stage_dve", N_STAGES)
            sp.wait_ge(sems["stage_dve"], t.at("stage_dve"))
            sp.dma_start(out, X[:]).then_inc(sems["stored"], t.add("stored", 16))
            sp.wait_ge(sems["stored"], t.at("stored"))

        @block.gpsimd
        def _(pool):
            t = Tally(pool)

            def after(stage):
                pool.wait_ge(sems["stage_pe"], stage)
                pool.wait_ge(sems["stage_act"], stage)
                pool.wait_ge(sems["stage_dve"], stage)

            def fetch(dst, src):
                pool.dma_start(dst, src).then_inc(sems["stage_loads"], t.add("stage_loads", 16))

            t.up("scratch", 32)
            pool.wait_ge(sems["scratch"], t.at("scratch"))
            for h in range(BHEADS):
                pool.dma_start(copies[h], scratch[0 if h < 4 else 1, h:h + 1, :].to_broadcast([P, RV])).then_inc(sems["spread"], t.add("spread", 16))
            pool.wait_ge(sems["spread"], t.at("spread"))

            def window(h, start, n):
                return bass.AP(copies.tensor, h * P * RV + start, [[RV - 1, P], [1, n]])

            for h in range(4):
                pool.dma_start(BDA[:, h, :], window(h, P - 1, SEQ)).then_inc(sems["biased"], t.add("biased", 16))
            for h in range(8):
                pool.dma_start(BSW[:, h % 4, h // 4 * 2 * P:(h // 4 + 1) * 2 * P],
                        window(4 + h, SEQ // 2 + P - 1, 2 * P)).then_inc(sems["biased"], t.add("biased", 16))
            for l in range(DEPTH):
                after(STAGE[f"lat{l}"])
                for h in range(8):
                    fetch(sm(SINK + 2 * (h % 4) + h // 4), d["sw_sinks"][l:l + 1, h:h + 1].to_broadcast([P, 1]))
                after(STAGE[f"ple{l}"])
                fetch(PX[:], d["p_t"][l])
            after(STAGE["ret"])
            fetch(RC[:], d["ret_angles"][:, 0, :])
            fetch(RS[:], d["ret_angles"][:, 1, :])
            fetch(RD[:], d["decay"].rearrange("h p n -> p h n"))
            after(STAGE["dil"])
            fetch(DC[:], d["dil_angles"][:, 0, :])
            fetch(DS[:], d["dil_angles"][:, 1, :])
            fetch(DM[0][:], d["masks"][:, 1, SEQ - 2 * P:SEQ])
            fetch(DM[1][:], d["masks"][:, 2, :])
            fetch(DM[2][:], d["masks"][:, 3, :])
            fetch(PERM[:], d["perm"])

        def run(e):
            def stage(name, f, *args):
                assert STAGES[e.stage] == name
                e.stage += 1
                if e.stage > 1:
                    e.begin_stage()
                f(*args)
                e.end()
                for s in ("stage_pe", "stage_act", "stage_dve"):
                    if s != e.mine:
                        e.t.up(s)

            stage("setup", e.setup)
            for l in range(DEPTH):
                stage(f"pre{l}", e.prenorm, [(HH, HL, f"pre{l}")], SQ1)
                stage(f"lat{l}", e.latents, l)
                stage(f"da{l}", e.attention, "da", l)
                stage(f"mla{l}", e.attention, "mla", l)
                stage(f"sw{l}", e.attention, "sw", l)
                stage(f"gate{l}", e.gates, l)
                stage(f"wout{l}", e.linear, 1, YH, YL, M1)
                stage(f"post{l}", e.postnorm, M1, SQ1, f"post{l}")
                stage(f"ple{l}", e.ple, l)
            stage("pre_ret", e.prenorm, [(HH, HL, "mixpre0")], SQ1)
            stage("ret", e.retention)
            stage("retout", e.linear, 2, RH, RL, M2)
            stage("post_ret", e.postnorm, M2, SQ2, "mixpost0")
            for l in range(DEPTH):
                if l == 1:
                    stage("pre_dil", e.prenorm, [(HH, HL, "kv"), (H2H, H2L, "mixpre1")], SQ2)
                    stage("dil", e.dilated)
                    stage("wo", e.linear, 1, H2H, H2L, M2, DO)
                    stage("post_dil", e.postnorm, M2, SQ2, "mixpost1")
                stage(f"preffn{l}", e.prenorm, [(HH, HL, f"ffnpre{l}")], SQ2)
                stage(f"up{l}", e.ffn_up, l)
                stage(f"down{l}", e.linear, 2, FHI, FLO, M2)
                stage(f"postffn{l}", e.postnorm, M2, SQ2, f"ffnpost{l}")

        def key_blocks(kind, i):
            n = min(i + 1, 2) if kind == "sw" else i + 1
            return i + 1 - n, n

        DAUX, DSCORES = 2, (3, 4, 5)

        def dil_bank(par, x):
            return (par + x) % 2

        def dil_width(i):
            return (key_blocks("sw", i)[1] + 2 * (i + 1)) * P

        UNITS = [(i, m) for i in range(QT) for m in range(2)]

        MLA_TILES = ((1, 0, 1, 2), (2, 0, 2, 3), (2, 1, 2, 3), (3, 0, 2, 4), (3, 1, 2, 4), (0, 0, 2, 4), (0, 1, 2, 4),
                     (1, 0, 1, 4))

        @block.tensor
        def _(pe):
            t = Tally(pe)

            class Programs:
                mine, stage = "stage_pe", 0

                def begin_stage(self):
                    pe.wait_ge(sems["stage_pe"], t.at("stage_pe"))
                    pe.wait_ge(sems["stage_act"], t.at("stage_act"))
                    pe.wait_ge(sems["stage_dve"], t.at("stage_dve"))

                def end(self):
                    pe.drain().then_inc(sems["stage_pe"], t.one("stage_pe"))

                def setup(self):
                    for n, c in (("chunk_done", RING), ("turned", 4), ("pv_done", 2)):
                        pe.sem_inc(sems[n], c)
                    t.up("loaded", 160)
                    pe.wait_ge(sems["loaded"], t.at("loaded"))
                    t.up("operand")
                    pe.wait_ge(sems["operand"], t.at("operand"))
                    for n, oh in enumerate((OHF, OHW)):
                        for h in range(2):
                            ins = pe.matmul(banks[2 * n + h][0:BHEADS, 0:RV // 2], TAB[:], oh[:, h * RV // 2:(h + 1) * RV // 2],
                                            start=True, stop=True)
                    ins.then_inc(sems["small"], t.one("small"))
                    t.up("operand", 2)

                def products(self, bank, tile, width, hi, lo, k, start, stop):
                    slot = t.c % RING
                    w = slice(tile * P, (tile + 1) * P)
                    pe.matmul(banks[bank][:], WH[slot][:, w], hi[:, k, :], start=start, stop=False)
                    pe.matmul(banks[bank][:], WH[slot][:, w], lo[:, k, :], start=False, stop=False)
                    return pe.matmul(banks[bank][:], WL[slot][:, w], hi[:, k, :], start=False, stop=stop)

                def begin(self):
                    t.up("lo_done")
                    pe.wait_ge(sems["lo_done"], t.at("lo_done", CREDITS["lo_done"]))

                def finish(self, ins):
                    ins.then_inc(sems["chunk_done"], t.one("chunk_done"))
                    t.c += 1

                def bank_free(self, of=LBANKS):
                    t.up("evicted")
                    pe.wait_ge(sems["evicted"], t.at("evicted", LBANKS - of))

                def whole(self, bank, hi=HH, lo=HL, of=LBANKS):
                    self.bank_free(of)
                    self.begin()
                    for k in range(KT):
                        ins = self.products(bank, k, 8, hi, lo, k, k == 0, k == KT - 1)
                    self.finish(ins)

                def some(self, bank, k, of):
                    if k == 0:
                        self.bank_free(of)
                        self.begin()
                    ins = self.products(bank, k, 8, HH, HL, k, k == 0, k == KT - 1)
                    if k == KT - 1:
                        self.finish(ins)

                def sums(self, bank, n, src, name="squared"):
                    for k in range(n):
                        t.up(name)
                        pe.wait_ge(sems[name], t.at(name))
                        ins = pe.matmul(banks[bank][:], ONES[:], src(k), start=(k == 0), stop=(k == n - 1))
                    ins.then_inc(sems["summed"], t.one("summed"))

                def prenorm(self, targets, sq):
                    self.sums(OUTB, KT, lambda k: sq[:, k, :])

                def postnorm(self, m, sq, g):
                    self.sums(OUTB, KT, lambda k: sq[:, k, :])

                def turn_v(self, src, bank=TURN):
                    for b in range(QT):
                        ins = pe.transpose(banks[bank][:, b * P:(b + 1) * P], src[:, b * P:(b + 1) * P], ID[:])
                    ins.then_inc(sems["v_turned"], t.one("v_turned"))

                def latents(self, l):
                    for j in range(7):
                        self.whole(j % LBANKS)
                    pe.wait_ge(sems["evicted"], t.at("evicted", LBANKS))
                    self.turn_v(VF)
                    t.up("v_token")
                    t.up("operand")
                    self.sums(OUTB, 2, lambda k: SS[k][:])
                    self.sums(S0, 1, lambda k: SS[2][:])

                def attention(self, kind, l):
                    def s_unit(i, m):
                        kb, n = key_blocks(kind, i)
                        r = slice(64 * m, 64 * m + 64)
                        keys = CK if kind == "sw" else AK
                        t.up("scored")
                        pe.wait_ge(sems["scored"], t.at("scored"))
                        q = slice(i * P, (i + 1) * P)
                        kk = slice(kb * P, (kb + n) * P)
                        o_ = banks[S0 + m][:, 0:n * P]
                        ins = pe.matmul(o_, AQ[r, q], keys[r, kk], start=True, stop=(kind != "mla"))
                        if kind == "mla":
                            rr = slice(64 * m, 64 * m + ROPE)
                            ins = pe.matmul(o_, AR[rr, q], KR[rr, kk], start=False, stop=True)
                        ins.then_inc(sems["s_ready"], t.one("s_ready"))

                    def t_unit(u, i):
                        _, n = key_blocks(kind, i)
                        t.up("probs")
                        pe.wait_ge(sems["probs"], t.at("probs"))
                        t.up("pt_copied")
                        pe.wait_ge(sems["pt_copied"], t.at("pt_copied"))
                        for b in range(n):
                            ins = pe.transpose(banks[TURN][:, b * P:(b + 1) * P], SS[u % 4][:, b * P:(b + 1) * P], ID[:])
                        ins.then_inc(sems["turned"], t.one("turned"))

                    def pv_unit(n_unit, i, m):
                        kb, n = key_blocks(kind, i)
                        ahead = 1 if kind != "da" and n_unit < len(UNITS) - 1 else 0
                        pe.wait_ge(sems["pt_copied"], t.at("pt_copied", CREDITS["pt_copied"] - ahead))
                        for b in range(n):
                            v = (CV if kind == "sw" else VT)[:, kb + b, :]
                            if kind != "da":
                                v = v[:, 64 * m:64 * m + 64]
                            r = slice(0, P) if kind == "da" else slice(64 * m, 64 * m + 64)
                            ins = pe.matmul(banks[OUTB][r, i * P:(i + 1) * P], v, PT[n_unit % 2][:, b * P:(b + 1) * P],
                                            start=(b == 0), stop=(b == n - 1))
                        ins.then_inc(sems["pv_done"], t.one("pv_done"))

                    def mla_tile(n):
                        bank, k, of_k, of = MLA_TILES[n]
                        hi, lo = (KNH, KNL) if of_k == 1 else (QNH, QNL)
                        if n == 0:
                            self.begin()
                        if k == 0:
                            self.bank_free(of)
                        ins = self.products(bank, n, 8, hi, lo, k, k == 0, k == of_k - 1)
                        if n == 7:
                            self.finish(ins)
                        elif k == of_k - 1:
                            ins.then_inc(sems["part_done"], t.one("part_done"))

                    def project(first, last):
                        for n in range(first, last):
                            if kind == "sw":
                                self.some(n // 8, n % 8, 2)
                            elif n < 8:
                                self.some(0, n, 1)
                            else:
                                mla_tile(n - 8)

                    def start():
                        if kind == "mla":
                            pe.wait_ge(sems["evicted"], t.at("evicted", LBANKS))
                        else:
                            pe.wait_ge(sems["evicted"], t.at("evicted", LBANKS - 1))
                        if kind != "sw":
                            self.turn_v(VF)
                            t.up("v_token")
                        s_unit(0, 0)
                        s_unit(0, 1)

                    if kind == "da":
                        for b in range(4):
                            self.whole(b)
                    else:
                        project(0, 16)
                    start()

                    def body(it):
                        more = not isinstance(it, int) or it < 3
                        t.up("o_used")
                        if kind == "da":
                            t.up("sum_used")
                            for i in range(QT):
                                if i + 1 < QT:
                                    s_unit(i + 1, 0)
                                    s_unit(i + 1, 1)
                                if more:
                                    if i == 3:
                                        pe.wait_ge(sems["sum_used"], t.at("sum_used"))
                                    for k in range(4):
                                        self.some(i, k, LBANKS)
                                if i == 0:
                                    pe.wait_ge(sems["v_token"], t.at("v_token"))
                                t_unit(2 * i, i)
                                if more:
                                    for k in range(4, 8):
                                        self.some(i, k, LBANKS)
                                if i == 0:
                                    pe.wait_ge(sems["o_used"], t.at("o_used"))
                                pv_unit(i, i, 0)
                            if more:
                                start()
                            pe.wait_ge(sems["evicted"], t.at("evicted", LBANKS))
                            self.sums(3, 1, lambda k: TA[:])
                        else:
                            for u, (i, m) in enumerate(UNITS):
                                if u + 2 < len(UNITS):
                                    s_unit(*UNITS[u + 2])
                                if u == 0:
                                    if more:
                                        project(0, 3)
                                    if kind == "mla":
                                        pe.wait_ge(sems["v_token"], t.at("v_token"))
                                    t_unit(0, 0)
                                    if more:
                                        project(3, 6)
                                elif more and u < 6:
                                    project(2 * u + 4, 2 * u + 6)
                                if u + 1 < len(UNITS):
                                    t_unit(u + 1, UNITS[u + 1][0])
                                if u == 0:
                                    pe.wait_ge(sems["o_used"], t.at("o_used"))
                                pv_unit(u, i, m)
                            if more:
                                start()
                    t.turns(4, body)

                def gates(self, l):
                    def body(it):
                        for j in range(6):
                            b, g = j % 3, 2 * (j % 2)
                            self.bank_free(2)
                            self.begin()
                            for k in range(KT):
                                self.products(g, k, 12, HH, HL, k, k == 0, k == KT - 1)
                            for k in range(4):
                                ins = self.products(g + 1, KT + k, 12, ZH, ZL, 4 * b + k, k == 0, k == 3)
                            self.finish(ins)
                    t.turns(4, body)

                def linear(self, parts, hi, lo, m, src=None):
                    if src is not None:
                        t.up("operand", KT)

                    def body(it):
                        for j in range(2):
                            self.bank_free(2)
                            for c in range(parts):
                                self.begin()
                                n = WIDTH[t.c]
                                for k in range(n):
                                    if src is not None and isinstance(it, int) and it + j == 0:
                                        pe.wait_ge(sems["operand"], t.at("operand", k + 1 - KT))
                                    ins = self.products(j, k, n, hi, lo, c * n + k, c + k == 0, c == parts - 1 and k == n - 1)
                                self.finish(ins)
                    t.turns(4, body)

                def ple(self, l):
                    t.up("operand", 10)
                    pe.wait_ge(sems["operand"], t.at("operand"))

                    def body(it):
                        for j in range(2):
                            self.bank_free(2)
                            self.begin()
                            for k in range(KT):
                                self.products(2 * j, k, 10, HH, HL, k, k == 0, k == KT - 1)
                            for k in range(2):
                                ins = self.products(2 * j + 1, KT + k, 10, PH, PL, k, k == 0, k == 1)
                            self.finish(ins)
                    t.turns(4, body)

                def ffn_up(self, l):
                    def body(it):
                        for j in range(2):
                            self.whole(2 * j)
                            self.whole(2 * j + 1)
                    t.turns(FT // 2, body)

                def retention(self):
                    def body(h):
                        for j in range(4):
                            self.whole(j)
                        for j in range(4):
                            self.whole(j)
                            pe.wait_ge(sems["evicted"], t.at("evicted", LBANKS))
                            if j:
                                pe.wait_ge(sems["v_token"], t.at("v_token"))
                            self.turn_v(RVF2)
                            t.up("v_token")
                        t.up("rotated", 4)
                        pe.wait_ge(sems["rotated"], t.at("rotated"))
                        for kt in range(QT):
                            if kt >= 2:
                                t.up("operand")
                                pe.wait_ge(sems["operand"], t.at("operand"))
                            n = SEQ - kt * P
                            for c in range(2):
                                ins = pe.matmul(banks[S0 + kt % 2][:, 0:n], RK[:, c, kt * P:(kt + 1) * P],
                                                RQ[:, c, kt * P:SEQ], start=(c == 0), stop=(c == 1))
                            ins.then_inc(sems["s_ready"], t.one("s_ready"))
                        t.up("operand", 2)
                        pe.wait_ge(sems["operand"], t.at("operand"))
                        pe.wait_ge(sems["v_token"], t.at("v_token"))
                        for e in range(4):
                            t.up("y_copied")
                            if e >= 2:
                                pe.wait_ge(sems["y_copied"], t.at("y_copied", -2))
                            for kt in range(QT):
                                ins = pe.matmul(banks[TURN + e % 2][:, kt * P:SEQ], RVT[:, kt, e * P:(e + 1) * P],
                                                RP[:, kt, kt * P:SEQ], start=(kt == 0), stop=(kt == QT - 1))
                            ins.then_inc(sems["small"], t.one("small"))
                        for j in range(4):
                            self.whole(j)
                        pe.wait_ge(sems["y_copied"], t.at("y_copied"))
                        for e in range(4):
                            ins = pe.matmul(banks[S0][:], ONES[:], RY[:, e, :], start=(e == 0), stop=(e == 3))
                        ins.then_inc(sems["small"], t.one("small"))
                        self.sums(S0 + 1, 4, lambda e: RSQ[:, e, :])
                    t.turns(RET_HEADS, body)

                def dilated(self):
                    def tiles_of(par, x, ks):
                        hi, lo = (H2H, H2L) if x % 3 == 0 else (HH, HL)
                        if ks[0] == 0:
                            self.bank_free(2)
                            self.begin()
                        for k in ks:
                            ins = self.products(dil_bank(par, x), k, 8, hi, lo, k, k == 0, k == KT - 1)
                        if ks[-1] == KT - 1:
                            self.finish(ins)

                    def post(x, begun):
                        if x % 3 < 2:
                            t.up("operand")
                            pe.wait_ge(sems["operand"], t.at("operand"))
                            if x % 3 == 0:
                                pe.wait_ge(sems["v_token"], t.at("v_token"))
                            else:
                                pe.wait_ge(sems["rotated"], t.at("rotated"))
                            pe.matmul(banks[DAUX][:], PERM[:], (TA, TB)[x % 3][:], start=True, stop=True).then_inc(sems["swapped"], t.one("swapped"))
                            t.up("rotated")
                        else:
                            pe.wait_ge(sems["evicted"], t.at("evicted", LBANKS - begun))
                            pe.wait_ge(sems["rotated"], t.at("rotated"))
                            self.turn_v(DF, DAUX)
                            t.up("v_token")

                    def s_unit(par, u):
                        i, m = UNITS[u]
                        r = slice(64 * m, 64 * m + 64)
                        t.up("scored")
                        pe.wait_ge(sems["scored"], t.at("scored", CREDITS["scored"] - 1))
                        for g in range(3):
                            kb, n = key_blocks("sw" if g == 0 else "da", i)
                            ins = pe.matmul(banks[DSCORES[g]][:, 0:n * P], DQ[par][r, g, i * P:(i + 1) * P],
                                            DK[par][r, g, kb * P:(kb + n) * P], start=True, stop=True)
                        ins.then_inc(sems["s_ready"], t.one("s_ready"))

                    def t_group(u, g):
                        i, m = UNITS[u]
                        at_ = sum(key_blocks("sw" if f == 0 else "da", i)[1] for f in range(g)) * P
                        t.up("pt_copied")
                        pe.wait_ge(sems["pt_copied"], t.at("pt_copied"))
                        for b in range(key_blocks("sw" if g == 0 else "da", i)[1]):
                            ins = pe.transpose(banks[TURN][:, b * P:(b + 1) * P], DP[u % 2][:, at_ + b * P:at_ + (b + 1) * P], ID[:])
                        ins.then_inc(sems["turned"], t.one("turned"))

                    def pv_unit(par, u):
                        i, m = UNITS[u]
                        pe.wait_ge(sems["pt_copied"], t.at("pt_copied", CREDITS["pt_copied"]))
                        if u == 0:
                            t.up("o_used")
                            pe.wait_ge(sems["o_used"], t.at("o_used"))
                        r = slice(64 * m, 64 * m + 64)
                        for g in range(3):
                            kb, n = key_blocks("sw" if g == 0 else "da", i)
                            for b in range(n):
                                ins = pe.matmul(banks[OUTB][r, i * P:(i + 1) * P], DVT[par][:, g, kb + b, 64 * m:64 * m + 64],
                                                DPT[g][:, b * P:(b + 1) * P], start=(g + b == 0), stop=(g == 2 and b == n - 1))
                        ins.then_inc(sems["pv_done"], t.one("pv_done"))

                    def pair(par, more):
                        nxt = 1 - par
                        for u in range(len(UNITS)):
                            if u + 1 < len(UNITS):
                                s_unit(par, u + 1)
                            if u == 0:
                                if more:
                                    tiles_of(nxt, 0, range(KT))
                                post(8, more)
                            if more:
                                tiles_of(nxt, u + 1, range(0, 3))
                                post(u, True)
                            t.up("probs")
                            pe.wait_ge(sems["probs"], t.at("probs"))
                            for g, ks in enumerate((range(3, 5), range(5, 7), range(7, 8))):
                                t_group(u, g)
                                if more:
                                    tiles_of(nxt, u + 1, ks)
                            pv_unit(par, u)
                        if more:
                            pe.wait_ge(sems["rotated"], t.at("rotated"))
                            s_unit(nxt, 0)

                    for x in range(9):
                        tiles_of(0, x, range(KT))
                        if x < 8:
                            post(x, False)
                    pe.wait_ge(sems["rotated"], t.at("rotated"))
                    s_unit(0, 0)

                    def body(it):
                        pair(0, True)
                        pair(1, not isinstance(it, int) or it < KT // 2 - 1)
                    t.turns(KT // 2, body)

            e = Programs()
            e.t = t
            run(e)

        @block.scalar
        def _(act):
            t = Tally(act)

            def hi_part():
                if t.c >= len(WIDTH):
                    return
                slot, n = t.c % RING, WIDTH[t.c] * P
                t.up(f"raw{slot}", 16)
                act.wait_ge(sems[f"raw{slot}"], t.at(f"raw{slot}"))
                t.up("slot_free")
                act.wait_ge(sems["slot_free"], t.at("slot_free"))
                act.copy(WH[slot][:, 0:n], RAW[slot][:, 0:n]).then_inc(sems["hi_done"], t.one("hi_done"))
                t.c += 1

            def std():
                t.up("var_ready")
                act.wait_ge(sems["var_ready"], t.at("var_ready"))
                act.activation(VAR[:], VAR[:], ACT.Sqrt).then_inc(sems["std_ready"], t.one("std_ready"))

            def squares(n, src, dst):
                for k in range(n):
                    act.activation(dst(k), src(k), ACT.Square).then_inc(sems["squared"], t.one("squared"))

            class Programs:
                mine, stage = "stage_act", 0

                def begin_stage(self):
                    act.wait_ge(sems["stage_pe"], t.at("stage_pe"))
                    act.wait_ge(sems["stage_act"], t.at("stage_act"))
                    act.wait_ge(sems["stage_dve"], t.at("stage_dve"))

                def end(self):
                    act.drain().then_inc(sems["stage_act"], t.one("stage_act"))

                def setup(self):
                    act.sem_inc(sems["pt_copied"], 1)
                    hi_part()
                    t.up("operand")
                    t.up("var_ready")
                    act.wait_ge(sems["var_ready"], t.at("var_ready"))
                    act.activation(SIN[:], TA[:], ACT.Sin).then_inc(sems["std_ready"], t.one("std_ready"))
                    act.activation(COS[:], TB[:], ACT.Sin).then_inc(sems["std_ready"], t.one("std_ready"))
                    t.up("var_ready")
                    act.wait_ge(sems["var_ready"], t.at("var_ready"))
                    act.activation(sm(DEN, 4), sm(MX, 4), ACT.Exp).then_inc(sems["std_ready"], t.one("std_ready"))
                    t.up("operand", 2)
                    act.wait_ge(sems["operand"], t.at("operand"))
                    act.dma_start(scratch[0], RVF[:]).then_inc(sems["scratch"], t.add("scratch", 16))
                    act.dma_start(scratch[1], RVW[:]).then_inc(sems["scratch"], t.add("scratch", 16))
                    act.wait_ge(sems["scratch"], t.at("scratch"))
                    t.up("small")

                def prenorm(self, targets, sq):
                    squares(KT, lambda k: X[:, k, :], lambda k: sq[:, k, :])
                    std()

                def postnorm(self, m, sq, g):
                    squares(KT, lambda k: m[:, k, :], lambda k: sq[:, k, :])
                    std()

                def v_out(self, dst, bank=TURN):
                    t.up("v_turned")
                    act.wait_ge(sems["v_turned"], t.at("v_turned"))
                    act.copy(dst, banks[bank][:].rearrange("p (b k) -> p b k", b=QT)).then_inc(sems["v_token"], t.one("v_token"))

                def latents(self, l):
                    for j in range(7):
                        hi_part()
                    self.v_out(CV[:])
                    t.up("operand")
                    act.wait_ge(sems["operand"], t.at("operand"))
                    squares(3, lambda k: LQ[:, k, :], lambda k: SS[k][:])
                    std()
                    std()

                def attention(self, kind, l):
                    def e_unit(u, m):
                        _, n = key_blocks(kind, UNITS[u][0])
                        t.up("scored")
                        act.wait_ge(sems["scored"], t.at("scored", CREDITS["scored"]))
                        if kind == "sw":
                            act.activation(sm(ES + u), sm(ST + m), ACT.Exp, bias=sm(NM + u)).then_inc(sems["act_step"], t.one("act_step"))
                        act.activation(SS[u % 4][:, 0:n * P], SS[u % 4][:, 0:n * P], ACT.Exp, bias=sm(NM + u), accum_out=sm(DEN + u)).then_inc(sems["exped"], t.one("exped"))

                    def c_unit(n_unit, i):
                        _, n = key_blocks(kind, i)
                        t.up("turned")
                        act.wait_ge(sems["turned"], t.at("turned", CREDITS["turned"]))
                        t.up("pv_done")
                        act.wait_ge(sems["pv_done"], t.at("pv_done"))
                        act.copy(PT[n_unit % 2][:, 0:n * P], banks[TURN][:, 0:n * P]).then_inc(sems["pt_copied"], t.one("pt_copied"))

                    def start():
                        if kind != "sw":
                            self.v_out(VT[:])
                        t.up("z_ready")
                        act.wait_ge(sems["z_ready"], t.at("z_ready"))
                        act.activation(TC[:], (NZ if kind == "mla" else TC)[:], ACT.Silu).then_inc(sems["gate"], t.one("gate"))
                        e_unit(0, 0)
                        e_unit(1, 1)

                    for _ in range({"da": 4, "mla": 2, "sw": 1}[kind]):
                        hi_part()
                    start()

                    def body(it):
                        more = not isinstance(it, int) or it < 3
                        t.up("o_used")
                        if kind == "da":
                            for i in range(QT):
                                if more:
                                    hi_part()
                                if i + 1 < QT:
                                    e_unit(2 * i + 2, 0)
                                    e_unit(2 * i + 3, 1)
                                c_unit(i, i)
                            act.wait_ge(sems["pv_done"], t.at("pv_done", CREDITS["pv_done"]))
                            act.wait_ge(sems["o_used"], t.at("o_used", CREDITS["o_used"]))
                            act.activation(TA[:], banks[OUTB][:], ACT.Square).then_inc(sems["squared"], t.one("squared"))
                            if more:
                                start()
                            std()
                        else:
                            for u in range(len(UNITS)):
                                if kind == "sw" and (u == 0 or more and u == 1) or kind == "mla" and more and u in (0, 2):
                                    hi_part()
                                if u + 2 < len(UNITS):
                                    e_unit(u + 2, u % 2)
                                if u == 0:
                                    c_unit(0, 0)
                                if u + 1 < len(UNITS):
                                    c_unit(u + 1, UNITS[u + 1][0])
                            act.wait_ge(sems["pv_done"], t.at("pv_done", CREDITS["pv_done"]))
                            if more:
                                start()
                    t.turns(4, body)

                def gates(self, l):
                    def body(it):
                        for j in range(6):
                            hi_part()
                            t.up("gate_in")
                            act.wait_ge(sems["gate_in"], t.at("gate_in"))
                            T_ = (TA, TB)[j % 2]
                            act.activation(T_[:], T_[:], ACT.Sigmoid).then_inc(sems["gate"], t.one("gate"))
                    t.turns(4, body)

                def linear(self, parts, hi, lo, m, src=None):
                    if src is not None:
                        for k in range(KT):
                            act.copy(hi[:, k, :], src[:, k, :]).then_inc(sems["operand_hi"], t.one("operand_hi"))

                    def body(it):
                        for j in range(2 * parts):
                            hi_part()
                    t.turns(4, body)

                def ple(self, l):
                    def body(it):
                        for j in range(2):
                            hi_part()
                            t.up("chunk_done")
                            act.wait_ge(sems["chunk_done"], t.at("chunk_done", CREDITS["chunk_done"]))
                            act.activation((TA, TB)[j][:], banks[2 * j][:], ACT.Sigmoid).then_inc(sems["gate"], t.one("gate"))
                    t.k["chunk_done"] = t.c - 1
                    t.up("operand", 10)
                    t.turns(4, body)

                def ffn_up(self, l):
                    def body(it):
                        for j in range(2):
                            hi_part()
                            hi_part()
                            t.up("gate_in")
                            act.wait_ge(sems["gate_in"], t.at("gate_in"))
                            act.activation(GL[j][:], CO[j][:], ACT.Gelu_apprx_tanh).then_inc(sems["gate"], t.one("gate"))
                    t.turns(FT // 2, body)

                def retention(self):
                    def body(h):
                        for j in range(4):
                            hi_part()
                        for j in range(4):
                            hi_part()
                            self.v_out(RVT[:, :, j * P:(j + 1) * P])
                        for e in range(4):
                            t.up("small")
                            act.wait_ge(sems["small"], t.at("small"))
                            act.copy(RY[:, e, :], banks[TURN + e % 2][:]).then_inc(sems["y_copied"], t.one("y_copied"))
                        for j in range(4):
                            hi_part()
                        t.up("small")
                        for e in range(4):
                            t.up("centred")
                            act.wait_ge(sems["centred"], t.at("centred"))
                            act.activation(RSQ[:, e, :], RY[:, e, :], ACT.Square).then_inc(sems["squared"], t.one("squared"))
                        std()
                        for e in range(4):
                            t.up("gate_in")
                            act.wait_ge(sems["gate_in"], t.at("gate_in"))
                            T_ = (TA, TB)[e % 2]
                            act.activation(T_[:], T_[:], ACT.Silu).then_inc(sems["gate"], t.one("gate"))
                    t.turns(RET_HEADS, body)

                def dilated(self):
                    def e_unit(u):
                        t.up("scored")
                        act.wait_ge(sems["scored"], t.at("scored", CREDITS["scored"]))
                        w = dil_width(UNITS[u][0])
                        act.activation(DP[u % 2][:, 0:w], DP[u % 2][:, 0:w], ACT.Exp, bias=sm(NM + u), accum_out=sm(DEN + u)).then_inc(sems["exped"], t.one("exped"))

                    def c_unit(u):
                        i, m = UNITS[u]
                        for g in range(3):
                            _, n = key_blocks("sw" if g == 0 else "da", i)
                            t.up("turned")
                            act.wait_ge(sems["turned"], t.at("turned", CREDITS["turned"]))
                            if g == 0:
                                act.wait_ge(sems["pv_done"], t.at("pv_done", CREDITS["pv_done"]))
                            act.copy(DPT[g][:, 0:n * P], banks[TURN][:, 0:n * P]).then_inc(sems["pt_copied"], t.one("pt_copied"))
                        t.up("pv_done")

                    def pair(par, more):
                        nxt = 1 - par
                        for u in range(len(UNITS)):
                            if more:
                                hi_part()
                            if u + 1 < len(UNITS):
                                e_unit(u + 1)
                            if u == 0:
                                self.v_out(DVT[par][:, 2], DAUX)
                                if more:
                                    hi_part()
                            elif more and u % 3 == 2:
                                self.v_out(DVT[nxt][:, u // 3], DAUX)
                            c_unit(u)
                        if more:
                            e_unit(0)

                    for x in range(9):
                        hi_part()
                        if x % 3 == 2 and x < 8:
                            self.v_out(DVT[0][:, x // 3], DAUX)
                    e_unit(0)

                    def body(it):
                        pair(0, True)
                        pair(1, not isinstance(it, int) or it < KT // 2 - 1)
                    t.turns(KT // 2, body)

            e = Programs()
            e.t = t
            run(e)

        @block.vector
        def _(dve):
            t = Tally(dve)

            def lo_part():
                if t.c >= len(WIDTH):
                    return
                slot, n = t.c % RING, WIDTH[t.c] * P
                t.up("hi_done")
                dve.wait_ge(sems["hi_done"], t.at("hi_done"))
                dve.tensor_tensor(WL[slot][:, 0:n], RAW[slot][:, 0:n], WH[slot][:, 0:n].bitcast(F32), ALU.subtract).then_inc(sems["lo_done"], t.one("lo_done"))
                t.c += 1

            def passed():
                dve.sem_inc(sems["waits_passed"], 1)

            def signal(name):
                dve.sem_inc(sems[name], 1)
                t.up(name)

            def chunk():
                t.up("chunk_done")
                dve.wait_ge(sems["chunk_done"], t.at("chunk_done", CREDITS["chunk_done"]))

            def split(hi, lo, src):
                dve.tensor_copy(hi, src).then_inc(sems["dve_step"], t.one("dve_step"))
                dve.wait_ge(sems["dve_step"], t.at("dve_step"))
                dve.tensor_tensor(lo, src, hi.bitcast(F32), ALU.subtract).then_inc(sems["dve_step"], t.one("dve_step"))
                dve.wait_ge(sems["dve_step"], t.at("dve_step"))

            def rstd(bank, n, dst=RSTD):
                t.up("summed")
                dve.wait_ge(sems["summed"], t.at("summed"))
                dve.tensor_scalar(VAR[:], banks[bank][:], 1.0 / n, EPS, ALU.mult, ALU.add).then_inc(sems["var_ready"], t.one("var_ready"))
                t.up("std_ready")
                dve.wait_ge(sems["std_ready"], t.at("std_ready"))
                dve.reciprocal(dst[:], VAR[:]).then_inc(sems["dve_step"], t.one("dve_step"))
                dve.wait_ge(sems["dve_step"], t.at("dve_step"))

            class Programs:
                mine, stage = "stage_dve", 0

                def begin_stage(self):
                    dve.wait_ge(sems["stage_pe"], t.at("stage_pe"))
                    dve.wait_ge(sems["stage_act"], t.at("stage_act"))
                    dve.wait_ge(sems["stage_dve"], t.at("stage_dve"))

                def end(self):
                    dve.drain().then_inc(sems["stage_dve"], t.one("stage_dve"))

                def setup(self):
                    for n, c in (("lo_done", RING), ("evicted", LBANKS), ("scored", 2), ("o_used", 1), ("sum_used", 1)):
                        dve.sem_inc(sems[n], c)
                    dve.memset(ONES[:], 1.0).then_inc(sems["dve_step"], t.one("dve_step"))
                    dve.wait_ge(sems["dve_step"], t.at("dve_step"))
                    lo_part()
                    t.up("loaded", 160)
                    dve.wait_ge(sems["loaded"], t.at("loaded"))
                    dve.memset(TAB[BUCKETS:BUCKETS + 1, :], 1.0).then_inc(sems["operand"], t.one("operand"))
                    dve.wait_ge(sems["operand"], t.at("operand"))
                    dve.tensor_copy(ANG[:], POSI[:]).then_inc(sems["dve_step"], t.one("dve_step"))
                    dve.wait_ge(sems["dve_step"], t.at("dve_step"))
                    dve.tensor_scalar(ANG[:], ANG[:], COLS[:, 0:1], None, ALU.mult).then_inc(sems["dve_step"], t.one("dve_step"))
                    dve.wait_ge(sems["dve_step"], t.at("dve_step"))
                    dve.tensor_scalar(TC[:], ANG[:], 1.0 / (2 * math.pi), None, ALU.mult).then_inc(sems["dve_step"], t.one("dve_step"))
                    dve.wait_ge(sems["dve_step"], t.at("dve_step"))
                    dve.tensor_scalar(TC[:], TC[:], MAGIC, None, ALU.add).then_inc(sems["dve_step"], t.one("dve_step"))
                    dve.wait_ge(sems["dve_step"], t.at("dve_step"))
                    dve.tensor_scalar(TC[:], TC[:], -MAGIC, None, ALU.add).then_inc(sems["dve_step"], t.one("dve_step"))
                    dve.wait_ge(sems["dve_step"], t.at("dve_step"))
                    for part in (TWO_PI_A, TWO_PI_B, TWO_PI_C):
                        dve.scalar_tensor_tensor(ANG[:], TC[:], -part, ANG[:], ALU.mult, ALU.add).then_inc(sems["dve_step"], t.one("dve_step"))
                        dve.wait_ge(sems["dve_step"], t.at("dve_step"))
                    dve.tensor_scalar(TB[:], ANG[:], math.pi / 2, None, ALU.add).then_inc(sems["dve_step"], t.one("dve_step"))
                    dve.wait_ge(sems["dve_step"], t.at("dve_step"))
                    dve.tensor_scalar(TC[:], TB[:], math.pi, -2 * math.pi, ALU.is_gt, ALU.mult).then_inc(sems["dve_step"], t.one("dve_step"))
                    dve.wait_ge(sems["dve_step"], t.at("dve_step"))
                    dve.tensor_tensor(TB[:], TB[:], TC[:], ALU.add).then_inc(sems["dve_step"], t.one("dve_step"))
                    dve.wait_ge(sems["dve_step"], t.at("dve_step"))
                    dve.tensor_scalar(TB[:], TB[:], 3.1415925, -3.1415925, ALU.min, ALU.max).then_inc(sems["dve_step"], t.one("dve_step"))
                    dve.wait_ge(sems["dve_step"], t.at("dve_step"))
                    dve.tensor_scalar(TA[:], ANG[:], 3.1415925, -3.1415925, ALU.min, ALU.max).then_inc(sems["var_ready"], t.one("var_ready"))
                    t.up("std_ready", 2)
                    dve.wait_ge(sems["std_ready"], t.at("std_ready"))
                    dve.tensor_scalar(SIN[:], SIN[:], COLS[:, 1:2], None, ALU.mult).then_inc(sems["dve_step"], t.one("dve_step"))
                    dve.wait_ge(sems["dve_step"], t.at("dve_step"))
                    for l in range(DEPTH):
                        for a in range(2):
                            ins = dve.tensor_tensor_reduce(TC[:, 0:HEAD], LAM[:, l, 2 * a, :], LAM[:, l, 2 * a + 1, :], 1.0, 0.0,
                                                           ALU.mult, ALU.add, sm(MX + 2 * l + a))
                            if (l, a) == (DEPTH - 1, 1):
                                ins.then_inc(sems["var_ready"], t.one("var_ready"))
                            else:
                                ins.then_inc(sems["dve_step"], t.one("dve_step"))
                                dve.wait_ge(sems["dve_step"], t.at("dve_step"))
                    t.up("std_ready")
                    dve.wait_ge(sems["std_ready"], t.at("std_ready"))
                    for l in range(DEPTH):
                        dve.tensor_tensor(sm(LAMC + l), sm(DEN + 2 * l + 1), sm(DEN + 2 * l), ALU.subtract).then_inc(sems["dve_step"], t.one("dve_step"))
                        dve.wait_ge(sems["dve_step"], t.at("dve_step"))
                        dve.tensor_scalar(sm(LAMC + l), sm(LAMC + l), -LAM_INIT[l], None, ALU.add).then_inc(sems["dve_step"], t.one("dve_step"))
                        dve.wait_ge(sems["dve_step"], t.at("dve_step"))
                        dve.tensor_scalar(sm(SUBG + l), gain(f"subln{l}"), 1.0 - LAM_INIT[l], None, ALU.mult).then_inc(sems["dve_step"], t.one("dve_step"))
                        dve.wait_ge(sems["dve_step"], t.at("dve_step"))
                    t.up("small")
                    dve.wait_ge(sems["small"], t.at("small"))
                    for n, dst in enumerate((RVF, RVW)):
                        dve.tensor_copy(dst[:, 0:RV // 2], banks[2 * n][0:BHEADS, 0:RV // 2]).then_inc(sems["dve_step"], t.one("dve_step"))
                        dve.wait_ge(sems["dve_step"], t.at("dve_step"))
                        dve.tensor_copy(dst[:, RV // 2:RV], banks[2 * n + 1][0:BHEADS, 0:RV // 2]).then_inc(sems["operand"], t.one("operand"))
                        dve.wait_ge(sems["operand"], t.at("operand"))

                def prenorm(self, targets, sq):
                    for hi, lo, g in targets:
                        for k in range(KT):
                            dve.tensor_scalar(hi[:, k, :], X[:, k, :], gain(g, k), None, ALU.mult).then_inc(sems["dve_step"], t.one("dve_step"))
                        dve.wait_ge(sems["dve_step"], t.at("dve_step"))
                        for k in range(KT):
                            dve.scalar_tensor_tensor(lo[:, k, :], X[:, k, :], gain(g, k), hi[:, k, :].bitcast(F32),
                                    ALU.mult, ALU.subtract).then_inc(sems["dve_step"], t.one("dve_step"))
                    rstd(OUTB, D)

                def postnorm(self, m, sq, g):
                    rstd(OUTB, D)
                    for k in range(KT):
                        dve.scalar_tensor_tensor(m[:, k, :], m[:, k, :], gain(g, k), RSTD[:], ALU.mult, ALU.mult).then_inc(sems["dve_step"], t.one("dve_step"))
                    dve.wait_ge(sems["dve_step"], t.at("dve_step"))
                    for k in range(KT):
                        dve.tensor_tensor(X[:, k, :], X[:, k, :], m[:, k, :], ALU.add).then_inc(sems["dve_step"], t.one("dve_step"))

                def latents(self, l):
                    for j, dst in enumerate((LQ[:, 0, :], LQ[:, 1, :], LQ[:, 2, :], TA[:], TB[:], CK[:], VF[:])):
                        lo_part()
                        chunk()
                        dve.tensor_tensor(dst, banks[j % LBANKS][:], RSTD[:], ALU.mult).then_inc(sems["evicted"], t.one("evicted"))
                        dve.wait_ge(sems["evicted"], t.at("evicted", CREDITS["evicted"]))
                    dve.tensor_tensor(TA[:], TA[:], COS[:], ALU.mult).then_inc(sems["dve_step"], t.one("dve_step"))
                    dve.wait_ge(sems["dve_step"], t.at("dve_step"))
                    dve.tensor_tensor(TB[:], TB[:], SIN[:], ALU.mult).then_inc(sems["dve_step"], t.one("dve_step"))
                    dve.wait_ge(sems["dve_step"], t.at("dve_step"))
                    dve.tensor_tensor(KR[:], TA[:], TB[:], ALU.add).then_inc(sems["operand"], t.one("operand"))
                    dve.wait_ge(sems["operand"], t.at("operand"))
                    rstd(OUTB, 2 * P, RSTD2)
                    for k in range(2):
                        dve.scalar_tensor_tensor(TA[:], LQ[:, k, :], gain(f"mlaq{l}", k), RSTD2[:], ALU.mult, ALU.mult).then_inc(sems["dve_step"], t.one("dve_step"))
                        dve.wait_ge(sems["dve_step"], t.at("dve_step"))
                        split(QNH[:, k, :], QNL[:, k, :], TA[:])
                    rstd(S0, P, RSTD2)
                    dve.scalar_tensor_tensor(TA[:], LQ[:, 2, :], gain(f"mlakv{l}"), RSTD2[:], ALU.mult, ALU.mult).then_inc(sems["dve_step"], t.one("dve_step"))
                    dve.wait_ge(sems["dve_step"], t.at("dve_step"))
                    split(KNH[:, 0, :], KNL[:, 0, :], TA[:])
                    t.up("stage_loads", 128)
                    dve.wait_ge(sems["stage_loads"], t.at("stage_loads"))
                    if l == 0:
                        t.up("biased", 16 * BHEADS)
                        dve.wait_ge(sems["biased"], t.at("biased"))

                def attention(self, kind, l):
                    scale = float((HEAD + ROPE) ** -0.5) if kind == "mla" else float(HEAD ** -0.5)
                    branch = ("da", "mla", "sw").index(kind)

                    def u1(u):
                        i, m = UNITS[u]
                        _, n = key_blocks(kind, i)
                        w = n * P
                        t.up("s_ready")
                        dve.wait_ge(sems["s_ready"], t.at("s_ready"))
                        if kind == "da":
                            if m == 0:
                                t.up("turned")
                            dve.wait_ge(sems["turned"], t.at("turned", CREDITS["turned"] - 2))
                        else:
                            t.up("turned")
                            dve.wait_ge(sems["turned"], t.at("turned"))
                        if kind == "sw":
                            bias = BT[:, (m + 1) * 2 * P - w:(m + 1) * 2 * P]
                        else:
                            bias = (BT if kind == "da" else MASK)[:, SEQ - w:SEQ]
                        passed()
                        dve.tensor_tensor_reduce(SS[u % 4][:, 0:w], banks[S0 + m][:, 0:w], bias, 1.0, LOWEST, ALU.add, ALU.max, sm(MX + u)).then_inc(sems["dve_step"], t.one("dve_step"))
                        dve.wait_ge(sems["dve_step"], t.at("dve_step"))
                        if kind == "sw":
                            ins = dve.tensor_scalar(sm(NM + u), sm(MX + u), -1.0, sm(NST + m), ALU.mult, ALU.min)
                        else:
                            ins = dve.tensor_scalar(sm(NM + u), sm(MX + u), -1.0, None, ALU.mult)
                        ins.then_inc(sems["scored"], t.one("scored"))

                    def u2(u):
                        i, m = UNITS[u]
                        w = key_blocks(kind, i)[1] * P
                        t.up("exped")
                        dve.wait_ge(sems["exped"], t.at("exped"))
                        if kind == "sw":
                            dve.tensor_tensor(sm(DEN + u), sm(DEN + u), sm(ES + u), ALU.add).then_inc(sems["dve_step"], t.one("dve_step"))
                            dve.wait_ge(sems["dve_step"], t.at("dve_step"))
                        dve.reciprocal(sm(RC1 + u), sm(DEN + u)).then_inc(sems["dve_step"], t.one("dve_step"))
                        dve.wait_ge(sems["dve_step"], t.at("dve_step"))
                        S_ = SS[u % 4][:, 0:w]
                        if kind != "da":
                            dve.tensor_scalar(S_, S_, sm(RC1 + u), None, ALU.mult).then_inc(sems["probs"], t.one("probs"))
                        elif m == 1:
                            dve.tensor_scalar(S_, S_, sm(RC1 + u), sm(LAMC + l), ALU.mult, ALU.mult).then_inc(sems["dve_step"], t.one("dve_step"))
                            dve.wait_ge(sems["dve_step"], t.at("dve_step"))
                            F_ = SS[(u - 1) % 4][:, 0:w]
                            dve.scalar_tensor_tensor(F_, F_, sm(RC1 + u - 1), S_, ALU.mult, ALU.add).then_inc(sems["probs"], t.one("probs"))

                    def evict(dst, bank, s=None):
                        if s is None:
                            dve.tensor_tensor(dst, banks[bank][:], RSTD[:], ALU.mult).then_inc(sems["evicted"], t.one("evicted"))
                            dve.wait_ge(sems["evicted"], t.at("evicted", CREDITS["evicted"]))
                        else:
                            dve.scalar_tensor_tensor(dst, banks[bank][:], s, RSTD[:], ALU.mult, ALU.mult).then_inc(sems["evicted"], t.one("evicted"))
                            dve.wait_ge(sems["evicted"], t.at("evicted", CREDITS["evicted"]))

                    def biases(it):
                        if kind != "mla":
                            src = (BDA if kind == "da" else BSW)[:, bass.ds(it, 1), :].rearrange("p o n -> p (o n)")
                            dve.tensor_scalar(BT[:], src, 1.0, None, ALU.mult).then_inc(sems["dve_step"], t.one("dve_step"))

                    def sinks(it):
                        if kind == "sw":
                            dve.tensor_scalar(sm(ST, 2), SM[:, bass.ds(SINK + 2 * it, 2)], 1.0, None, ALU.mult).then_inc(sems["dve_step"], t.one("dve_step"))
                            dve.tensor_scalar(sm(NST, 2), SM[:, bass.ds(SINK + 2 * it, 2)], -1.0, None, ALU.mult).then_inc(sems["dve_step"], t.one("dve_step"))

                    def part():
                        t.up("part_done")
                        dve.wait_ge(sems["part_done"], t.at("part_done"))

                    def mla_evict(n):
                        if n == 0:
                            chunk()
                            evict(NZ[:], 0)
                        elif n == 1:
                            part()
                            dve.tensor_copy(VF[:], banks[1][:]).then_inc(sems["evicted"], t.one("evicted"))
                        elif n == 2:
                            part()
                            dve.tensor_scalar(AQ[:], banks[2][:], scale, None, ALU.mult).then_inc(sems["evicted"], t.one("evicted"))
                        elif n == 3:
                            part()
                            dve.scalar_tensor_tensor(AR[:], banks[3][:], scale, COS[:], ALU.mult, ALU.mult).then_inc(sems["evicted"], t.one("evicted"))
                        elif n == 4:
                            part()
                            dve.scalar_tensor_tensor(TA[:], banks[0][:], scale, SIN[:], ALU.mult, ALU.mult).then_inc(sems["evicted"], t.one("evicted"))
                            dve.wait_ge(sems["evicted"], t.at("evicted", CREDITS["evicted"]))
                            dve.tensor_tensor(AR[:], AR[:], TA[:], ALU.add).then_inc(sems["dve_step"], t.one("dve_step"))
                            dve.wait_ge(sems["dve_step"], t.at("dve_step"))
                        else:
                            chunk()
                            dve.tensor_copy(AK[:], banks[1][:]).then_inc(sems["evicted"], t.one("evicted"))

                    def gate_tile():
                        if kind != "mla":
                            chunk()
                            evict(TC[:], 3 if kind == "da" else 1)
                        signal("z_ready")

                    def first_units():
                        u1(0)
                        if kind == "da":
                            u1(1)
                            u2(0)
                            u2(1)
                        else:
                            u2(0)
                            u1(1)

                    biases(0)
                    sinks(0)
                    if kind == "da":
                        for j, dst in enumerate((AQ, AK, VF)):
                            lo_part()
                            chunk()
                            evict(dst[:], j, (scale, None, None)[j])
                        lo_part()
                    elif kind == "sw":
                        lo_part()
                        chunk()
                        evict(AQ[:], 0, scale)
                    else:
                        lo_part()
                        mla_evict(0)
                        lo_part()
                        for n in range(1, 6):
                            mla_evict(n)
                        dve.wait_ge(sems["evicted"], t.at("evicted", CREDITS["evicted"]))
                    gate_tile()
                    first_units()

                    def body(it):
                        more = not isinstance(it, int) or it < 3
                        if kind == "da":
                            for i in range(QT):
                                if i + 1 < QT:
                                    u1(2 * i + 2)
                                    u1(2 * i + 3)
                                if more:
                                    lo_part()
                                if i + 1 < QT:
                                    u2(2 * i + 2)
                                    u2(2 * i + 3)
                                if more and i == 2:
                                    chunk()
                                    evict(AQ[:], 0, scale)
                                    chunk()
                                    evict(AK[:], 1)
                                elif more and i == 3:
                                    chunk()
                                    evict(VF[:], 2)
                                    biases(it + 1)
                            t.up("pv_done", QT)
                        else:
                            for u in range(len(UNITS)):
                                if u + 1 < len(UNITS):
                                    u2(u + 1)
                                if u + 2 < len(UNITS):
                                    u1(u + 2)
                                if kind == "sw" and (u == 0 or more and u == 1) or kind == "mla" and more and u in (0, 2):
                                    lo_part()
                                if not more:
                                    continue
                                if kind == "sw" and u == 5:
                                    chunk()
                                    evict(AQ[:], 0, scale)
                                    biases(it + 1)
                                elif kind == "mla":
                                    if u == 2:
                                        dve.wait_ge(sems["gate"], t.at("gate", 1))
                                    for n in {2: (0,), 3: (1,), 5: (2, 3), 6: (4, 5)}.get(u, ()):
                                        mla_evict(n)
                            t.up("pv_done", len(UNITS))
                        t.up("gate")
                        dve.wait_ge(sems["gate"], t.at("gate"))
                        dve.wait_ge(sems["pv_done"], t.at("pv_done", CREDITS["pv_done"]))
                        dve.tensor_tensor(TB[:], banks[OUTB][:], TC[:], ALU.mult).then_inc(sems["o_used"], t.one("o_used"))
                        dve.wait_ge(sems["o_used"], t.at("o_used", CREDITS["o_used"]))
                        if more:
                            sinks(it + 1)
                            gate_tile()
                            first_units()
                        if kind == "da":
                            rstd(3, P, RSTD2)
                            signal("sum_used")
                            dve.scalar_tensor_tensor(TB[:], TB[:], sm(SUBG + l), RSTD2[:], ALU.mult, ALU.mult).then_inc(sems["dve_step"], t.one("dve_step"))
                            dve.wait_ge(sems["dve_step"], t.at("dve_step"))
                        z = bass.ds(it + 4 * branch, 1)
                        split(ZH[:, z, :].rearrange("p o n -> p (o n)"), ZL[:, z, :].rearrange("p o n -> p (o n)"), TB[:])
                    t.turns(4, body)

                def gates(self, l):
                    def body(it):
                        for j in range(6):
                            b, g, T_ = j % 3, 2 * (j % 2), (TA, TB)[j % 2]
                            lo_part()
                            chunk()
                            dve.tensor_tensor(T_[:], banks[g][:], RSTD[:], ALU.mult).then_inc(sems["gate_in"], t.one("gate_in"))
                            t.up("gate")
                            dve.wait_ge(sems["gate"], t.at("gate"))
                            if b == 0:
                                dve.tensor_tensor(TC[:], T_[:], banks[g + 1][:], ALU.mult).then_inc(sems["evicted"], t.one("evicted"))
                                dve.wait_ge(sems["evicted"], t.at("evicted", CREDITS["evicted"]))
                            else:
                                dve.tensor_tensor(T_[:], T_[:], banks[g + 1][:], ALU.mult).then_inc(sems["evicted"], t.one("evicted"))
                                dve.wait_ge(sems["evicted"], t.at("evicted", CREDITS["evicted"]))
                                dve.tensor_tensor(TC[:], TC[:], T_[:], ALU.add).then_inc(sems["dve_step"], t.one("dve_step"))
                                dve.wait_ge(sems["dve_step"], t.at("dve_step"))
                            if b == 2:
                                n = bass.ds(2 * it + j // 3, 1)
                                split(YH[:, n, :].rearrange("p o n -> p (o n)"), YL[:, n, :].rearrange("p o n -> p (o n)"), TC[:])
                    t.turns(4, body)

                def linear(self, parts, hi, lo, m, src=None):
                    if src is not None:
                        for k in range(KT):
                            t.up("operand_hi")
                            dve.wait_ge(sems["operand_hi"], t.at("operand_hi"))
                            dve.tensor_tensor(lo[:, k, :], src[:, k, :], hi[:, k, :].bitcast(F32), ALU.subtract).then_inc(sems["operand"], t.one("operand"))

                    def body(it):
                        for j in range(2):
                            for c in range(parts):
                                lo_part()
                                chunk()
                            n = bass.ds(2 * it + j, 1)
                            dve.tensor_copy(m[:, n, :].rearrange("p o n -> p (o n)"), banks[j][:]).then_inc(sems["evicted"], t.one("evicted"))
                    t.turns(4, body)

                def ple(self, l):
                    for k in range(KT):
                        dve.tensor_copy(HH[:, k, :], X[:, k, :]).then_inc(sems["dve_step"], t.one("dve_step"))
                        dve.wait_ge(sems["dve_step"], t.at("dve_step"))
                        dve.tensor_tensor(HL[:, k, :], X[:, k, :], HH[:, k, :].bitcast(F32), ALU.subtract).then_inc(sems["operand"], t.one("operand"))
                        dve.wait_ge(sems["operand"], t.at("operand"))
                    t.up("stage_loads", 16)
                    dve.wait_ge(sems["stage_loads"], t.at("stage_loads"))
                    for k in range(2):
                        dve.tensor_copy(PH[:, k, :], PX[:, k, :]).then_inc(sems["dve_step"], t.one("dve_step"))
                        dve.wait_ge(sems["dve_step"], t.at("dve_step"))
                        dve.tensor_tensor(PL[:, k, :], PX[:, k, :], PH[:, k, :].bitcast(F32), ALU.subtract).then_inc(sems["operand"], t.one("operand"))
                        dve.wait_ge(sems["operand"], t.at("operand"))

                    def body(it):
                        for j in range(2):
                            lo_part()
                            chunk()
                            t.up("gate")
                            dve.wait_ge(sems["gate"], t.at("gate"))
                            T_ = (TA, TB)[j]
                            dve.tensor_tensor(T_[:], T_[:], banks[2 * j + 1][:], ALU.mult).then_inc(sems["evicted"], t.one("evicted"))
                            dve.wait_ge(sems["evicted"], t.at("evicted", CREDITS["evicted"]))
                            xn = X[:, bass.ds(2 * it + j, 1), :].rearrange("p o n -> p (o n)")
                            dve.tensor_tensor(xn, xn, T_[:], ALU.add).then_inc(sems["dve_step"], t.one("dve_step"))
                            dve.wait_ge(sems["dve_step"], t.at("dve_step"))
                    t.turns(4, body)

                def ffn_up(self, l):
                    for n in range(2):
                        dve.memset(GE[n][:, 0:2], 0.0).then_inc(sems["dve_step"], t.one("dve_step"))
                        dve.wait_ge(sems["dve_step"], t.at("dve_step"))

                    def body(it):
                        for j in range(2):
                            def conv(c):
                                k = GAINS[f"conv{l}"] + c * FT + 2 * it + j
                                return G[:, bass.ds(k, 1)]
                            lo_part()
                            chunk()
                            dve.tensor_tensor(GE[j][:, 2:SEQ + 2], banks[2 * j][:], RSTD[:], ALU.mult).then_inc(sems["evicted"], t.one("evicted"))
                            dve.wait_ge(sems["evicted"], t.at("evicted", CREDITS["evicted"]))
                            dve.tensor_scalar(CO[j][:], GE[j][:, 0:SEQ], conv(0), conv(3), ALU.mult, ALU.add).then_inc(sems["dve_step"], t.one("dve_step"))
                            dve.wait_ge(sems["dve_step"], t.at("dve_step"))
                            dve.scalar_tensor_tensor(CO[j][:], GE[j][:, 1:SEQ + 1], conv(1), CO[j][:], ALU.mult, ALU.add).then_inc(sems["dve_step"], t.one("dve_step"))
                            dve.wait_ge(sems["dve_step"], t.at("dve_step"))
                            dve.scalar_tensor_tensor(CO[j][:], GE[j][:, 2:SEQ + 2], conv(2), CO[j][:], ALU.mult, ALU.add).then_inc(sems["gate_in"], t.one("gate_in"))
                            lo_part()
                            chunk()
                            dve.tensor_tensor(TA[:], banks[2 * j + 1][:], RSTD[:], ALU.mult).then_inc(sems["evicted"], t.one("evicted"))
                            dve.wait_ge(sems["evicted"], t.at("evicted", CREDITS["evicted"]))
                            t.up("gate")
                            dve.wait_ge(sems["gate"], t.at("gate"))
                            dve.tensor_tensor(TA[:], TA[:], GL[j][:], ALU.mult).then_inc(sems["dve_step"], t.one("dve_step"))
                            dve.wait_ge(sems["dve_step"], t.at("dve_step"))
                            n = bass.ds(2 * it + j, 1)
                            split(FHI[:, n, :].rearrange("p o n -> p (o n)"), FLO[:, n, :].rearrange("p o n -> p (o n)"), TA[:])
                    t.turns(FT // 2, body)

                def retention(self):
                    t.up("stage_loads", 48)
                    dve.wait_ge(sems["stage_loads"], t.at("stage_loads"))

                    def body(h):
                        for dst, b in ((RQ, 0), (RK, 2)):
                            for a in range(2):
                                lo_part()
                                chunk()
                                dve.tensor_tensor((TA, TB)[a][:], banks[b + a][:], RSTD[:], ALU.mult).then_inc(sems["evicted"], t.one("evicted"))
                                dve.wait_ge(sems["evicted"], t.at("evicted", CREDITS["evicted"]))
                            dve.tensor_tensor(dst[:, 0, :], TA[:], RC[:], ALU.mult).then_inc(sems["dve_step"], t.one("dve_step"))
                            dve.wait_ge(sems["dve_step"], t.at("dve_step"))
                            dve.tensor_tensor(TC[:], TB[:], RS[:], ALU.mult).then_inc(sems["dve_step"], t.one("dve_step"))
                            dve.wait_ge(sems["dve_step"], t.at("dve_step"))
                            dve.tensor_tensor(dst[:, 0, :], dst[:, 0, :], TC[:], ALU.subtract).then_inc(sems["rotated"], t.one("rotated"))
                            dve.wait_ge(sems["rotated"], t.at("rotated"))
                            dve.tensor_tensor(dst[:, 1, :], TB[:], RC[:], ALU.mult).then_inc(sems["dve_step"], t.one("dve_step"))
                            dve.wait_ge(sems["dve_step"], t.at("dve_step"))
                            dve.tensor_tensor(TC[:], TA[:], RS[:], ALU.mult).then_inc(sems["dve_step"], t.one("dve_step"))
                            dve.wait_ge(sems["dve_step"], t.at("dve_step"))
                            dve.tensor_tensor(dst[:, 1, :], dst[:, 1, :], TC[:], ALU.add).then_inc(sems["rotated"], t.one("rotated"))
                            dve.wait_ge(sems["rotated"], t.at("rotated"))
                        for j in range(4):
                            lo_part()
                            chunk()
                            t.up("v_turned")
                            if j:
                                dve.wait_ge(sems["v_turned"], t.at("v_turned", -1))
                            dve.tensor_tensor(RVF2[:], banks[j][:], RSTD[:], ALU.mult).then_inc(sems["evicted"], t.one("evicted"))
                        for kt in range(QT):
                            t.up("s_ready")
                            dve.wait_ge(sems["s_ready"], t.at("s_ready"))
                            n = SEQ - kt * P
                            dec = RD[:, bass.ds(h, 1), 0:n].rearrange("p o n -> p (o n)")
                            dve.tensor_tensor(RP[:, kt, kt * P:SEQ], banks[S0 + kt % 2][:, 0:n], dec, ALU.mult).then_inc(sems["operand"], t.one("operand"))
                        for j in range(4):
                            lo_part()
                        t.up("small", 5)
                        dve.wait_ge(sems["small"], t.at("small"))
                        dve.tensor_scalar(VAR[:], banks[S0][:], 1.0 / RET_V, None, ALU.mult).then_inc(sems["dve_step"], t.one("dve_step"))
                        dve.wait_ge(sems["dve_step"], t.at("dve_step"))
                        for e in range(4):
                            dve.tensor_tensor(RY[:, e, :], RY[:, e, :], VAR[:], ALU.subtract).then_inc(sems["centred"], t.one("centred"))
                            dve.wait_ge(sems["centred"], t.at("centred"))
                        rstd(S0 + 1, RET_V, RSTD2)
                        for e in range(4):
                            T_ = (TA, TB)[e % 2]
                            chunk()
                            dve.tensor_tensor(T_[:], banks[e][:], RSTD[:], ALU.mult).then_inc(sems["evicted"], t.one("evicted"))
                            dve.wait_ge(sems["evicted"], t.at("evicted", CREDITS["evicted"]))
                            signal("gate_in")
                            gn = G[:, bass.ds(GAINS["gn"] + 4 * h + e, 1)]
                            dve.scalar_tensor_tensor(TC[:], RY[:, e, :], gn, RSTD2[:], ALU.mult, ALU.mult).then_inc(sems["dve_step"], t.one("dve_step"))
                            dve.wait_ge(sems["dve_step"], t.at("dve_step"))
                            t.up("gate")
                            dve.wait_ge(sems["gate"], t.at("gate"))
                            dve.tensor_tensor(TC[:], TC[:], T_[:], ALU.mult).then_inc(sems["dve_step"], t.one("dve_step"))
                            dve.wait_ge(sems["dve_step"], t.at("dve_step"))
                            n = bass.ds(4 * h + e, 1)
                            split(RH[:, n, :].rearrange("p o n -> p (o n)"), RL[:, n, :].rearrange("p o n -> p (o n)"), TC[:])
                    t.turns(RET_HEADS, body)

                def dilated(self):
                    t.up("stage_loads", 96)
                    dve.wait_ge(sems["stage_loads"], t.at("stage_loads"))

                    def evict(par, x):
                        chunk()
                        g, bank = x // 3, banks[dil_bank(par, x)]
                        if x % 3 == 0:
                            dve.scalar_tensor_tensor(TA[:], bank[:], float(HEAD ** -0.5), RSTD[:], ALU.mult, ALU.mult).then_inc(sems["evicted"], t.one("evicted"))
                        else:
                            dve.tensor_tensor((TB if x % 3 == 1 else DF)[:], bank[:], RSTD[:], ALU.mult).then_inc(sems["evicted"], t.one("evicted"))
                        dve.wait_ge(sems["evicted"], t.at("evicted", CREDITS["evicted"]))
                        if x % 3 < 2:
                            signal("operand")
                            dst, T_ = ((DQ, TA), (DK, TB))[x % 3]
                            dve.tensor_tensor(dst[par][:, g, :], T_[:], DC[:], ALU.mult).then_inc(sems["dve_step"], t.one("dve_step"))

                    def rotate(par, x):
                        dst = ((DQ, DK)[x % 3])[par][:, x // 3, :]
                        t.up("swapped")
                        dve.wait_ge(sems["swapped"], t.at("swapped"))
                        dve.tensor_tensor(TC[:], banks[DAUX][:], DS[:], ALU.mult).then_inc(sems["dve_step"], t.one("dve_step"))
                        dve.wait_ge(sems["dve_step"], t.at("dve_step"))
                        dve.tensor_tensor(dst, dst, TC[:], ALU.add).then_inc(sems["rotated"], t.one("rotated"))

                    def u1(u):
                        i, m = UNITS[u]
                        t.up("s_ready")
                        dve.wait_ge(sems["s_ready"], t.at("s_ready"))
                        if u >= 2:
                            t.up("turned", 3)
                            dve.wait_ge(sems["turned"], t.at("turned", CREDITS["turned"]))
                        at_ = 0
                        for g in range(3):
                            w = key_blocks("sw" if g == 0 else "da", i)[1] * P
                            full = 2 * P if g == 0 else SEQ
                            passed()
                            dve.tensor_tensor_reduce(DP[u % 2][:, at_:at_ + w], banks[DSCORES[g]][:, 0:w],
                                    DM[g][:, full - w:full], 1.0, LOWEST, ALU.add, ALU.max, sm((MX, RC1, ES)[g] + u)).then_inc(sems["dve_step"], t.one("dve_step"))
                            dve.wait_ge(sems["dve_step"], t.at("dve_step"))
                            at_ += w
                        dve.tensor_tensor(sm(MX + u), sm(MX + u), sm(RC1 + u), ALU.max).then_inc(sems["dve_step"], t.one("dve_step"))
                        dve.wait_ge(sems["dve_step"], t.at("dve_step"))
                        dve.tensor_tensor(sm(MX + u), sm(MX + u), sm(ES + u), ALU.max).then_inc(sems["dve_step"], t.one("dve_step"))
                        dve.wait_ge(sems["dve_step"], t.at("dve_step"))
                        dve.tensor_scalar(sm(NM + u), sm(MX + u), -1.0, None, ALU.mult).then_inc(sems["scored"], t.one("scored"))

                    def u2(u):
                        w = dil_width(UNITS[u][0])
                        t.up("exped")
                        dve.wait_ge(sems["exped"], t.at("exped"))
                        dve.reciprocal(sm(RC1 + u), sm(DEN + u)).then_inc(sems["dve_step"], t.one("dve_step"))
                        dve.wait_ge(sems["dve_step"], t.at("dve_step"))
                        dve.tensor_scalar(DP[u % 2][:, 0:w], DP[u % 2][:, 0:w], sm(RC1 + u), None, ALU.mult).then_inc(sems["probs"], t.one("probs"))

                    def pair(par, more, it):
                        nxt = 1 - par
                        for u in range(len(UNITS)):
                            if u + 1 < len(UNITS):
                                u1(u + 1)
                            if more:
                                lo_part()
                                if u == 0:
                                    evict(nxt, 0)
                                    lo_part()
                                if u % 3 < 2:
                                    rotate(nxt, u)
                            if u + 1 < len(UNITS):
                                u2(u + 1)
                            if more:
                                evict(nxt, u + 1)
                        t.up("turned", 6)
                        t.up("pv_done", len(UNITS))
                        dve.wait_ge(sems["pv_done"], t.at("pv_done", CREDITS["pv_done"]))
                        z = bass.ds(2 * it + par, 1)
                        dve.tensor_scalar(DO[:, z, :].rearrange("p o n -> p (o n)"), banks[OUTB][:], 1.0, None, ALU.mult).then_inc(sems["o_used"], t.one("o_used"))
                        if more:
                            u1(0)
                            u2(0)

                    for x in range(9):
                        lo_part()
                        evict(0, x)
                        if x % 3 < 2:
                            rotate(0, x)
                    u1(0)
                    u2(0)

                    def body(it):
                        pair(0, True, it)
                        pair(1, not isinstance(it, int) or it < KT // 2 - 1, it)
                    t.turns(KT // 2, body)

            e = Programs()
            e.t = t
            run(e)


def tiles(w, columns):
    columns = np.asarray(columns)
    part = w[:, np.maximum(columns, 0)]
    if (columns < 0).any():
        part = part.copy()
        part[:, columns < 0] = 0
    return part.reshape(-1, P, P).transpose(1, 0, 2)


def plain(w, at=0, n=None):
    n = (w.shape[1] - at) // P if n is None else n
    return [tiles(w, np.arange(at + j * P, at + (j + 1) * P)) for j in range(n)]


def chunks(parts, width):
    a = np.concatenate(parts, 1)
    return np.ascontiguousarray(a.reshape(P, -1, width * P).transpose(1, 0, 2))


def interleave(*lists):
    return [x for group in zip(*lists) for x in group]


def per_partition(v):
    return v.reshape(-1, P).T


def lay_out(a):
    names, w = {}, {}
    in_sizes = (512, 512, 512, 512, 256, 128, ROPE, 512, 512, 128, 128, 512, 3072)
    o = dict(zip(("aq", "ak", "av", "az", "bq", "bkv", "bkr", "bz", "cq", "ck", "cv", "cz", "g"),
                 np.cumsum((0,) + in_sizes[:-1])))
    sw_cols = [np.concatenate([np.arange(HEAD) + HEAD * h for h in (n, 4 + n)]) for n in range(4)]
    rope, swap, gap = np.arange(ROPE), np.roll(np.arange(ROPE), HALF), np.full(ROPE, -1)
    for l in range(DEPTH):
        wi = a["w_in"][l]
        kr = [tiles(wi, np.concatenate([o["bkr"] + r, gap, o["bkr"] + r, gap])) for r in (rope, swap)]
        w[f"lat{l}"] = chunks(plain(wi, o["bq"], 3) + kr + plain(wi, o["ck"], 2), 8)
        w[f"da{l}"] = chunks(interleave(*(plain(wi, o[n], 4) for n in ("aq", "ak", "av", "az"))), 8)
        parts = []
        qb, kvb = a["mla_w_qb"][l], a["mla_w_kvb"][l]
        bz = plain(wi, o["bz"], 4)
        for n in range(4):
            h = (2 * n, 2 * n + 1)
            parts += [bz[n], tiles(kvb, np.concatenate([P * x + HEAD + np.arange(HEAD) for x in h])),
                      tiles(qb, np.concatenate([96 * x + np.arange(HEAD) for x in h])),
                      tiles(qb, np.concatenate([y for x in h for y in (96 * x + HEAD + rope, gap)])),
                      tiles(qb, np.concatenate([y for x in h for y in (96 * x + HEAD + swap, gap)])),
                      tiles(kvb, np.concatenate([P * x + np.arange(HEAD) for x in h]))]
        w[f"mla{l}"] = chunks(parts, 8)
        w[f"sw{l}"] = chunks([tiles(wi, o[s] + c) for c in sw_cols for s in ("cq", "cz")], 8)
        g = [plain(wi, o["g"] + D * b, KT) for b in range(3)]
        rows = np.concatenate(sw_cols)
        br = [plain(x, 0, KT) for x in (a["w_br_a"][l], a["w_br_b"][l], a["w_br_c"][l][rows])]
        w[f"gate{l}"] = chunks(interleave(g[0], br[0], g[1], br[1], g[2], br[2]), 12)
        w[f"wout{l}"] = chunks(plain(a["w_out"][l]), 8)
        w[f"ple{l}"] = chunks(interleave(plain(a["w_ple_gate"][l]), plain(a["w_ple_proj"][l])), 10)
    ri = a["ret_w_in_2"][0]
    parts = []
    for h in range(RET_HEADS):
        parts += plain(ri, 256 * h, 2) + plain(ri, D + 256 * h, 2) + plain(ri, 2 * D + RET_V * h, 4)
        parts += plain(ri, 4 * D + RET_V * h, 4)
    w["ret"] = chunks(parts, 8)
    w["retout"] = chunks(plain(a["ret_w_out_2"][0]), 8)
    kv, q = a["att_w_kv_2"], a["att_w_q_2"][0]
    parts = []
    for n in range(KT):
        for g in range(3):
            parts += plain(q, D * g + P * n, 1) + plain(kv, D * g + P * n, 1) + plain(kv, 3 * D + D * g + P * n, 1)
    w["dil"] = chunks(parts, 8)
    w["wo"] = chunks(plain(a["att_w_o_2"][0]), 8)
    for l in range(DEPTH):
        up = a["ffn_w_up_2"][l]
        w[f"up{l}"] = chunks(interleave(plain(up, 0, FT), plain(up, DFF, FT)), 8)
        w[f"down{l}"] = chunks(plain(a["ffn_w_down_2"][l]), FH)
    for n, k, width in STREAM:
        assert w[n].shape == (k, P, width * P), (n, w[n].shape)
        names["w_" + n] = w[n]
    gains = []
    for n in GAINS:
        stem, l = n.rstrip("01"), int(n[-1]) if n[-1] in "01" else 0
        if stem == "conv":
            gains += [per_partition(a["ffn_conv_w_2"][l, c]) for c in range(3)] + [per_partition(a["ffn_conv_b_2"][l])]
        else:
            src = {"pre": "norm_pre", "post": "norm_post", "mixpre": "norm_mix_pre_2", "mixpost": "norm_mix_post_2",
                   "ffnpre": "norm_ffn_pre_2", "ffnpost": "norm_ffn_post_2", "kv": "kv_norm_2", "mlaq": "mla_q_norm",
                   "mlakv": "mla_kv_norm", "subln": "da_subln", "gn": "ret_gn_gain_2"}[stem]
            gains.append(per_partition(a[src] if stem == "kv" else a[src][l]))
    names["gains"] = np.ascontiguousarray(np.concatenate(gains, 1))
    names["x_t"] = np.ascontiguousarray(a["x"][0].T.reshape(KT, P, SEQ).transpose(1, 0, 2))
    names["p_t"] = np.ascontiguousarray(a["p"][:, 0].transpose(0, 2, 1).reshape(DEPTH, 2, P, SEQ).transpose(0, 2, 1, 3))
    names["positions"] = np.ascontiguousarray(a["positions"])
    names["rel_bias"] = np.ascontiguousarray(a["rel_bias"])
    names["da_lambda"] = np.ascontiguousarray(a["da_lambda"].reshape(1, -1))
    names["sw_sinks"] = np.ascontiguousarray(a["sw_sinks"])
    names.update(constants())
    return names


def kernel(**inputs):
    import concourse.bacc as _bacc
    from concourse.bass_utils import run_bass_kernel_spmd as _run

    nc = _bacc.Bacc("TRN2", target_bir_lowering=False, num_devices=1)
    arrays, aps = {}, {}
    for name, value in lay_out({k: np.asarray(v) for k, v in inputs.items()}).items():
        arrays[f"in_{name}"] = value
        aps[name] = nc.dram_tensor(f"in_{name}", value.shape, mybir.dt.from_np(value.dtype), kind="ExternalInput").ap()
    out = nc.dram_tensor("out_x", (P, KT, SEQ), F32, kind="ExternalOutput").ap()
    two_stacks_kernel(nc, aps, out)
    r = _run(nc, [arrays], core_ids=[0])
    got = r.results[0]["out_x"]
    return np.ascontiguousarray(got.transpose(1, 0, 2).reshape(1, D, SEQ).transpose(0, 2, 1))
```

```python
import math
from contextlib import ExitStack, contextmanager

import numpy as np

import concourse.bass as bass
from concourse import mybir

F32 = mybir.dt.float32
F32R = mybir.dt.float32r
I32 = mybir.dt.int32
ALU = mybir.AluOpType
ACT = mybir.ActivationFunctionType

P = 128
SEQ = 512
QT = SEQ // P
D = 1024
KT = D // P
DEPTH = 2
HEAD = 64
ROPE = 32
HALF = ROPE // 2
DFF = 2816
FT = DFF // P
FH = FT // 2
RET_HEADS = 4
RET_V = 512
EPS = 1e-6
NEG = -1e30
LOWEST = -3.0e38
RING = 2
SLOT = 12
LBANKS = 4
VBANK = 2
S0, TURN, OUTB = 4, 6, 7
BUCKETS, BHEADS = 32, 12
RV = 640
TWO_PI_A = 6.28125
TWO_PI_B = float(np.float32(2 * math.pi - 6.28125))
TWO_PI_C = float(np.float32(2 * math.pi - 6.28125 - TWO_PI_B))
MAGIC = 12582912.0
LAM_INIT = [0.8 - 0.6 * math.exp(-0.3 * l) for l in range(DEPTH)]

GAINS = {}
_at = 0
for _name, _n in (("pre0", KT), ("pre1", KT), ("post0", KT), ("post1", KT), ("mixpre0", KT), ("mixpre1", KT),
                  ("mixpost0", KT), ("mixpost1", KT), ("ffnpre0", KT), ("ffnpre1", KT), ("ffnpost0", KT),
                  ("ffnpost1", KT), ("kv", KT), ("mlaq0", 2), ("mlaq1", 2), ("mlakv0", 1), ("mlakv1", 1),
                  ("subln0", 1), ("subln1", 1), ("gn", 16), ("conv0", 4 * FT), ("conv1", 4 * FT)):
    GAINS[_name] = _at
    _at += _n
NGAIN = _at

STREAM = []
for _l in range(DEPTH):
    STREAM += [(f"lat{_l}", 7, 8), (f"da{_l}", 16, 8), (f"mla{_l}", 8, 8), (f"sw{_l}", 8, 8),
               (f"gate{_l}", 24, 12), (f"wout{_l}", 8, 8), (f"ple{_l}", 8, 10)]
STREAM += [("ret", 48, 8), ("retout", 16, 8), ("up0", 44, 8), ("down0", 16, FH),
           ("dil", 72, 8), ("wo", 8, 8), ("up1", 44, 8), ("down1", 16, FH)]
WIDTH = [w for _, n, w in STREAM for _ in range(n)]

SEMAPHORES = (
    "loaded", "x_loaded", "scratch", "spread", "biased", "raw0", "raw1",
    "hi_done", "lo_done", "chunk_done",
    "dve_step", "act_step",
    "evicted", "part_done",
    "squared", "m_squared", "summed", "var_ready", "std_ready",
    "operand",
    "operand_hi", "m_ready", "x_ready",
    "made",
    "s_ready", "scored", "exped", "probs", "turned", "pt_copied", "pv_done", "o_used", "sum_used",
    "v_turned", "v_token", "z_ready", "gate_in", "gate", "swapped", "rotated", "y_copied", "centred",
    "small",
    "stage_pe", "stage_act", "stage_dve",
    "stage_loads", "stored", "waits_passed",
)
CREDITS = {"chunk_done": RING, "lo_done": RING, "evicted": LBANKS, "scored": 2, "turned": 4,
           "pt_copied": 1, "pv_done": 2, "o_used": 1, "sum_used": 1}
ALIASES = {"slot_free": "chunk_done", "raw_free": "lo_done"}


STAGES = ["setup"]
for _l in range(DEPTH):
    STAGES += [f"{_s}{_l}" for _s in ("mix", "ple")]
STAGES += ["ret", "ffn0", "dil", "ffn1", "end"]
N_STAGES = len(STAGES)
STAGE = {n: i for i, n in enumerate(STAGES)}


class Tally:

    def __init__(self, eng):
        self.eng = eng
        self.base, self.k = {}, {}
        self.extra = {}
        self.c = 0

    def up(self, name, n=1):
        self.k[name] = self.k.get(name, 0) + n

    def add(self, name, n):
        self.up(name, n)
        return n

    def one(self, name):
        return self.add(name, 1)

    def at(self, name, plus=0):
        value = self.base.get(name, 0) + self.k.get(name, 0) + plus
        assert not isinstance(value, int) or value > 0, (name, value)
        return value

    def once(self, i, f):
        if isinstance(i, int) and i == 0:
            before = dict(self.k)
            f()
            for s, v in self.k.items():
                self.extra[s] = self.extra.get(s, 0) + v - before.get(s, 0)

    def turns(self, n, body):
        before, c0 = dict(self.k), self.c
        self.extra = {}
        body(0)
        for s, v in self.extra.items():
            before[s] = before.get(s, 0) + v
        per = {s: v - before.get(s, 0) for s, v in self.k.items()}
        per_c = self.c - c0
        assert n == 1 or per_c % RING == 0
        if n > 2:
            outer = dict(self.base)
            for s in per:
                self.k[s] = 0
            with self.eng.Fori(1, n - 1) as i:
                for s, v in per.items():
                    self.base[s] = outer.get(s, 0) + before.get(s, 0) + i * v if v else outer.get(s, 0) + before.get(s, 0)
                body(i)
            for s, v in per.items():
                assert self.k[s] == v, (s, self.k[s], v)
                self.base[s] = outer.get(s, 0)
                self.k[s] = before.get(s, 0) + (n - 1) * v
            self.c = c0 + (n - 1) * per_c
        if n > 1:
            body(n - 1)


def rel_window(n):
    return n - 1 - np.arange(RV)


def constants():
    f = np.float32
    c = {}
    rel = rel_window(SEQ)
    n = np.maximum(rel, 0)
    large = 16 + (np.log(np.maximum(n, 1).astype(f) / f(16)) / f(math.log(8.0)) * f(16)).astype(np.int32)
    bucket = np.where(n < 16, n, np.minimum(large, BUCKETS - 1))
    for name, valid in (("oh_full", rel >= 0), ("oh_window", (rel >= 0) & (rel < 128))):
        oh = np.zeros((BUCKETS + 1, RV), f)
        oh[bucket[valid], np.nonzero(valid)[0]] = 1.0
        oh[BUCKETS, ~valid] = NEG
        c[name] = oh
    q, k = np.arange(P)[:, None], np.arange(SEQ)[None, :]
    rel = SEQ - P + q - k
    c["masks"] = np.stack([np.where(ok, f(0), f(NEG)) for ok in (
        rel >= 0, (rel >= 0) & (rel <= 128), (rel >= 0) & (rel % 4 == 0), (rel >= 0) & (rel % 16 == 0))], 1)
    p = np.arange(P)
    inv = (10000.0 ** (-np.arange(HALF, dtype=np.float64) / HALF)).astype(f)
    sign = np.where(p % ROPE < HALF, -1.0, 1.0)
    c["columns"] = np.stack([inv[p % HALF], sign], 1).astype(f)
    c["ident"] = np.eye(P, dtype=f)
    pos = np.arange(SEQ, dtype=f)[None, :]
    ret = (1.0 / (10000.0 ** np.linspace(0.0, 1.0, P, dtype=np.float64))).astype(f)
    ang = (pos * ret[:, None]).astype(np.float64)
    c["ret_angles"] = np.stack([np.cos(ang), np.sin(ang)], 1).astype(f)
    gamma = 1.0 - 2.0 ** (-5.0 - np.arange(RET_HEADS))
    diff = np.arange(SEQ)[None, :] - p[:, None]
    c["decay"] = np.stack([np.where(diff >= 0, g ** np.maximum(diff, 0), 0.0) / 16.0 for g in gamma]).astype(f)
    inv2 = (500000.0 ** (-np.arange(0, 16, 2, dtype=np.float64) / 16)).astype(f)
    r = p % HEAD
    ang = (pos * inv2[r % 8][:, None]).astype(np.float64)
    rot = (r < 16)[:, None]
    c["dil_angles"] = np.stack([np.where(rot, np.cos(ang), 1.0),
                                np.where(rot, np.sin(ang) * np.where(r < 8, -1.0, 1.0)[:, None], 0.0)], 1).astype(f)
    perm = np.zeros((P, P), f)
    for m in range(P):
        if m % HEAD < 16:
            perm[m + 8 if m % HEAD < 8 else m - 8, m] = 1.0
    c["perm"] = perm
    return {k: np.ascontiguousarray(v.astype(f)) for k, v in c.items()}


CONSTANTS = ("oh_full", "oh_window", "masks", "columns", "ident", "ret_angles", "decay", "dil_angles", "perm")


def two_stacks_kernel(nc, d, out):
    scratch = nc.dram_tensor("bias_vectors", (2, BHEADS, RV), F32, kind="Internal").ap()
    copies = nc.dram_tensor("bias_copies", (BHEADS, P, RV), F32, kind="Internal").ap()
    with ExitStack() as ctx:
        sems = {n: ctx.enter_context(nc.semaphore(n)) for n in SEMAPHORES}
        sems |= {a: sems[n] for a, n in ALIASES.items()}

        def sb(name, shape, dt=F32):
            return ctx.enter_context(nc.sbuf_tensor(name, shape, dt))

        X = sb("x_res", [P, KT, SEQ])
        HH = sb("h_hi", [P, KT, SEQ], F32R)
        HL = sb("h_lo", [P, KT, SEQ], F32R)
        RAW = [sb(f"w_raw{s}", [P, SLOT * P]) for s in range(RING)]
        WH = [sb(f"w_hi{s}", [P, SLOT * P], F32R) for s in range(RING)]
        WL = [sb(f"w_lo{s}", [P, SLOT * P], F32R) for s in range(RING)]
        G = sb("gains", [P, NGAIN])
        COLS = sb("columns", [P, 2])
        ID = sb("ident", [P, P])
        ONES = sb("ones", [P, P])
        RSTD = sb("rstd", [P, SEQ])
        RSTD2 = sb("rstd2", [P, SEQ])
        VAR = sb("var", [P, SEQ])
        TA = sb("ta", [P, SEQ])
        TB = sb("tb", [P, SEQ])
        TC = sb("tc", [P, SEQ])
        SM = sb("small_columns", [P, 64])
        arena_bytes = 54 * SEQ * 4
        base = -(-nc.sbuf_base // 32) * 32
        sb("arena", [P, arena_bytes // 4])

        def at(name, shape, offset, dt=F32):
            size = int(np.prod(shape[1:])) * 4
            assert offset + size <= arena_bytes, (name, offset + size, arena_bytes)
            return nc.alloc_sbuf_tensor_at(name, shape, dt, offset=base + offset)

        T1 = SEQ * 4
        ZH = at("zo_hi", [P, 12, SEQ], 0, F32R)
        ZL = at("zo_lo", [P, 12, SEQ], 12 * T1, F32R)
        M1 = at("m1", [P, KT, SEQ], 0)
        SQ1 = at("sq1", [P, KT, SEQ], KT * T1)
        o = 24 * T1
        YH = at("y_hi", [P, KT, SEQ], o, F32R)
        YL = at("y_lo", [P, KT, SEQ], o + KT * T1, F32R)
        PX = at("ple_raw", [P, 2, SEQ], o)
        PH = at("ple_hi", [P, 2, SEQ], o + 2 * T1, F32R)
        PL = at("ple_lo", [P, 2, SEQ], o + 4 * T1, F32R)
        QNH = at("qn_hi", [P, 2, SEQ], o, F32R)
        QNL = at("qn_lo", [P, 2, SEQ], o + 2 * T1, F32R)
        KNH = at("kvn_hi", [P, 1, SEQ], o + 4 * T1, F32R)
        KNL = at("kvn_lo", [P, 1, SEQ], o + 5 * T1, F32R)
        KR = at("k_rope", [P, SEQ], o + 6 * T1)
        CK = at("c_k", [P, SEQ], o + 7 * T1)
        CV = at("c_v", [P, QT, P], o + 8 * T1)
        LQ = at("lat_q", [P, 3, SEQ], o + 9 * T1)
        AQ = at("att_q", [P, SEQ], o + 9 * T1)
        AK = at("att_k", [P, SEQ], o + 10 * T1)
        AR = at("att_qr", [P, SEQ], o + 11 * T1)
        BT = AR
        NZ = VAR
        VF = RSTD2
        VT = at("att_vt", [P, QT, P], o + 12 * T1)
        SS = [at(f"probs{n}", [P, SEQ], o + (13 + n) * T1) for n in range(4)]
        PT = [at(f"pt{n}", [P, SEQ], o + (17 + n) * T1) for n in range(2)]
        COS = at("cos", [P, SEQ], o + 19 * T1)
        SIN = at("sin", [P, SEQ], o + 20 * T1)
        MASK = at("mask", [P, SEQ], o + 21 * T1)
        BDA = at("bias_da", [P, 4, SEQ], o + 22 * T1)
        BSW = at("bias_sw", [P, 4, SEQ], o + 26 * T1)
        POSI = at("pos_i", [P, SEQ], 0, I32)
        ANG = at("ang", [P, SEQ], T1)
        OHF = at("oh_full_sb", [BUCKETS + 1, RV], 2 * T1)
        OHW = at("oh_window_sb", [BUCKETS + 1, RV], 4 * T1)
        TAB = at("table", [BUCKETS + 1, BHEADS], 6 * T1)
        RVF = at("rv_full", [BHEADS, RV], 7 * T1)
        RVW = at("rv_window", [BHEADS, RV], 9 * T1)
        LAM = at("lam_in", [P, DEPTH, 4, HEAD], 11 * T1)
        RH = at("ret_hi", [P, 16, SEQ], 0, F32R)
        RL = at("ret_lo", [P, 16, SEQ], 16 * T1, F32R)
        RQ = at("ret_q", [P, 2, SEQ], 32 * T1)
        RK = at("ret_k", [P, 2, SEQ], 34 * T1)
        RY = at("ret_y", [P, QT, SEQ], 32 * T1)
        RVT = at("ret_vt", [P, QT, RET_V], 36 * T1)
        RSQ = at("ret_sq", [P, QT, SEQ], 36 * T1)
        RP = at("ret_p", [P, QT, SEQ], 40 * T1)
        RVF2 = at("ret_vf", [P, SEQ], 44 * T1)
        RC = at("ret_cos", [P, SEQ], 45 * T1)
        RS = at("ret_sin", [P, SEQ], 46 * T1)
        RD = at("ret_decay", [P, RET_HEADS, SEQ], 47 * T1)
        FHI = at("f_hi", [P, FT, SEQ], 0, F32R)
        FLO = at("f_lo", [P, FT, SEQ], FT * T1, F32R)
        M2 = at("m2", [P, KT, SEQ], 2 * FT * T1)
        SQ2 = at("sq2", [P, KT, SEQ], 0)
        GE = [at(f"conv_in{n}", [P, SEQ + 2], (2 * FT + 2 * n) * T1) for n in range(2)]
        CO = [at(f"conv_out{n}", [P, SEQ], (2 * FT + 4 + n) * T1) for n in range(2)]
        GL = [at(f"gelu{n}", [P, SEQ], (2 * FT + 6 + n) * T1) for n in range(2)]
        DO = at("dil_out", [P, KT, SEQ], 0)
        H2H = at("h2_hi", [P, KT, SEQ], 8 * T1, F32R)
        H2L = at("h2_lo", [P, KT, SEQ], 16 * T1, F32R)
        DQ = [at(f"dil_q{n}", [P, 3, SEQ], (24 + 9 * n) * T1) for n in range(2)]
        DK = [at(f"dil_k{n}", [P, 3, SEQ], (27 + 9 * n) * T1) for n in range(2)]
        DVT = [at(f"dil_vt{n}", [P, 3, QT, P], (30 + 9 * n) * T1) for n in range(2)]
        DP = [at(f"dil_p{n}", [P, 10 * P], 42 * T1 + n * 5 * P * 8) for n in range(2)]
        DPT = [at(f"dil_pt{n}", [P, SEQ], 47 * T1 + n * T1) for n in range(2)] + [VAR]
        DC = at("dil_cos", [P, SEQ], 49 * T1)
        DS = at("dil_sin", [P, SEQ], 50 * T1)
        DM = [at("dil_mask0", [P, 2 * P], 51 * T1), at("dil_mask1", [P, SEQ], 52 * T1),
              at("dil_mask2", [P, SEQ], 53 * T1)]
        SQD = at("dil_sq", [P, KT, SEQ], 33 * T1)
        PERM = at("perm_sb", [P, P], 51 * T1 + T1 // 2)
        DF = RSTD2

        MX, NM, DEN, ES, RC1, SINK, ST, NST, LAMC, SUBG = 0, 8, 16, 24, 32, 40, 48, 50, 56, 58

        def sm(c, n=1):
            return SM[:, c:c + n]

        def gain(name, k=0):
            c = GAINS[name] + k
            return G[:, c:c + 1]

        banks = [ctx.enter_context(nc.psum_tensor(f"bank{b}", [P, SEQ], F32)) for b in range(8)]
        block = ctx.enter_context(nc.Block())

        @block.sync
        def _(sp):
            t = Tally(sp)
            for dst, src in ((G[:], d["gains"]), (COLS[:], d["columns"]), (ID[:], d["ident"]),
                             (POSI[:], d["positions"].to_broadcast([P, SEQ])), (OHF[:], d["oh_full"]),
                             (OHW[:], d["oh_window"]), (TAB[0:BUCKETS, :], d["rel_bias"]),
                             (LAM[:].rearrange("p a b c -> p (a b c)"),
                              d["da_lambda"].to_broadcast([P, DEPTH * 4 * HEAD])),
                             (MASK[:], d["masks"][:, 0, :])):
                sp.dma_start(dst, src).then_inc(sems["loaded"], t.add("loaded", 16))

            def load(w, width, i):
                slot = t.c % RING
                t.up("raw_free")
                sp.wait_ge(sems["raw_free"], t.at("raw_free"))
                src = w[i] if isinstance(i, int) else w[bass.ds(i, 1), :, :].rearrange("o p n -> p (o n)")
                sp.dma_start(RAW[slot][:, 0:width * P], src).then_inc(sems[f"raw{slot}"], t.add(f"raw{slot}", 16))
                t.c += 1

            for name, n, width in STREAM:
                w = d["w_" + name]

                def pair(i):
                    load(w, width, 2 * i)
                    load(w, width, 2 * i + 1)
                t.turns(n // 2, pair)
                if n % 2:
                    load(w, width, n - 1)
            t.up("x_ready", 5 * KT)
            for k in range(KT):
                t.up("x_ready")
                sp.wait_ge(sems["x_ready"], t.at("x_ready"))
                sp.dma_start(out[:, k, :], X[:, k, :]).then_inc(sems["stored"], t.add("stored", 16))
            sp.wait_ge(sems["stored"], t.at("stored"))

        @block.gpsimd
        def _(pool):
            t = Tally(pool)

            def after(stage):
                pool.wait_ge(sems["stage_pe"], stage)
                pool.wait_ge(sems["stage_act"], stage)
                pool.wait_ge(sems["stage_dve"], stage)

            def fetch(dst, src):
                pool.dma_start(dst, src).then_inc(sems["stage_loads"], t.add("stage_loads", 16))

            t.up("scratch", 32)
            pool.wait_ge(sems["scratch"], t.at("scratch"))
            for h in range(BHEADS):
                pool.dma_start(copies[h], scratch[0 if h < 4 else 1, h:h + 1, :].to_broadcast([P, RV])).then_inc(sems["spread"], t.add("spread", 16))
            pool.wait_ge(sems["spread"], t.at("spread"))

            def window(h, start, n):
                return bass.AP(copies.tensor, h * P * RV + start, [[RV - 1, P], [1, n]])

            for h in range(4):
                pool.dma_start(BDA[:, h, :], window(h, P - 1, SEQ)).then_inc(sems["biased"], t.add("biased", 16))
            for h in range(8):
                pool.dma_start(BSW[:, h % 4, h // 4 * 2 * P:(h // 4 + 1) * 2 * P],
                        window(4 + h, SEQ // 2 + P - 1, 2 * P)).then_inc(sems["biased"], t.add("biased", 16))
            for l in range(DEPTH):
                after(STAGE[f"mix{l}"])
                for h in range(8):
                    fetch(sm(SINK + 2 * (h % 4) + h // 4), d["sw_sinks"][l:l + 1, h:h + 1].to_broadcast([P, 1]))
                after(STAGE[f"ple{l}"])
                fetch(PX[:], d["p_t"][l])
            after(STAGE["ret"])
            fetch(RC[:], d["ret_angles"][:, 0, :])
            fetch(RS[:], d["ret_angles"][:, 1, :])
            fetch(RD[:], d["decay"].rearrange("h p n -> p h n"))
            after(STAGE["dil"])
            pool.wait_ge(sems["x_ready"], 4 * KT)
            fetch(DC[:], d["dil_angles"][:, 0, :])
            fetch(DS[:], d["dil_angles"][:, 1, :])
            fetch(DM[0][:], d["masks"][:, 1, SEQ - 2 * P:SEQ])
            fetch(DM[1][:], d["masks"][:, 2, :])
            fetch(DM[2][:], d["masks"][:, 3, :])
            fetch(PERM[:], d["perm"])

        def mix(e, l):
            e.latents(l)
            for kind in ("da", "mla", "sw"):
                e.attention(kind, l)
            e.gates(l)
            e.linear(1, YH, YL, M1, f"post{l}")

        def retention(e):
            e.retention()
            e.linear(2, RH, RL, M2, "mixpost0")

        def dilated(e):
            e.dilated()
            e.linear(1, H2H, H2L, M2, "mixpost1", DO)

        def ffn(e, l):
            e.ffn_up(l)
            e.linear(2, FHI, FLO, M2, f"ffnpost{l}")

        def run(e):
            def stage(name, f, *args):
                assert STAGES[e.stage] == name
                e.stage += 1
                if e.stage > 1:
                    e.begin_stage()
                f(*args)
                e.end()
                for s in ("stage_pe", "stage_act", "stage_dve"):
                    if s != e.mine:
                        e.t.up(s)

            stage("setup", e.setup)
            for l in range(DEPTH):
                stage(f"mix{l}", mix, e, l)
                stage(f"ple{l}", e.ple, l)
            stage("ret", retention, e)
            stage("ffn0", ffn, e, 0)
            stage("dil", dilated, e)
            stage("ffn1", ffn, e, 1)
            stage("end", e.postnorm, M2)

        def key_blocks(kind, i):
            n = min(i + 1, 2) if kind == "sw" else i + 1
            return i + 1 - n, n

        DAUX, DSCORES = 2, (3, 4, 5)

        def dil_bank(par, x):
            return (par + x) % 2

        def dil_width(i):
            return (key_blocks("sw", i)[1] + 2 * (i + 1)) * P

        UNITS = [(i, m) for i in range(QT) for m in range(2)]

        MLA_TILES = ((1, 0, 1, 2), (2, 0, 2, 3), (2, 1, 2, 3), (3, 0, 2, 4), (3, 1, 2, 4), (0, 0, 2, 4), (0, 1, 2, 4),
                     (1, 0, 1, 4))

        @block.tensor
        def _(pe):
            t = Tally(pe)

            class Programs:
                mine, stage = "stage_pe", 0

                def begin_stage(self):
                    pe.wait_ge(sems["stage_pe"], t.at("stage_pe"))
                    pe.wait_ge(sems["stage_act"], t.at("stage_act"))
                    pe.wait_ge(sems["stage_dve"], t.at("stage_dve"))

                def end(self):
                    pe.drain().then_inc(sems["stage_pe"], t.one("stage_pe"))

                def setup(self):
                    for n, c in (("chunk_done", RING), ("turned", 4), ("pv_done", 2)):
                        pe.sem_inc(sems[n], c)
                    t.up("loaded", 144)
                    pe.wait_ge(sems["loaded"], t.at("loaded"))
                    t.up("operand")
                    pe.wait_ge(sems["operand"], t.at("operand"))
                    for n, oh in enumerate((OHF, OHW)):
                        for h in range(2):
                            ins = pe.matmul(banks[2 * n + h][0:BHEADS, 0:RV // 2], TAB[:], oh[:, h * RV // 2:(h + 1) * RV // 2],
                                            start=True, stop=True)
                    ins.then_inc(sems["small"], t.one("small"))
                    t.up("operand", 2)

                def products(self, bank, tile, width, hi, lo, k, start, stop):
                    slot = t.c % RING
                    w = slice(tile * P, (tile + 1) * P)
                    pe.matmul(banks[bank][:], WH[slot][:, w], hi[:, k, :], start=start, stop=False)
                    pe.matmul(banks[bank][:], WH[slot][:, w], lo[:, k, :], start=False, stop=False)
                    return pe.matmul(banks[bank][:], WL[slot][:, w], hi[:, k, :], start=False, stop=stop)

                def begin(self):
                    t.up("lo_done")
                    pe.wait_ge(sems["lo_done"], t.at("lo_done", CREDITS["lo_done"]))

                def finish(self, ins):
                    ins.then_inc(sems["chunk_done"], t.one("chunk_done"))
                    t.c += 1

                def bank_free(self, of=LBANKS):
                    t.up("evicted")
                    pe.wait_ge(sems["evicted"], t.at("evicted", LBANKS - of))

                def whole(self, bank, hi=HH, lo=HL, of=LBANKS, fresh=False):
                    self.bank_free(of)
                    self.begin()
                    for k in range(KT):
                        if fresh:
                            pe.wait_ge(sems["operand"], t.at("operand", k + 1 - KT))
                        ins = self.products(bank, k, 8, hi, lo, k, k == 0, k == KT - 1)
                    self.finish(ins)

                def some(self, bank, k, of):
                    if k == 0:
                        self.bank_free(of)
                        self.begin()
                    ins = self.products(bank, k, 8, HH, HL, k, k == 0, k == KT - 1)
                    if k == KT - 1:
                        self.finish(ins)

                def sums(self, bank, n, src, name="squared"):
                    for k in range(n):
                        t.up(name)
                        pe.wait_ge(sems[name], t.at(name))
                        ins = pe.matmul(banks[bank][:], ONES[:], src(k), start=(k == 0), stop=(k == n - 1))
                    ins.then_inc(sems["summed"], t.one("summed"))

                def prenorm(self, sq):
                    self.sums(OUTB, KT, lambda k: sq[:, k, :])

                def postnorm(self, m):
                    pe.matmul(banks[OUTB][:], ONES[:], TC[:], start=True, stop=True).then_inc(sems["summed"], t.one("summed"))

                def turn_v(self, src, bank=TURN):
                    for b in range(QT):
                        ins = pe.transpose(banks[bank][:, b * P:(b + 1) * P], src[:, b * P:(b + 1) * P], ID[:])
                    ins.then_inc(sems["v_turned"], t.one("v_turned"))

                def latents(self, l):
                    t.up("operand", KT)
                    for j in range(7):
                        self.whole(j % LBANKS, fresh=(j == 0))
                        if j == 0:
                            self.prenorm(SQ1)
                        elif j == 4:
                            self.sums(OUTB, 2, lambda k: SS[k][:])
                            self.sums(S0, 1, lambda k: SS[2][:])
                    pe.wait_ge(sems["evicted"], t.at("evicted", LBANKS))
                    self.turn_v(VF)
                    t.up("v_token")
                    t.up("operand")

                def attention(self, kind, l):
                    def s_unit(i, m):
                        kb, n = key_blocks(kind, i)
                        r = slice(64 * m, 64 * m + 64)
                        keys = CK if kind == "sw" else AK
                        t.up("scored")
                        pe.wait_ge(sems["scored"], t.at("scored"))
                        q = slice(i * P, (i + 1) * P)
                        kk = slice(kb * P, (kb + n) * P)
                        o_ = banks[S0 + m][:, 0:n * P]
                        ins = pe.matmul(o_, AQ[r, q], keys[r, kk], start=True, stop=(kind != "mla"))
                        if kind == "mla":
                            rr = slice(64 * m, 64 * m + ROPE)
                            ins = pe.matmul(o_, AR[rr, q], KR[rr, kk], start=False, stop=True)
                        ins.then_inc(sems["s_ready"], t.one("s_ready"))

                    def t_unit(u, i):
                        _, n = key_blocks(kind, i)
                        t.up("probs")
                        pe.wait_ge(sems["probs"], t.at("probs"))
                        t.up("pt_copied")
                        pe.wait_ge(sems["pt_copied"], t.at("pt_copied"))
                        for b in range(n):
                            ins = pe.transpose(banks[TURN][:, b * P:(b + 1) * P], SS[u % 4][:, b * P:(b + 1) * P], ID[:])
                        ins.then_inc(sems["turned"], t.one("turned"))

                    def pv_unit(n_unit, i, m, more=False):
                        kb, n = key_blocks(kind, i)
                        ahead = 1 if kind != "da" and (more or n_unit < len(UNITS) - 1) else 0
                        pe.wait_ge(sems["pt_copied"], t.at("pt_copied", CREDITS["pt_copied"] - ahead))
                        for b in range(n):
                            v = (CV if kind == "sw" else VT)[:, kb + b, :]
                            if kind != "da":
                                v = v[:, 64 * m:64 * m + 64]
                            r = slice(0, P) if kind == "da" else slice(64 * m, 64 * m + 64)
                            ins = pe.matmul(banks[OUTB][r, i * P:(i + 1) * P], v, PT[n_unit % 2][:, b * P:(b + 1) * P],
                                            start=(b == 0), stop=(b == n - 1))
                        ins.then_inc(sems["pv_done"], t.one("pv_done"))

                    def mla_tile(n):
                        bank, k, of_k, of = MLA_TILES[n]
                        hi, lo = (KNH, KNL) if of_k == 1 else (QNH, QNL)
                        if n == 0:
                            self.begin()
                        if k == 0:
                            self.bank_free(of)
                        ins = self.products(bank, n, 8, hi, lo, k, k == 0, k == of_k - 1)
                        if n == 7:
                            self.finish(ins)
                        elif k == of_k - 1:
                            ins.then_inc(sems["part_done"], t.one("part_done"))

                    def project(first, last):
                        for n in range(first, last):
                            if kind == "sw":
                                self.some(n // 8, n % 8, 2)
                            elif n < 8:
                                self.some(0, n, 1)
                            else:
                                mla_tile(n - 8)

                    def start():
                        if kind == "mla":
                            pe.wait_ge(sems["evicted"], t.at("evicted", LBANKS))
                        else:
                            pe.wait_ge(sems["evicted"], t.at("evicted", LBANKS - 1))
                        s_unit(0, 0)
                        s_unit(0, 1)

                    def turn_values(ahead):
                        if kind != "sw":
                            pe.wait_ge(sems["evicted"], t.at("evicted", LBANKS - ahead))
                            self.turn_v(VF, VBANK)
                            t.up("v_token")

                    if kind == "da":
                        for b in range(4):
                            self.whole(b)
                        pe.wait_ge(sems["v_token"], t.at("v_token"))
                    else:
                        project(0, 8)
                        if kind == "mla":
                            pe.wait_ge(sems["sum_used"], t.at("sum_used", CREDITS["sum_used"]))
                        project(8, 16)
                    start()
                    if kind != "da":
                        t_unit(0, 0)
                    turn_values(1 if kind == "da" else 0)

                    def body(it):
                        more = not isinstance(it, int) or it < 3
                        t.up("o_used")
                        if kind == "da":
                            t.up("sum_used")
                            for i in range(QT):
                                if i + 1 < QT:
                                    s_unit(i + 1, 0)
                                    s_unit(i + 1, 1)
                                elif more:
                                    pe.wait_ge(sems["evicted"], t.at("evicted", LBANKS - 1))
                                    s_unit(0, 0)
                                    s_unit(0, 1)
                                if more:
                                    if i == 3:
                                        pe.wait_ge(sems["sum_used"], t.at("sum_used"))
                                    for k in range(4):
                                        self.some(i, k, LBANKS)
                                t_unit(2 * i, i)
                                if more:
                                    for k in range(4, 8):
                                        self.some(i, k, LBANKS)
                                if i == 0:
                                    pe.wait_ge(sems["v_token"], t.at("v_token"))
                                    pe.wait_ge(sems["o_used"], t.at("o_used"))
                                pv_unit(i, i, 0)
                            if more:
                                turn_values(1)
                            pe.wait_ge(sems["evicted"], t.at("evicted", LBANKS))
                            self.sums(3, 1, lambda k: TA[:])
                        else:
                            cuts = (0, 6, 9, 12, 15, 16) if kind == "mla" else (0, 6, 8, 10, 12, 14, 16)
                            for u, (i, m) in enumerate(UNITS):
                                if u + 2 < len(UNITS):
                                    s_unit(*UNITS[u + 2])
                                elif more:
                                    pe.wait_ge(sems["evicted"], t.at("evicted", LBANKS - (kind == "sw")))
                                    s_unit(*UNITS[u + 2 - len(UNITS)])
                                if more and u + 1 < len(cuts) and (kind, u) != ("sw", 0):
                                    project(cuts[u], cuts[u + 1])
                                if more or u + 1 < len(UNITS):
                                    t_unit((u + 1) % len(UNITS), UNITS[(u + 1) % len(UNITS)][0])
                                if u == 0:
                                    if kind == "mla":
                                        pe.wait_ge(sems["v_token"], t.at("v_token"))
                                    pe.wait_ge(sems["o_used"], t.at("o_used"))
                                pv_unit(u, i, m, more)
                                if more and (kind, u) == ("sw", 0):
                                    project(cuts[0], cuts[1])
                            if more:
                                turn_values(0)
                    t.turns(4, body)

                def gates(self, l):
                    t.up("made")

                    def body(it):
                        for j in range(6):
                            b, g = j % 3, 2 * (j % 2)
                            self.bank_free(2)
                            self.begin()
                            for k in range(KT):
                                self.products(g, k, 12, HH, HL, k, k == 0, k == KT - 1)
                            if j == 2 and isinstance(it, int) and it == 0:
                                pe.wait_ge(sems["made"], t.at("made"))
                            for k in range(4):
                                ins = self.products(g + 1, KT + k, 12, ZH, ZL, 4 * b + k, k == 0, k == 3)
                            self.finish(ins)
                    t.turns(4, body)

                def linear(self, parts, hi, lo, m, g, src=None):
                    if src is not None:
                        t.up("operand", KT)
                    else:
                        t.up("made")

                    def body(it):
                        for j in range(2):
                            self.bank_free(2)
                            if not (isinstance(it, int) and it == 0):
                                pe.wait_ge(sems["m_squared"], t.at("m_squared", -1))
                            t.up("m_squared")
                            for c in range(parts):
                                self.begin()
                                n = WIDTH[t.c]
                                for k in range(n):
                                    if src is None and isinstance(it, int) and it + j == 0 and c == parts - 1 and k == n - 4:
                                        pe.wait_ge(sems["made"], t.at("made"))
                                    if src is not None and isinstance(it, int) and it + j == 0:
                                        pe.wait_ge(sems["operand"], t.at("operand", k + 1 - KT))
                                    ins = self.products(j, k, n, hi, lo, c * n + k, c + k == 0, c == parts - 1 and k == n - 1)
                                self.finish(ins)
                    t.turns(4, body)

                def ple(self, l):
                    self.postnorm(M1)
                    t.up("operand", 10)

                    def body(it):
                        for j in range(2):
                            self.bank_free(2)
                            self.begin()
                            first = isinstance(it, int) and it + j == 0
                            for k in range(KT):
                                if first:
                                    pe.wait_ge(sems["operand"], t.at("operand", k + 1 - 10))
                                self.products(2 * j, k, 10, HH, HL, k, k == 0, k == KT - 1)
                            if first:
                                pe.wait_ge(sems["operand"], t.at("operand"))
                            for k in range(2):
                                ins = self.products(2 * j + 1, KT + k, 10, PH, PL, k, k == 0, k == 1)
                            self.finish(ins)
                    t.turns(4, body)

                def ffn_up(self, l):
                    self.postnorm(M2)
                    t.up("operand", KT)

                    def body(it):
                        for j in range(2):
                            self.whole(2 * j, fresh=(j == 0 and isinstance(it, int) and it == 0))
                            if j == 0:
                                t.once(it, lambda: self.prenorm(SQ2))
                            self.whole(2 * j + 1)
                    t.turns(FT // 2, body)

                def retention(self):
                    t.up("operand", KT)

                    def body(h):
                        for j in range(4):
                            self.whole(j, fresh=(j == 0 and isinstance(h, int) and h == 0))
                            if j == 0:
                                t.once(h, lambda: self.prenorm(SQ2))
                        def turn(j, later):
                            pe.wait_ge(sems["evicted"], t.at("evicted", LBANKS - later))
                            if j:
                                pe.wait_ge(sems["v_token"], t.at("v_token"))
                            self.turn_v(RVF2)
                            t.up("v_token")

                        for j in range(4):
                            self.whole(j)
                            if j:
                                turn(j - 1, 1)
                        t.up("rotated", 4)
                        pe.wait_ge(sems["rotated"], t.at("rotated"))
                        for kt in range(QT):
                            if kt >= 2:
                                t.up("operand")
                                pe.wait_ge(sems["operand"], t.at("operand"))
                            n = SEQ - kt * P
                            for c in range(2):
                                ins = pe.matmul(banks[S0 + kt % 2][:, 0:n], RK[:, c, kt * P:(kt + 1) * P],
                                                RQ[:, c, kt * P:SEQ], start=(c == 0), stop=(c == 1))
                            ins.then_inc(sems["s_ready"], t.one("s_ready"))
                            if kt == 1:
                                turn(3, 0)
                        t.up("operand", 2)
                        pe.wait_ge(sems["operand"], t.at("operand"))
                        pe.wait_ge(sems["v_token"], t.at("v_token"))
                        for e in range(4):
                            t.up("y_copied")
                            if e >= 2:
                                pe.wait_ge(sems["y_copied"], t.at("y_copied", -2))
                            for kt in range(QT):
                                ins = pe.matmul(banks[TURN + e % 2][:, kt * P:SEQ], RVT[:, kt, e * P:(e + 1) * P],
                                                RP[:, kt, kt * P:SEQ], start=(kt == 0), stop=(kt == QT - 1))
                            ins.then_inc(sems["small"], t.one("small"))
                        self.whole(0)
                        pe.wait_ge(sems["y_copied"], t.at("y_copied"))
                        for e in range(4):
                            ins = pe.matmul(banks[S0][:], ONES[:], RY[:, e, :], start=(e == 0), stop=(e == 3))
                        ins.then_inc(sems["small"], t.one("small"))
                        self.whole(1)
                        self.whole(2)
                        self.sums(S0 + 1, 4, lambda e: RSQ[:, e, :])
                        self.whole(3)
                    t.turns(RET_HEADS, body)

                def dilated(self):
                    def tiles_of(par, x, ks, fresh=0):
                        hi, lo = (H2H, H2L) if x % 3 == 0 else (HH, HL)
                        if ks[0] == 0:
                            self.bank_free(2)
                            self.begin()
                        for k in ks:
                            if fresh:
                                pe.wait_ge(sems["operand"], t.at("operand", k + 1 + fresh))
                            ins = self.products(dil_bank(par, x), k, 8, hi, lo, k, k == 0, k == KT - 1)
                        if ks[-1] == KT - 1:
                            self.finish(ins)

                    def post(x, begun):
                        if x % 3 < 2:
                            t.up("operand")
                            pe.wait_ge(sems["operand"], t.at("operand"))
                            if x % 3 == 0:
                                pe.wait_ge(sems["v_token"], t.at("v_token"))
                            else:
                                pe.wait_ge(sems["rotated"], t.at("rotated"))
                            pe.matmul(banks[DAUX][:], PERM[:], (TA, TB)[x % 3][:], start=True, stop=True).then_inc(sems["swapped"], t.one("swapped"))
                            t.up("rotated")
                        else:
                            pe.wait_ge(sems["evicted"], t.at("evicted", LBANKS - begun))
                            pe.wait_ge(sems["rotated"], t.at("rotated"))
                            self.turn_v(DF, DAUX)
                            t.up("v_token")

                    def s_unit(par, u):
                        i, m = UNITS[u]
                        r = slice(64 * m, 64 * m + 64)
                        t.up("scored")
                        pe.wait_ge(sems["scored"], t.at("scored", CREDITS["scored"] - 1))
                        for g in range(3):
                            kb, n = key_blocks("sw" if g == 0 else "da", i)
                            ins = pe.matmul(banks[DSCORES[g]][:, 0:n * P], DQ[par][r, g, i * P:(i + 1) * P],
                                            DK[par][r, g, kb * P:(kb + n) * P], start=True, stop=True)
                        ins.then_inc(sems["s_ready"], t.one("s_ready"))

                    def t_group(u, g):
                        i, m = UNITS[u]
                        at_ = sum(key_blocks("sw" if f == 0 else "da", i)[1] for f in range(g)) * P
                        t.up("pt_copied")
                        pe.wait_ge(sems["pt_copied"], t.at("pt_copied"))
                        for b in range(key_blocks("sw" if g == 0 else "da", i)[1]):
                            ins = pe.transpose(banks[TURN][:, b * P:(b + 1) * P], DP[u % 2][:, at_ + b * P:at_ + (b + 1) * P], ID[:])
                        ins.then_inc(sems["turned"], t.one("turned"))

                    def pv_unit(par, u):
                        i, m = UNITS[u]
                        pe.wait_ge(sems["pt_copied"], t.at("pt_copied", CREDITS["pt_copied"]))
                        if u == 0:
                            t.up("o_used")
                            pe.wait_ge(sems["o_used"], t.at("o_used"))
                        r = slice(64 * m, 64 * m + 64)
                        for g in range(3):
                            kb, n = key_blocks("sw" if g == 0 else "da", i)
                            for b in range(n):
                                ins = pe.matmul(banks[OUTB][r, i * P:(i + 1) * P], DVT[par][:, g, kb + b, 64 * m:64 * m + 64],
                                                DPT[g][:, b * P:(b + 1) * P], start=(g + b == 0), stop=(g == 2 and b == n - 1))
                        ins.then_inc(sems["pv_done"], t.one("pv_done"))

                    def pair(par, more):
                        nxt = 1 - par
                        for u in range(len(UNITS)):
                            if u + 1 < len(UNITS):
                                s_unit(par, u + 1)
                            if u == 0:
                                if more:
                                    tiles_of(nxt, 0, range(KT))
                                post(8, more)
                            if more:
                                tiles_of(nxt, u + 1, range(0, 3))
                                post(u, True)
                            t.up("probs")
                            pe.wait_ge(sems["probs"], t.at("probs"))
                            for g, ks in enumerate((range(3, 5), range(5, 7), range(7, 8))):
                                t_group(u, g)
                                if more:
                                    tiles_of(nxt, u + 1, ks)
                            pv_unit(par, u)
                        if more:
                            pe.wait_ge(sems["rotated"], t.at("rotated"))
                            s_unit(nxt, 0)

                    self.postnorm(M2)
                    t.up("operand", 2 * KT)
                    for x in range(9):
                        tiles_of(0, x, range(KT), {0: -2 * KT, 1: -KT - 1}.get(x, 0))
                        if x == 0:
                            self.prenorm(SQD)
                        if x < 8:
                            post(x, False)
                    pe.wait_ge(sems["rotated"], t.at("rotated"))
                    s_unit(0, 0)

                    def body(it):
                        pair(0, True)
                        pair(1, not isinstance(it, int) or it < KT // 2 - 1)
                    t.turns(KT // 2, body)

            e = Programs()
            e.t = t
            run(e)

        @block.scalar
        def _(act):
            t = Tally(act)

            def hi_part():
                if t.c >= len(WIDTH):
                    return
                slot, n = t.c % RING, WIDTH[t.c] * P
                t.up(f"raw{slot}", 16)
                act.wait_ge(sems[f"raw{slot}"], t.at(f"raw{slot}"))
                t.up("slot_free")
                act.wait_ge(sems["slot_free"], t.at("slot_free"))
                act.copy(WH[slot][:, 0:n], RAW[slot][:, 0:n]).then_inc(sems["hi_done"], t.one("hi_done"))
                t.c += 1

            def std():
                t.up("var_ready")
                act.wait_ge(sems["var_ready"], t.at("var_ready"))
                act.activation(VAR[:], VAR[:], ACT.Sqrt).then_inc(sems["std_ready"], t.one("std_ready"))

            def squares(n, src, dst):
                for k in range(n):
                    act.activation(dst(k), src(k), ACT.Square).then_inc(sems["squared"], t.one("squared"))

            class Programs:
                mine, stage = "stage_act", 0

                def begin_stage(self):
                    act.wait_ge(sems["stage_pe"], t.at("stage_pe"))
                    act.wait_ge(sems["stage_act"], t.at("stage_act"))
                    act.wait_ge(sems["stage_dve"], t.at("stage_dve"))

                def end(self):
                    act.drain().then_inc(sems["stage_act"], t.one("stage_act"))

                def setup(self):
                    act.dma_start(X[:], d["x_t"]).then_inc(sems["x_loaded"], t.add("x_loaded", 16))
                    act.sem_inc(sems["pt_copied"], 1)
                    t.up("operand")
                    t.up("var_ready")
                    act.wait_ge(sems["var_ready"], t.at("var_ready"))
                    act.activation(SIN[:], TA[:], ACT.Sin).then_inc(sems["std_ready"], t.one("std_ready"))
                    act.activation(COS[:], TB[:], ACT.Sin).then_inc(sems["std_ready"], t.one("std_ready"))
                    t.up("var_ready")
                    act.wait_ge(sems["var_ready"], t.at("var_ready"))
                    act.activation(sm(DEN, 4), sm(MX, 4), ACT.Exp).then_inc(sems["std_ready"], t.one("std_ready"))
                    t.up("operand", 2)
                    act.wait_ge(sems["operand"], t.at("operand"))
                    act.dma_start(scratch[0], RVF[:]).then_inc(sems["scratch"], t.add("scratch", 16))
                    act.dma_start(scratch[1], RVW[:]).then_inc(sems["scratch"], t.add("scratch", 16))
                    act.wait_ge(sems["scratch"], t.at("scratch"))
                    t.up("small")
                    hi_part()

                def prenorm(self, targets, sq, updated=False):
                    for n, (hi, lo, g) in enumerate(targets):
                        for k in range(KT):
                            if updated and n == 0:
                                t.up("x_ready")
                                act.wait_ge(sems["x_ready"], t.at("x_ready"))
                            act.activation(hi[:, k, :], X[:, k, :], ACT.Copy, scale=gain(g, k)).then_inc(sems["operand_hi"], t.one("operand_hi"))
                        if n == 0:
                            squares(KT, lambda k: X[:, k, :], lambda k: sq[:, k, :])

                def postnorm(self, m):
                    std()

                def v_out(self, dst, bank=TURN):
                    t.up("v_turned")
                    act.wait_ge(sems["v_turned"], t.at("v_turned"))
                    act.copy(dst, banks[bank][:].rearrange("p (b k) -> p b k", b=QT)).then_inc(sems["v_token"], t.one("v_token"))

                def latents(self, l):
                    if l == 0:
                        act.wait_ge(sems["x_loaded"], t.at("x_loaded"))
                    self.prenorm([(HH, HL, f"pre{l}")], SQ1)
                    for j in range(7):
                        hi_part()
                        if j == 2:
                            t.up("operand", KT + 1)
                            act.wait_ge(sems["operand"], t.at("operand"))
                            squares(3, lambda k: LQ[:, k, :], lambda k: SS[k][:])
                        elif j in (0, 4, 5):
                            std()
                    self.v_out(CV[:])

                def attention(self, kind, l):
                    def e_unit(u, m):
                        _, n = key_blocks(kind, UNITS[u][0])
                        t.up("scored")
                        act.wait_ge(sems["scored"], t.at("scored", CREDITS["scored"]))
                        if kind == "sw":
                            act.activation(sm(ES + u), sm(ST + m), ACT.Exp, bias=sm(NM + u)).then_inc(sems["act_step"], t.one("act_step"))
                        act.activation(SS[u % 4][:, 0:n * P], SS[u % 4][:, 0:n * P], ACT.Exp, bias=sm(NM + u), accum_out=sm(DEN + u)).then_inc(sems["exped"], t.one("exped"))

                    def c_unit(n_unit, i):
                        _, n = key_blocks(kind, i)
                        t.up("turned")
                        act.wait_ge(sems["turned"], t.at("turned", CREDITS["turned"]))
                        t.up("pv_done")
                        act.wait_ge(sems["pv_done"], t.at("pv_done"))
                        act.copy(PT[n_unit % 2][:, 0:n * P], banks[TURN][:, 0:n * P]).then_inc(sems["pt_copied"], t.one("pt_copied"))

                    def silu():
                        t.up("z_ready")
                        act.wait_ge(sems["z_ready"], t.at("z_ready"))
                        act.activation(TC[:], (NZ if kind == "mla" else TC)[:], ACT.Silu).then_inc(sems["gate"], t.one("gate"))

                    for _ in range({"da": 4, "mla": 2, "sw": 1}[kind]):
                        hi_part()
                    e_unit(0, 0)
                    e_unit(1, 1)
                    if kind != "da":
                        c_unit(0, 0)
                    if kind != "sw":
                        self.v_out(VT[:], VBANK)

                    def body(it):
                        more = not isinstance(it, int) or it < 3
                        t.up("o_used")
                        if kind == "da":
                            for i in range(QT):
                                if more:
                                    hi_part()
                                if more or i + 1 < QT:
                                    e_unit((2 * i + 2) % len(UNITS), 0)
                                    e_unit((2 * i + 3) % len(UNITS), 1)
                                c_unit(i, i)
                                if i == 0:
                                    silu()
                            act.wait_ge(sems["pv_done"], t.at("pv_done", CREDITS["pv_done"]))
                            act.wait_ge(sems["o_used"], t.at("o_used", CREDITS["o_used"]))
                            act.activation(TA[:], banks[OUTB][:], ACT.Square).then_inc(sems["squared"], t.one("squared"))
                            if more:
                                self.v_out(VT[:], VBANK)
                            std()
                        else:
                            for u in range(len(UNITS)):
                                if kind == "sw" and (u == 0 or more and u == 1) or kind == "mla" and more and u in (0, 2):
                                    hi_part()
                                if more or u + 2 < len(UNITS):
                                    e_unit((u + 2) % len(UNITS), u % 2)
                                if u == 0:
                                    silu()
                                if more or u + 1 < len(UNITS):
                                    c_unit((u + 1) % len(UNITS), UNITS[(u + 1) % len(UNITS)][0])
                            if more and kind == "mla":
                                act.wait_ge(sems["pv_done"], t.at("pv_done", CREDITS["pv_done"] - 1))
                                self.v_out(VT[:], VBANK)
                    t.turns(4, body)

                def gates(self, l):
                    def body(it):
                        for j in range(6):
                            hi_part()
                            t.up("gate_in")
                            act.wait_ge(sems["gate_in"], t.at("gate_in"))
                            T_ = (TA, TB)[j % 2]
                            act.activation(T_[:], T_[:], ACT.Sigmoid).then_inc(sems["gate"], t.one("gate"))
                    t.turns(4, body)

                def linear(self, parts, hi, lo, m, g, src=None):
                    if src is not None:
                        t.up("o_used", KT)
                        for k in range(KT):
                            if k == KT - 1:
                                act.wait_ge(sems["o_used"], t.at("o_used", CREDITS["o_used"]))
                            act.copy(hi[:, k, :], src[:, k, :]).then_inc(sems["operand_hi"], t.one("operand_hi"))

                    def body(it):
                        for j in range(2):
                            for c in range(parts):
                                hi_part()
                            t.up("m_ready")
                            act.wait_ge(sems["m_ready"], t.at("m_ready"))
                            act.activation((TA, TB)[j][:], banks[j][:], ACT.Square).then_inc(sems["m_squared"], t.one("m_squared"))
                    t.turns(4, body)

                def ple(self, l):
                    self.postnorm(M1)
                    for k in range(KT):
                        t.up("x_ready")
                        act.wait_ge(sems["x_ready"], t.at("x_ready"))
                        act.copy(HH[:, k, :], X[:, k, :]).then_inc(sems["operand_hi"], t.one("operand_hi"))

                    def body(it):
                        for j in range(2):
                            hi_part()
                            t.up("chunk_done")
                            act.wait_ge(sems["chunk_done"], t.at("chunk_done", CREDITS["chunk_done"]))
                            act.activation((TA, TB)[j][:], banks[2 * j][:], ACT.Sigmoid).then_inc(sems["gate"], t.one("gate"))
                    t.k["chunk_done"] = t.c - 1
                    t.up("operand", 10)
                    t.turns(4, body)

                def ffn_up(self, l):
                    self.postnorm(M2)
                    self.prenorm([(HH, HL, f"ffnpre{l}")], SQ2, True)

                    def body(it):
                        for j in range(2):
                            hi_part()
                            if j == 0:
                                t.once(it, std)
                            hi_part()
                            t.up("gate_in")
                            act.wait_ge(sems["gate_in"], t.at("gate_in"))
                            act.activation(GL[j][:], CO[j][:], ACT.Gelu_apprx_tanh).then_inc(sems["gate"], t.one("gate"))
                    t.turns(FT // 2, body)

                def retention(self):
                    self.prenorm([(HH, HL, "mixpre0")], SQ2)

                    def body(h):
                        for j in range(4):
                            hi_part()
                            if j == 0:
                                t.once(h, std)
                        for j in range(4):
                            hi_part()
                            if j:
                                self.v_out(RVT[:, :, (j - 1) * P:j * P])
                        self.v_out(RVT[:, :, 3 * P:4 * P])
                        for e in range(4):
                            t.up("small")
                            act.wait_ge(sems["small"], t.at("small"))
                            act.copy(RY[:, e, :], banks[TURN + e % 2][:]).then_inc(sems["y_copied"], t.one("y_copied"))
                        hi_part()
                        t.up("small")
                        for e in range(4):
                            t.up("centred")
                            act.wait_ge(sems["centred"], t.at("centred"))
                            act.activation(RSQ[:, e, :], RY[:, e, :], ACT.Square).then_inc(sems["squared"], t.one("squared"))
                        for j in range(3):
                            hi_part()
                        std()
                        for e in range(4):
                            t.up("gate_in")
                            act.wait_ge(sems["gate_in"], t.at("gate_in"))
                            act.activation(RP[:, e, :], RP[:, e, :], ACT.Silu).then_inc(sems["gate"], t.one("gate"))
                    t.turns(RET_HEADS, body)

                def dilated(self):
                    def e_unit(u):
                        t.up("scored")
                        act.wait_ge(sems["scored"], t.at("scored", CREDITS["scored"]))
                        w = dil_width(UNITS[u][0])
                        act.activation(DP[u % 2][:, 0:w], DP[u % 2][:, 0:w], ACT.Exp, bias=sm(NM + u), accum_out=sm(DEN + u)).then_inc(sems["exped"], t.one("exped"))

                    def c_unit(u):
                        i, m = UNITS[u]
                        for g in range(3):
                            _, n = key_blocks("sw" if g == 0 else "da", i)
                            t.up("turned")
                            act.wait_ge(sems["turned"], t.at("turned", CREDITS["turned"]))
                            if g == 0:
                                act.wait_ge(sems["pv_done"], t.at("pv_done", CREDITS["pv_done"]))
                            act.copy(DPT[g][:, 0:n * P], banks[TURN][:, 0:n * P]).then_inc(sems["pt_copied"], t.one("pt_copied"))
                        t.up("pv_done")

                    def pair(par, more):
                        nxt = 1 - par
                        for u in range(len(UNITS)):
                            if more:
                                hi_part()
                            if u + 1 < len(UNITS):
                                e_unit(u + 1)
                            if u == 0:
                                self.v_out(DVT[par][:, 2], DAUX)
                                if more:
                                    hi_part()
                            elif more and u % 3 == 2:
                                self.v_out(DVT[nxt][:, u // 3], DAUX)
                            c_unit(u)
                        if more:
                            e_unit(0)

                    self.postnorm(M2)
                    self.prenorm([(H2H, H2L, "mixpre1"), (HH, HL, "kv")], SQD, True)
                    for x in range(9):
                        hi_part()
                        if x == 0:
                            std()
                        if x % 3 == 2 and x < 8:
                            self.v_out(DVT[0][:, x // 3], DAUX)
                    e_unit(0)

                    def body(it):
                        pair(0, True)
                        pair(1, not isinstance(it, int) or it < KT // 2 - 1)
                    t.turns(KT // 2, body)

            e = Programs()
            e.t = t
            run(e)

        @block.vector
        def _(dve):
            t = Tally(dve)

            def lo_part():
                if t.c >= len(WIDTH):
                    return
                slot, n = t.c % RING, WIDTH[t.c] * P
                t.up("hi_done")
                dve.wait_ge(sems["hi_done"], t.at("hi_done"))
                dve.tensor_tensor(WL[slot][:, 0:n], RAW[slot][:, 0:n], WH[slot][:, 0:n].bitcast(F32), ALU.subtract).then_inc(sems["lo_done"], t.one("lo_done"))
                t.c += 1

            def passed():
                dve.sem_inc(sems["waits_passed"], 1)

            def signal(name):
                dve.sem_inc(sems[name], 1)
                t.up(name)

            def chunk():
                t.up("chunk_done")
                dve.wait_ge(sems["chunk_done"], t.at("chunk_done", CREDITS["chunk_done"]))

            def split(hi, lo, src):
                dve.tensor_copy(hi, src).then_inc(sems["dve_step"], t.one("dve_step"))
                dve.wait_ge(sems["dve_step"], t.at("dve_step"))
                dve.tensor_tensor(lo, src, hi.bitcast(F32), ALU.subtract).then_inc(sems["dve_step"], t.one("dve_step"))
                dve.wait_ge(sems["dve_step"], t.at("dve_step"))

            def rstd(bank, n, dst=RSTD):
                t.up("summed")
                dve.wait_ge(sems["summed"], t.at("summed"))
                dve.tensor_scalar(VAR[:], banks[bank][:], 1.0 / n, EPS, ALU.mult, ALU.add).then_inc(sems["var_ready"], t.one("var_ready"))
                t.up("std_ready")
                dve.wait_ge(sems["std_ready"], t.at("std_ready"))
                dve.reciprocal(dst[:], VAR[:]).then_inc(sems["dve_step"], t.one("dve_step"))
                dve.wait_ge(sems["dve_step"], t.at("dve_step"))

            class Programs:
                mine, stage = "stage_dve", 0

                def begin_stage(self):
                    dve.wait_ge(sems["stage_pe"], t.at("stage_pe"))
                    dve.wait_ge(sems["stage_act"], t.at("stage_act"))
                    dve.wait_ge(sems["stage_dve"], t.at("stage_dve"))

                def end(self):
                    dve.drain().then_inc(sems["stage_dve"], t.one("stage_dve"))

                def setup(self):
                    for n, c in (("lo_done", RING), ("evicted", LBANKS), ("scored", 2), ("o_used", 1), ("sum_used", 1)):
                        dve.sem_inc(sems[n], c)
                    dve.memset(ONES[:], 1.0).then_inc(sems["dve_step"], t.one("dve_step"))
                    dve.wait_ge(sems["dve_step"], t.at("dve_step"))
                    t.up("loaded", 144)
                    dve.wait_ge(sems["loaded"], t.at("loaded"))
                    dve.memset(TAB[BUCKETS:BUCKETS + 1, :], 1.0).then_inc(sems["operand"], t.one("operand"))
                    dve.wait_ge(sems["operand"], t.at("operand"))
                    dve.tensor_copy(ANG[:], POSI[:]).then_inc(sems["dve_step"], t.one("dve_step"))
                    dve.wait_ge(sems["dve_step"], t.at("dve_step"))
                    dve.tensor_scalar(ANG[:], ANG[:], COLS[:, 0:1], None, ALU.mult).then_inc(sems["dve_step"], t.one("dve_step"))
                    dve.wait_ge(sems["dve_step"], t.at("dve_step"))
                    dve.tensor_scalar(TC[:], ANG[:], 1.0 / (2 * math.pi), None, ALU.mult).then_inc(sems["dve_step"], t.one("dve_step"))
                    dve.wait_ge(sems["dve_step"], t.at("dve_step"))
                    dve.tensor_scalar(TC[:], TC[:], MAGIC, None, ALU.add).then_inc(sems["dve_step"], t.one("dve_step"))
                    dve.wait_ge(sems["dve_step"], t.at("dve_step"))
                    dve.tensor_scalar(TC[:], TC[:], -MAGIC, None, ALU.add).then_inc(sems["dve_step"], t.one("dve_step"))
                    dve.wait_ge(sems["dve_step"], t.at("dve_step"))
                    for part in (TWO_PI_A, TWO_PI_B, TWO_PI_C):
                        dve.scalar_tensor_tensor(ANG[:], TC[:], -part, ANG[:], ALU.mult, ALU.add).then_inc(sems["dve_step"], t.one("dve_step"))
                        dve.wait_ge(sems["dve_step"], t.at("dve_step"))
                    dve.tensor_scalar(TB[:], ANG[:], math.pi / 2, None, ALU.add).then_inc(sems["dve_step"], t.one("dve_step"))
                    dve.wait_ge(sems["dve_step"], t.at("dve_step"))
                    dve.tensor_scalar(TC[:], TB[:], math.pi, -2 * math.pi, ALU.is_gt, ALU.mult).then_inc(sems["dve_step"], t.one("dve_step"))
                    dve.wait_ge(sems["dve_step"], t.at("dve_step"))
                    dve.tensor_tensor(TB[:], TB[:], TC[:], ALU.add).then_inc(sems["dve_step"], t.one("dve_step"))
                    dve.wait_ge(sems["dve_step"], t.at("dve_step"))
                    dve.tensor_scalar(TB[:], TB[:], 3.1415925, -3.1415925, ALU.min, ALU.max).then_inc(sems["dve_step"], t.one("dve_step"))
                    dve.wait_ge(sems["dve_step"], t.at("dve_step"))
                    dve.tensor_scalar(TA[:], ANG[:], 3.1415925, -3.1415925, ALU.min, ALU.max).then_inc(sems["var_ready"], t.one("var_ready"))
                    t.up("std_ready", 2)
                    dve.wait_ge(sems["std_ready"], t.at("std_ready"))
                    dve.tensor_scalar(SIN[:], SIN[:], COLS[:, 1:2], None, ALU.mult).then_inc(sems["dve_step"], t.one("dve_step"))
                    dve.wait_ge(sems["dve_step"], t.at("dve_step"))
                    for l in range(DEPTH):
                        for a in range(2):
                            ins = dve.tensor_tensor_reduce(TC[:, 0:HEAD], LAM[:, l, 2 * a, :], LAM[:, l, 2 * a + 1, :], 1.0, 0.0,
                                                           ALU.mult, ALU.add, sm(MX + 2 * l + a))
                            if (l, a) == (DEPTH - 1, 1):
                                ins.then_inc(sems["var_ready"], t.one("var_ready"))
                            else:
                                ins.then_inc(sems["dve_step"], t.one("dve_step"))
                                dve.wait_ge(sems["dve_step"], t.at("dve_step"))
                    t.up("std_ready")
                    dve.wait_ge(sems["std_ready"], t.at("std_ready"))
                    for l in range(DEPTH):
                        dve.tensor_tensor(sm(LAMC + l), sm(DEN + 2 * l + 1), sm(DEN + 2 * l), ALU.subtract).then_inc(sems["dve_step"], t.one("dve_step"))
                        dve.wait_ge(sems["dve_step"], t.at("dve_step"))
                        dve.tensor_scalar(sm(LAMC + l), sm(LAMC + l), -LAM_INIT[l], None, ALU.add).then_inc(sems["dve_step"], t.one("dve_step"))
                        dve.wait_ge(sems["dve_step"], t.at("dve_step"))
                        dve.tensor_scalar(sm(SUBG + l), gain(f"subln{l}"), 1.0 - LAM_INIT[l], None, ALU.mult).then_inc(sems["dve_step"], t.one("dve_step"))
                        dve.wait_ge(sems["dve_step"], t.at("dve_step"))
                    t.up("small")
                    dve.wait_ge(sems["small"], t.at("small"))
                    for n, dst in enumerate((RVF, RVW)):
                        dve.tensor_copy(dst[:, 0:RV // 2], banks[2 * n][0:BHEADS, 0:RV // 2]).then_inc(sems["dve_step"], t.one("dve_step"))
                        dve.wait_ge(sems["dve_step"], t.at("dve_step"))
                        dve.tensor_copy(dst[:, RV // 2:RV], banks[2 * n + 1][0:BHEADS, 0:RV // 2]).then_inc(sems["operand"], t.one("operand"))
                        dve.wait_ge(sems["operand"], t.at("operand"))
                    lo_part()

                def lo_tile(self, k, hi, lo, g=None):
                    t.up("operand_hi")
                    dve.wait_ge(sems["operand_hi"], t.at("operand_hi"))
                    if g is None:
                        ins = dve.tensor_tensor(lo[:, k, :], X[:, k, :], hi[:, k, :].bitcast(F32), ALU.subtract)
                    else:
                        ins = dve.scalar_tensor_tensor(lo[:, k, :], X[:, k, :], gain(g, k), hi[:, k, :].bitcast(F32), ALU.mult, ALU.subtract)
                    ins.then_inc(sems["operand"], t.one("operand"))

                def prenorm(self, targets):
                    for hi, lo, g in targets:
                        for k in range(KT):
                            self.lo_tile(k, hi, lo, g)

                def postnorm(self, m, target=None):
                    rstd(OUTB, D)
                    for k in range(KT + 3):
                        if k < KT:
                            dve.tensor_tensor(m[:, k, :], m[:, k, :], RSTD[:], ALU.mult).then_inc(sems["dve_step"], t.one("dve_step"))
                        if 0 < k <= KT:
                            dve.wait_ge(sems["dve_step"], t.at("dve_step", -1 if k < KT else 0))
                            dve.tensor_tensor(X[:, k - 1, :], X[:, k - 1, :], m[:, k - 1, :], ALU.add).then_inc(sems["x_ready"], t.one("x_ready"))
                        if target is not None and k >= 3:
                            dve.wait_ge(sems["x_ready"], t.at("x_ready", -2 if k < KT + 1 else 0))
                            self.lo_tile(k - 3, *target)

                def latents(self, l):
                    if l == 0:
                        t.up("x_loaded", 16)
                        dve.wait_ge(sems["x_loaded"], t.at("x_loaded"))
                    self.prenorm([(HH, HL, f"pre{l}")])

                    def latent(bank, n, k, name, hi, lo):
                        rstd(bank, n * P, RSTD2)
                        for a in range(n):
                            dve.scalar_tensor_tensor(TC[:], LQ[:, k + a, :], gain(name, a), RSTD2[:], ALU.mult, ALU.mult).then_inc(sems["dve_step"], t.one("dve_step"))
                            dve.wait_ge(sems["dve_step"], t.at("dve_step"))
                            split(hi[:, a, :], lo[:, a, :], TC[:])

                    for j, dst in enumerate((LQ[:, 0, :], LQ[:, 1, :], LQ[:, 2, :], TA[:], TB[:], CK[:], VF[:])):
                        lo_part()
                        if j == 0:
                            rstd(OUTB, D)
                        chunk()
                        dve.tensor_tensor(dst, banks[j % LBANKS][:], RSTD[:], ALU.mult).then_inc(sems["evicted"], t.one("evicted"))
                        dve.wait_ge(sems["evicted"], t.at("evicted", CREDITS["evicted"]))
                        if j == 2:
                            signal("operand")
                        elif j == 4:
                            latent(OUTB, 2, 0, f"mlaq{l}", QNH, QNL)
                        elif j == 5:
                            latent(S0, 1, 2, f"mlakv{l}", KNH, KNL)
                    t.up("v_turned")
                    dve.tensor_tensor(TA[:], TA[:], COS[:], ALU.mult).then_inc(sems["dve_step"], t.one("dve_step"))
                    dve.wait_ge(sems["dve_step"], t.at("dve_step"))
                    dve.tensor_tensor(TB[:], TB[:], SIN[:], ALU.mult).then_inc(sems["dve_step"], t.one("dve_step"))
                    dve.wait_ge(sems["dve_step"], t.at("dve_step"))
                    dve.tensor_tensor(KR[:], TA[:], TB[:], ALU.add).then_inc(sems["dve_step"], t.one("dve_step"))
                    dve.wait_ge(sems["dve_step"], t.at("dve_step"))
                    t.up("stage_loads", 128)
                    dve.wait_ge(sems["stage_loads"], t.at("stage_loads"))
                    if l == 0:
                        t.up("biased", 16 * BHEADS)
                        dve.wait_ge(sems["biased"], t.at("biased"))

                def attention(self, kind, l):
                    scale = float((HEAD + ROPE) ** -0.5) if kind == "mla" else float(HEAD ** -0.5)
                    branch = ("da", "mla", "sw").index(kind)

                    def u1(u):
                        i, m = UNITS[u]
                        _, n = key_blocks(kind, i)
                        w = n * P
                        t.up("s_ready")
                        dve.wait_ge(sems["s_ready"], t.at("s_ready"))
                        if kind == "da":
                            if m == 0:
                                t.up("turned")
                            dve.wait_ge(sems["turned"], t.at("turned", CREDITS["turned"] - 2))
                        else:
                            t.up("turned")
                            dve.wait_ge(sems["turned"], t.at("turned"))
                        if kind == "sw":
                            bias = BT[:, (m + 1) * 2 * P - w:(m + 1) * 2 * P]
                        else:
                            bias = (BT if kind == "da" else MASK)[:, SEQ - w:SEQ]
                        passed()
                        dve.tensor_tensor_reduce(SS[u % 4][:, 0:w], banks[S0 + m][:, 0:w], bias, 1.0, LOWEST, ALU.add, ALU.max, sm(MX + u)).then_inc(sems["dve_step"], t.one("dve_step"))
                        dve.wait_ge(sems["dve_step"], t.at("dve_step"))
                        if kind == "sw":
                            ins = dve.tensor_scalar(sm(NM + u), sm(MX + u), -1.0, sm(NST + m), ALU.mult, ALU.min)
                        else:
                            ins = dve.tensor_scalar(sm(NM + u), sm(MX + u), -1.0, None, ALU.mult)
                        ins.then_inc(sems["scored"], t.one("scored"))

                    def u2(u):
                        i, m = UNITS[u]
                        w = key_blocks(kind, i)[1] * P
                        t.up("exped")
                        dve.wait_ge(sems["exped"], t.at("exped"))
                        if kind == "sw":
                            dve.tensor_tensor(sm(DEN + u), sm(DEN + u), sm(ES + u), ALU.add).then_inc(sems["dve_step"], t.one("dve_step"))
                            dve.wait_ge(sems["dve_step"], t.at("dve_step"))
                        dve.reciprocal(sm(RC1 + u), sm(DEN + u)).then_inc(sems["dve_step"], t.one("dve_step"))
                        dve.wait_ge(sems["dve_step"], t.at("dve_step"))
                        S_ = SS[u % 4][:, 0:w]
                        if kind != "da":
                            dve.tensor_scalar(S_, S_, sm(RC1 + u), None, ALU.mult).then_inc(sems["probs"], t.one("probs"))
                        elif m == 1:
                            dve.tensor_scalar(S_, S_, sm(RC1 + u), sm(LAMC + l), ALU.mult, ALU.mult).then_inc(sems["dve_step"], t.one("dve_step"))
                            dve.wait_ge(sems["dve_step"], t.at("dve_step"))
                            F_ = SS[(u - 1) % 4][:, 0:w]
                            dve.scalar_tensor_tensor(F_, F_, sm(RC1 + u - 1), S_, ALU.mult, ALU.add).then_inc(sems["probs"], t.one("probs"))

                    def evict(dst, bank, s=None):
                        if s is None:
                            dve.tensor_tensor(dst, banks[bank][:], RSTD[:], ALU.mult).then_inc(sems["evicted"], t.one("evicted"))
                            dve.wait_ge(sems["evicted"], t.at("evicted", CREDITS["evicted"]))
                        else:
                            dve.scalar_tensor_tensor(dst, banks[bank][:], s, RSTD[:], ALU.mult, ALU.mult).then_inc(sems["evicted"], t.one("evicted"))
                            dve.wait_ge(sems["evicted"], t.at("evicted", CREDITS["evicted"]))

                    def biases(it):
                        if kind != "mla":
                            src = (BDA if kind == "da" else BSW)[:, bass.ds(it, 1), :].rearrange("p o n -> p (o n)")
                            dve.tensor_scalar(BT[:], src, 1.0, None, ALU.mult).then_inc(sems["dve_step"], t.one("dve_step"))

                    def sinks(it):
                        if kind == "sw":
                            dve.tensor_scalar(sm(ST, 2), SM[:, bass.ds(SINK + 2 * it, 2)], 1.0, None, ALU.mult).then_inc(sems["dve_step"], t.one("dve_step"))
                            dve.tensor_scalar(sm(NST, 2), SM[:, bass.ds(SINK + 2 * it, 2)], -1.0, None, ALU.mult).then_inc(sems["dve_step"], t.one("dve_step"))

                    def part():
                        t.up("part_done")
                        dve.wait_ge(sems["part_done"], t.at("part_done"))

                    def mla_evict(n):
                        if n == 0:
                            chunk()
                            evict(NZ[:], 0)
                        elif n == 1:
                            part()
                            dve.tensor_copy(VF[:], banks[1][:]).then_inc(sems["evicted"], t.one("evicted"))
                        elif n == 2:
                            part()
                            dve.tensor_scalar(AQ[:], banks[2][:], scale, None, ALU.mult).then_inc(sems["evicted"], t.one("evicted"))
                        elif n == 3:
                            part()
                            dve.scalar_tensor_tensor(AR[:], banks[3][:], scale, COS[:], ALU.mult, ALU.mult).then_inc(sems["evicted"], t.one("evicted"))
                        elif n == 4:
                            part()
                            dve.scalar_tensor_tensor(TA[:], banks[0][:], scale, SIN[:], ALU.mult, ALU.mult).then_inc(sems["evicted"], t.one("evicted"))
                            dve.wait_ge(sems["evicted"], t.at("evicted", CREDITS["evicted"]))
                            dve.tensor_tensor(AR[:], AR[:], TA[:], ALU.add).then_inc(sems["dve_step"], t.one("dve_step"))
                            dve.wait_ge(sems["dve_step"], t.at("dve_step"))
                        else:
                            chunk()
                            dve.tensor_copy(AK[:], banks[1][:]).then_inc(sems["evicted"], t.one("evicted"))

                    def gate_tile():
                        if kind != "mla":
                            chunk()
                            evict(TC[:], 3 if kind == "da" else 1)
                        signal("z_ready")

                    def first_units():
                        u1(0)
                        if kind == "da":
                            u1(1)
                            u2(0)
                            u2(1)
                        else:
                            u2(0)
                            u1(1)

                    t.up("v_turned", 0 if kind == "sw" else 4)
                    biases(0)
                    sinks(0)
                    if kind == "da":
                        for j, dst in enumerate((AQ, AK, VF)):
                            lo_part()
                            chunk()
                            evict(dst[:], j, (scale, None, None)[j])
                        lo_part()
                    elif kind == "sw":
                        lo_part()
                        chunk()
                        evict(AQ[:], 0, scale)
                    else:
                        lo_part()
                        mla_evict(0)
                        lo_part()
                        for n in range(1, 6):
                            mla_evict(n)
                        dve.wait_ge(sems["evicted"], t.at("evicted", CREDITS["evicted"]))
                    first_units()
                    gate_tile()

                    def body(it):
                        more = not isinstance(it, int) or it < 3
                        if kind == "da":
                            for i in range(QT):
                                if more or i + 1 < QT:
                                    u1((2 * i + 2) % len(UNITS))
                                    u1((2 * i + 3) % len(UNITS))
                                if more:
                                    lo_part()
                                if more or i + 1 < QT:
                                    u2((2 * i + 2) % len(UNITS))
                                    u2((2 * i + 3) % len(UNITS))
                                if more and i == 2:
                                    chunk()
                                    evict(AQ[:], 0, scale)
                                    chunk()
                                    evict(AK[:], 1)
                                    biases(it + 1)
                                    chunk()
                                    evict(VF[:], 2)
                            t.up("pv_done", QT)
                        else:
                            for u in range(len(UNITS)):
                                if more or u + 1 < len(UNITS):
                                    u2((u + 1) % len(UNITS))
                                if kind == "sw" and u == 0:
                                    lo_part()
                                if more and u == 6:
                                    sinks(it + 1)
                                if more or u + 2 < len(UNITS):
                                    u1((u + 2) % len(UNITS))
                                if kind == "sw" and more and u == 1 or kind == "mla" and more and u in (0, 2):
                                    lo_part()
                                if not more:
                                    continue
                                if kind == "sw" and u == 5:
                                    chunk()
                                    evict(AQ[:], 0, scale)
                                    biases(it + 1)
                                elif kind == "mla":
                                    if u == 2:
                                        dve.wait_ge(sems["gate"], t.at("gate", 1))
                                    for n in {2: (0, 1), 5: (2, 3, 4, 5)}.get(u, ()):
                                        mla_evict(n)
                            t.up("pv_done", len(UNITS))
                        t.up("gate")
                        dve.wait_ge(sems["gate"], t.at("gate"))
                        dve.wait_ge(sems["pv_done"], t.at("pv_done", CREDITS["pv_done"]))
                        dve.tensor_tensor(TB[:], banks[OUTB][:], TC[:], ALU.mult).then_inc(sems["o_used"], t.one("o_used"))
                        dve.wait_ge(sems["o_used"], t.at("o_used", CREDITS["o_used"]))
                        if more:
                            gate_tile()
                        if kind == "da":
                            rstd(3, P, RSTD2)
                            signal("sum_used")
                            dve.scalar_tensor_tensor(TB[:], TB[:], sm(SUBG + l), RSTD2[:], ALU.mult, ALU.mult).then_inc(sems["dve_step"], t.one("dve_step"))
                            dve.wait_ge(sems["dve_step"], t.at("dve_step"))
                        z = bass.ds(it + 4 * branch, 1)
                        split(ZH[:, z, :].rearrange("p o n -> p (o n)"), ZL[:, z, :].rearrange("p o n -> p (o n)"), TB[:])
                    t.turns(4, body)
                    if kind == "sw":
                        signal("made")

                def gates(self, l):
                    def body(it):
                        for j in range(6):
                            b, g, T_ = j % 3, 2 * (j % 2), (TA, TB)[j % 2]
                            lo_part()
                            chunk()
                            dve.tensor_tensor(T_[:], banks[g][:], RSTD[:], ALU.mult).then_inc(sems["gate_in"], t.one("gate_in"))
                            t.up("gate")
                            dve.wait_ge(sems["gate"], t.at("gate"))
                            if b == 0:
                                dve.tensor_tensor(TC[:], T_[:], banks[g + 1][:], ALU.mult).then_inc(sems["evicted"], t.one("evicted"))
                                dve.wait_ge(sems["evicted"], t.at("evicted", CREDITS["evicted"]))
                            else:
                                dve.tensor_tensor(T_[:], T_[:], banks[g + 1][:], ALU.mult).then_inc(sems["evicted"], t.one("evicted"))
                                dve.wait_ge(sems["evicted"], t.at("evicted", CREDITS["evicted"]))
                                dve.tensor_tensor(TC[:], TC[:], T_[:], ALU.add).then_inc(sems["dve_step"], t.one("dve_step"))
                                dve.wait_ge(sems["dve_step"], t.at("dve_step"))
                            if b == 2:
                                n = bass.ds(2 * it + j // 3, 1)
                                split(YH[:, n, :].rearrange("p o n -> p (o n)"), YL[:, n, :].rearrange("p o n -> p (o n)"), TC[:])
                    t.turns(4, body)
                    signal("made")

                def linear(self, parts, hi, lo, m, g, src=None):
                    if src is not None:
                        for k in range(KT):
                            t.up("operand_hi")
                            dve.wait_ge(sems["operand_hi"], t.at("operand_hi"))
                            dve.tensor_tensor(lo[:, k, :], src[:, k, :], hi[:, k, :].bitcast(F32), ALU.subtract).then_inc(sems["operand"], t.one("operand"))

                    dve.memset(TC[:], 0.0).then_inc(sems["dve_step"], t.one("dve_step"))
                    dve.wait_ge(sems["dve_step"], t.at("dve_step"))

                    def body(it):
                        for j in range(2):
                            for c in range(parts):
                                lo_part()
                                chunk()
                            n = bass.ds(2 * it + j, 1)
                            dve.tensor_scalar(m[:, n, :].rearrange("p o n -> p (o n)"), banks[j][:],
                                              G[:, bass.ds(GAINS[g] + 2 * it + j, 1)], None, ALU.mult).then_inc(sems["evicted"], t.one("evicted"))
                            dve.wait_ge(sems["evicted"], t.at("evicted", CREDITS["evicted"]))
                            signal("m_ready")
                            t.up("m_squared")
                            dve.wait_ge(sems["m_squared"], t.at("m_squared"))
                            dve.tensor_tensor(TC[:], TC[:], (TA, TB)[j][:], ALU.add).then_inc(sems["dve_step"], t.one("dve_step"))
                            dve.wait_ge(sems["dve_step"], t.at("dve_step"))
                    t.turns(4, body)

                def ple(self, l):
                    self.postnorm(M1, (HH, HL))
                    t.up("stage_loads", 16)
                    dve.wait_ge(sems["stage_loads"], t.at("stage_loads"))
                    for k in range(2):
                        dve.tensor_copy(PH[:, k, :], PX[:, k, :]).then_inc(sems["dve_step"], t.one("dve_step"))
                        dve.wait_ge(sems["dve_step"], t.at("dve_step"))
                        dve.tensor_tensor(PL[:, k, :], PX[:, k, :], PH[:, k, :].bitcast(F32), ALU.subtract).then_inc(sems["operand"], t.one("operand"))
                        dve.wait_ge(sems["operand"], t.at("operand"))

                    def body(it):
                        for j in range(2):
                            lo_part()
                            chunk()
                            t.up("gate")
                            dve.wait_ge(sems["gate"], t.at("gate"))
                            T_ = (TA, TB)[j]
                            dve.tensor_tensor(T_[:], T_[:], banks[2 * j + 1][:], ALU.mult).then_inc(sems["evicted"], t.one("evicted"))
                            dve.wait_ge(sems["evicted"], t.at("evicted", CREDITS["evicted"]))
                            xn = X[:, bass.ds(2 * it + j, 1), :].rearrange("p o n -> p (o n)")
                            dve.tensor_tensor(xn, xn, T_[:], ALU.add).then_inc(sems["dve_step"], t.one("dve_step"))
                            dve.wait_ge(sems["dve_step"], t.at("dve_step"))
                    t.turns(4, body)

                def ffn_up(self, l):
                    self.postnorm(M2, (HH, HL, f"ffnpre{l}"))
                    for n in range(2):
                        dve.memset(GE[n][:, 0:2], 0.0).then_inc(sems["dve_step"], t.one("dve_step"))
                        dve.wait_ge(sems["dve_step"], t.at("dve_step"))

                    def body(it):
                        for j in range(2):
                            def conv(c):
                                k = GAINS[f"conv{l}"] + c * FT + 2 * it + j
                                return G[:, bass.ds(k, 1)]
                            lo_part()
                            if j == 0:
                                t.once(it, lambda: rstd(OUTB, D))
                            chunk()
                            dve.tensor_tensor(GE[j][:, 2:SEQ + 2], banks[2 * j][:], RSTD[:], ALU.mult).then_inc(sems["evicted"], t.one("evicted"))
                            dve.wait_ge(sems["evicted"], t.at("evicted", CREDITS["evicted"]))
                            dve.tensor_scalar(CO[j][:], GE[j][:, 0:SEQ], conv(0), conv(3), ALU.mult, ALU.add).then_inc(sems["dve_step"], t.one("dve_step"))
                            dve.wait_ge(sems["dve_step"], t.at("dve_step"))
                            dve.scalar_tensor_tensor(CO[j][:], GE[j][:, 1:SEQ + 1], conv(1), CO[j][:], ALU.mult, ALU.add).then_inc(sems["dve_step"], t.one("dve_step"))
                            dve.wait_ge(sems["dve_step"], t.at("dve_step"))
                            dve.scalar_tensor_tensor(CO[j][:], GE[j][:, 2:SEQ + 2], conv(2), CO[j][:], ALU.mult, ALU.add).then_inc(sems["gate_in"], t.one("gate_in"))
                            lo_part()
                            chunk()
                            dve.tensor_tensor(TA[:], banks[2 * j + 1][:], RSTD[:], ALU.mult).then_inc(sems["evicted"], t.one("evicted"))
                            dve.wait_ge(sems["evicted"], t.at("evicted", CREDITS["evicted"]))
                            t.up("gate")
                            dve.wait_ge(sems["gate"], t.at("gate"))
                            dve.tensor_tensor(TA[:], TA[:], GL[j][:], ALU.mult).then_inc(sems["dve_step"], t.one("dve_step"))
                            dve.wait_ge(sems["dve_step"], t.at("dve_step"))
                            n = bass.ds(2 * it + j, 1)
                            split(FHI[:, n, :].rearrange("p o n -> p (o n)"), FLO[:, n, :].rearrange("p o n -> p (o n)"), TA[:])
                    t.turns(FT // 2, body)
                    signal("made")

                def retention(self):
                    self.prenorm([(HH, HL, "mixpre0")])
                    t.up("stage_loads", 48)
                    dve.wait_ge(sems["stage_loads"], t.at("stage_loads"))

                    def body(h):
                        for dst, b in ((RQ, 0), (RK, 2)):
                            for a in range(2):
                                lo_part()
                                if b + a == 0:
                                    t.once(h, lambda: rstd(OUTB, D))
                                chunk()
                                dve.tensor_tensor((TA, TB)[a][:], banks[b + a][:], RSTD[:], ALU.mult).then_inc(sems["evicted"], t.one("evicted"))
                                dve.wait_ge(sems["evicted"], t.at("evicted", CREDITS["evicted"]))
                            dve.tensor_tensor(dst[:, 0, :], TA[:], RC[:], ALU.mult).then_inc(sems["dve_step"], t.one("dve_step"))
                            dve.wait_ge(sems["dve_step"], t.at("dve_step"))
                            dve.tensor_tensor(TC[:], TB[:], RS[:], ALU.mult).then_inc(sems["dve_step"], t.one("dve_step"))
                            dve.wait_ge(sems["dve_step"], t.at("dve_step"))
                            dve.tensor_tensor(dst[:, 0, :], dst[:, 0, :], TC[:], ALU.subtract).then_inc(sems["rotated"], t.one("rotated"))
                            dve.wait_ge(sems["rotated"], t.at("rotated"))
                            dve.tensor_tensor(dst[:, 1, :], TB[:], RC[:], ALU.mult).then_inc(sems["dve_step"], t.one("dve_step"))
                            dve.wait_ge(sems["dve_step"], t.at("dve_step"))
                            dve.tensor_tensor(TC[:], TA[:], RS[:], ALU.mult).then_inc(sems["dve_step"], t.one("dve_step"))
                            dve.wait_ge(sems["dve_step"], t.at("dve_step"))
                            dve.tensor_tensor(dst[:, 1, :], dst[:, 1, :], TC[:], ALU.add).then_inc(sems["rotated"], t.one("rotated"))
                            dve.wait_ge(sems["rotated"], t.at("rotated"))
                        for j in range(4):
                            lo_part()
                            chunk()
                            t.up("v_turned")
                            if j:
                                dve.wait_ge(sems["v_turned"], t.at("v_turned", -1))
                            dve.tensor_tensor(RVF2[:], banks[j][:], RSTD[:], ALU.mult).then_inc(sems["evicted"], t.one("evicted"))
                        for kt in range(QT):
                            t.up("s_ready")
                            dve.wait_ge(sems["s_ready"], t.at("s_ready"))
                            n = SEQ - kt * P
                            dec = RD[:, bass.ds(h, 1), 0:n].rearrange("p o n -> p (o n)")
                            dve.tensor_tensor(RP[:, kt, kt * P:SEQ], banks[S0 + kt % 2][:, 0:n], dec, ALU.mult).then_inc(sems["operand"], t.one("operand"))
                        def gate_tile(e):
                            chunk()
                            dve.tensor_tensor(RP[:, e, :], banks[e][:], RSTD[:], ALU.mult).then_inc(sems["evicted"], t.one("evicted"))
                            dve.wait_ge(sems["evicted"], t.at("evicted", CREDITS["evicted"]))
                            signal("gate_in")

                        lo_part()
                        gate_tile(0)
                        t.up("small", 5)
                        dve.wait_ge(sems["small"], t.at("small"))
                        dve.tensor_scalar(VAR[:], banks[S0][:], 1.0 / RET_V, None, ALU.mult).then_inc(sems["dve_step"], t.one("dve_step"))
                        dve.wait_ge(sems["dve_step"], t.at("dve_step"))
                        for e in range(4):
                            dve.tensor_tensor(RY[:, e, :], RY[:, e, :], VAR[:], ALU.subtract).then_inc(sems["centred"], t.one("centred"))
                            dve.wait_ge(sems["centred"], t.at("centred"))
                        for e in range(1, 3):
                            lo_part()
                            gate_tile(e)
                        lo_part()
                        rstd(S0 + 1, RET_V, RSTD2)
                        gate_tile(3)
                        for e in range(4):
                            gn = G[:, bass.ds(GAINS["gn"] + 4 * h + e, 1)]
                            dve.scalar_tensor_tensor(TC[:], RY[:, e, :], gn, RSTD2[:], ALU.mult, ALU.mult).then_inc(sems["dve_step"], t.one("dve_step"))
                            dve.wait_ge(sems["dve_step"], t.at("dve_step"))
                            t.up("gate")
                            dve.wait_ge(sems["gate"], t.at("gate"))
                            dve.tensor_tensor(TC[:], TC[:], RP[:, e, :], ALU.mult).then_inc(sems["dve_step"], t.one("dve_step"))
                            dve.wait_ge(sems["dve_step"], t.at("dve_step"))
                            n = bass.ds(4 * h + e, 1)
                            split(RH[:, n, :].rearrange("p o n -> p (o n)"), RL[:, n, :].rearrange("p o n -> p (o n)"), TC[:])
                    t.turns(RET_HEADS, body)
                    signal("made")

                def dilated(self):
                    self.postnorm(M2, (H2H, H2L, "mixpre1"))
                    self.prenorm([(HH, HL, "kv")])
                    t.up("stage_loads", 96)
                    dve.wait_ge(sems["stage_loads"], t.at("stage_loads"))

                    def evict(par, x):
                        chunk()
                        g, bank = x // 3, banks[dil_bank(par, x)]
                        if x % 3 == 0:
                            dve.scalar_tensor_tensor(TA[:], bank[:], float(HEAD ** -0.5), RSTD[:], ALU.mult, ALU.mult).then_inc(sems["evicted"], t.one("evicted"))
                        else:
                            dve.tensor_tensor((TB if x % 3 == 1 else DF)[:], bank[:], RSTD[:], ALU.mult).then_inc(sems["evicted"], t.one("evicted"))
                        dve.wait_ge(sems["evicted"], t.at("evicted", CREDITS["evicted"]))
                        if x % 3 < 2:
                            signal("operand")
                            dst, T_ = ((DQ, TA), (DK, TB))[x % 3]
                            dve.tensor_tensor(dst[par][:, g, :], T_[:], DC[:], ALU.mult).then_inc(sems["dve_step"], t.one("dve_step"))

                    def rotate(par, x):
                        dst = ((DQ, DK)[x % 3])[par][:, x // 3, :]
                        t.up("swapped")
                        dve.wait_ge(sems["swapped"], t.at("swapped"))
                        dve.tensor_tensor(TC[:], banks[DAUX][:], DS[:], ALU.mult).then_inc(sems["dve_step"], t.one("dve_step"))
                        dve.wait_ge(sems["dve_step"], t.at("dve_step"))
                        dve.tensor_tensor(dst, dst, TC[:], ALU.add).then_inc(sems["rotated"], t.one("rotated"))

                    def u1(u):
                        i, m = UNITS[u]
                        t.up("s_ready")
                        dve.wait_ge(sems["s_ready"], t.at("s_ready"))
                        if u >= 2:
                            t.up("turned", 3)
                            dve.wait_ge(sems["turned"], t.at("turned", CREDITS["turned"]))
                        at_ = 0
                        for g in range(3):
                            w = key_blocks("sw" if g == 0 else "da", i)[1] * P
                            full = 2 * P if g == 0 else SEQ
                            passed()
                            dve.tensor_tensor_reduce(DP[u % 2][:, at_:at_ + w], banks[DSCORES[g]][:, 0:w],
                                    DM[g][:, full - w:full], 1.0, LOWEST, ALU.add, ALU.max, sm((MX, RC1, ES)[g] + u)).then_inc(sems["dve_step"], t.one("dve_step"))
                            dve.wait_ge(sems["dve_step"], t.at("dve_step"))
                            at_ += w
                        dve.tensor_tensor(sm(MX + u), sm(MX + u), sm(RC1 + u), ALU.max).then_inc(sems["dve_step"], t.one("dve_step"))
                        dve.wait_ge(sems["dve_step"], t.at("dve_step"))
                        dve.tensor_tensor(sm(MX + u), sm(MX + u), sm(ES + u), ALU.max).then_inc(sems["dve_step"], t.one("dve_step"))
                        dve.wait_ge(sems["dve_step"], t.at("dve_step"))
                        dve.tensor_scalar(sm(NM + u), sm(MX + u), -1.0, None, ALU.mult).then_inc(sems["scored"], t.one("scored"))

                    def u2(u):
                        w = dil_width(UNITS[u][0])
                        t.up("exped")
                        dve.wait_ge(sems["exped"], t.at("exped"))
                        dve.reciprocal(sm(RC1 + u), sm(DEN + u)).then_inc(sems["dve_step"], t.one("dve_step"))
                        dve.wait_ge(sems["dve_step"], t.at("dve_step"))
                        dve.tensor_scalar(DP[u % 2][:, 0:w], DP[u % 2][:, 0:w], sm(RC1 + u), None, ALU.mult).then_inc(sems["probs"], t.one("probs"))

                    def pair(par, more, it):
                        nxt = 1 - par
                        for u in range(len(UNITS)):
                            if u + 1 < len(UNITS):
                                u1(u + 1)
                            if more:
                                lo_part()
                                if u == 0:
                                    evict(nxt, 0)
                                    lo_part()
                                if u % 3 < 2:
                                    rotate(nxt, u)
                            if u + 1 < len(UNITS):
                                u2(u + 1)
                            if more:
                                evict(nxt, u + 1)
                        t.up("turned", 6)
                        t.up("pv_done", len(UNITS))
                        dve.wait_ge(sems["pv_done"], t.at("pv_done", CREDITS["pv_done"]))
                        z = bass.ds(2 * it + par, 1)
                        dve.tensor_scalar(DO[:, z, :].rearrange("p o n -> p (o n)"), banks[OUTB][:], 1.0, None, ALU.mult).then_inc(sems["o_used"], t.one("o_used"))
                        if more:
                            u1(0)
                            u2(0)

                    for x in range(9):
                        lo_part()
                        if x == 0:
                            rstd(OUTB, D)
                        evict(0, x)
                        if x % 3 < 2:
                            rotate(0, x)
                    u1(0)
                    u2(0)

                    def body(it):
                        pair(0, True, it)
                        pair(1, not isinstance(it, int) or it < KT // 2 - 1, it)
                    t.turns(KT // 2, body)

            e = Programs()
            e.t = t
            run(e)


def tiles(w, columns):
    columns = np.asarray(columns)
    part = w[:, np.maximum(columns, 0)]
    if (columns < 0).any():
        part = part.copy()
        part[:, columns < 0] = 0
    return part.reshape(-1, P, P).transpose(1, 0, 2)


def plain(w, at=0, n=None):
    n = (w.shape[1] - at) // P if n is None else n
    return [tiles(w, np.arange(at + j * P, at + (j + 1) * P)) for j in range(n)]


def chunks(parts, width):
    a = np.concatenate(parts, 1)
    return np.ascontiguousarray(a.reshape(P, -1, width * P).transpose(1, 0, 2))


def interleave(*lists):
    return [x for group in zip(*lists) for x in group]


def per_partition(v):
    return v.reshape(-1, P).T


def lay_out(a):
    names, w = {}, {}
    in_sizes = (512, 512, 512, 512, 256, 128, ROPE, 512, 512, 128, 128, 512, 3072)
    o = dict(zip(("aq", "ak", "av", "az", "bq", "bkv", "bkr", "bz", "cq", "ck", "cv", "cz", "g"),
                 np.cumsum((0,) + in_sizes[:-1])))
    sw_cols = [np.concatenate([np.arange(HEAD) + HEAD * h for h in (n, 4 + n)]) for n in range(4)]
    rope, swap, gap = np.arange(ROPE), np.roll(np.arange(ROPE), HALF), np.full(ROPE, -1)
    for l in range(DEPTH):
        wi = a["w_in"][l]
        kr = [tiles(wi, np.concatenate([o["bkr"] + r, gap, o["bkr"] + r, gap])) for r in (rope, swap)]
        w[f"lat{l}"] = chunks(plain(wi, o["bq"], 3) + kr + plain(wi, o["ck"], 2), 8)
        w[f"da{l}"] = chunks(interleave(*(plain(wi, o[n], 4) for n in ("aq", "ak", "av", "az"))), 8)
        parts = []
        qb, kvb = a["mla_w_qb"][l], a["mla_w_kvb"][l]
        bz = plain(wi, o["bz"], 4)
        for n in range(4):
            h = (2 * n, 2 * n + 1)
            parts += [bz[n], tiles(kvb, np.concatenate([P * x + HEAD + np.arange(HEAD) for x in h])),
                      tiles(qb, np.concatenate([96 * x + np.arange(HEAD) for x in h])),
                      tiles(qb, np.concatenate([y for x in h for y in (96 * x + HEAD + rope, gap)])),
                      tiles(qb, np.concatenate([y for x in h for y in (96 * x + HEAD + swap, gap)])),
                      tiles(kvb, np.concatenate([P * x + np.arange(HEAD) for x in h]))]
        w[f"mla{l}"] = chunks(parts, 8)
        w[f"sw{l}"] = chunks([tiles(wi, o[s] + c) for c in sw_cols for s in ("cq", "cz")], 8)
        g = [plain(wi, o["g"] + D * b, KT) for b in range(3)]
        rows = np.concatenate(sw_cols)
        br = [plain(x, 0, KT) for x in (a["w_br_a"][l], a["w_br_b"][l], a["w_br_c"][l][rows])]
        w[f"gate{l}"] = chunks(interleave(g[0], br[0], g[1], br[1], g[2], br[2]), 12)
        w[f"wout{l}"] = chunks(plain(a["w_out"][l]), 8)
        w[f"ple{l}"] = chunks(interleave(plain(a["w_ple_gate"][l]), plain(a["w_ple_proj"][l])), 10)
    ri = a["ret_w_in_2"][0]
    parts = []
    for h in range(RET_HEADS):
        parts += plain(ri, 256 * h, 2) + plain(ri, D + 256 * h, 2) + plain(ri, 2 * D + RET_V * h, 4)
        parts += plain(ri, 4 * D + RET_V * h, 4)
    w["ret"] = chunks(parts, 8)
    w["retout"] = chunks(plain(a["ret_w_out_2"][0]), 8)
    kv, q = a["att_w_kv_2"], a["att_w_q_2"][0]
    parts = []
    for n in range(KT):
        for g in range(3):
            parts += plain(q, D * g + P * n, 1) + plain(kv, D * g + P * n, 1) + plain(kv, 3 * D + D * g + P * n, 1)
    w["dil"] = chunks(parts, 8)
    w["wo"] = chunks(plain(a["att_w_o_2"][0]), 8)
    for l in range(DEPTH):
        up = a["ffn_w_up_2"][l]
        w[f"up{l}"] = chunks(interleave(plain(up, 0, FT), plain(up, DFF, FT)), 8)
        w[f"down{l}"] = chunks(plain(a["ffn_w_down_2"][l]), FH)
    for n, k, width in STREAM:
        assert w[n].shape == (k, P, width * P), (n, w[n].shape)
        names["w_" + n] = w[n]
    gains = []
    for n in GAINS:
        stem, l = n.rstrip("01"), int(n[-1]) if n[-1] in "01" else 0
        if stem == "conv":
            gains += [per_partition(a["ffn_conv_w_2"][l, c]) for c in range(3)] + [per_partition(a["ffn_conv_b_2"][l])]
        else:
            src = {"pre": "norm_pre", "post": "norm_post", "mixpre": "norm_mix_pre_2", "mixpost": "norm_mix_post_2",
                   "ffnpre": "norm_ffn_pre_2", "ffnpost": "norm_ffn_post_2", "kv": "kv_norm_2", "mlaq": "mla_q_norm",
                   "mlakv": "mla_kv_norm", "subln": "da_subln", "gn": "ret_gn_gain_2"}[stem]
            gains.append(per_partition(a[src] if stem == "kv" else a[src][l]))
    names["gains"] = np.ascontiguousarray(np.concatenate(gains, 1))
    names["x_t"] = np.ascontiguousarray(a["x"][0].T.reshape(KT, P, SEQ).transpose(1, 0, 2))
    names["p_t"] = np.ascontiguousarray(a["p"][:, 0].transpose(0, 2, 1).reshape(DEPTH, 2, P, SEQ).transpose(0, 2, 1, 3))
    names["positions"] = np.ascontiguousarray(a["positions"])
    names["rel_bias"] = np.ascontiguousarray(a["rel_bias"])
    names["da_lambda"] = np.ascontiguousarray(a["da_lambda"].reshape(1, -1))
    names["sw_sinks"] = np.ascontiguousarray(a["sw_sinks"])
    names.update(constants())
    return names


def kernel(**inputs):
    import concourse.bacc as _bacc
    from concourse.bass_utils import run_bass_kernel_spmd as _run

    nc = _bacc.Bacc("TRN2", target_bir_lowering=False, num_devices=1)
    arrays, aps = {}, {}
    for name, value in lay_out({k: np.asarray(v) for k, v in inputs.items()}).items():
        arrays[f"in_{name}"] = value
        aps[name] = nc.dram_tensor(f"in_{name}", value.shape, mybir.dt.from_np(value.dtype), kind="ExternalInput").ap()
    out = nc.dram_tensor("out_x", (P, KT, SEQ), F32, kind="ExternalOutput").ap()
    two_stacks_kernel(nc, aps, out)
    r = _run(nc, [arrays], core_ids=[0])
    got = r.results[0]["out_x"]
    return np.ascontiguousarray(got.transpose(1, 0, 2).reshape(1, D, SEQ).transpose(0, 2, 1))
```
